# Optimizing a Trainium2 kernel written in Bass

```python
import jax, jax.numpy as jnp
from jax import lax
import numpy as np
import math

D_MODEL = 1024
BATCH = 1
SEQ = 256
DEPTH = 1

CTX_LEN = 256
GRID_W = 64
EPS = 1e-6
N_MOD = 6
GDN_HEADS = 8
GDN_HEAD_DIM = 128
GDN_WIDTH = GDN_HEADS * GDN_HEAD_DIM
GDN_CHUNK = 64
CONV_SIZE = 3
GLA_HEADS = 4
GLA_KEY_DIM = D_MODEL // 2
GLA_VALUE_DIM = D_MODEL
GLA_DK = GLA_KEY_DIM // GLA_HEADS
GLA_DV = GLA_VALUE_DIM // GLA_HEADS
GLA_GATE_RANK = 16
GLA_GATE_NORMALIZER = 16.0
GLA_CHUNK = 64
N_EXPERTS = 32
TOP_K = 4
D_EXPERT = D_MODEL
SWIGLU_LIMIT = 7.0
SWIGLU_ALPHA = 1.702
MOE_BLOCK = 128
IN_SPLITS = (GDN_WIDTH, GDN_WIDTH, GDN_WIDTH, GDN_WIDTH, 2 * GDN_HEADS, 2 * GDN_HEADS,
             GLA_KEY_DIM, GLA_KEY_DIM, GLA_VALUE_DIM, GLA_VALUE_DIM, 2 * GLA_GATE_RANK, 2 * D_MODEL)
D_IN = 4 * GDN_WIDTH + 4 * GDN_HEADS + 2 * GLA_KEY_DIM + 2 * GLA_VALUE_DIM + 2 * GLA_GATE_RANK + 2 * D_MODEL


F32 = jnp.float32

def rms_norm(x, g):
    xf = x.astype(F32)
    y = xf * lax.rsqrt(jnp.mean(xf * xf, axis=-1, keepdims=True) + EPS)
    return (y * g.astype(F32)).astype(x.dtype)

def l2_normalize(t):
    tf = t.astype(F32)
    return tf * lax.rsqrt(jnp.sum(tf * tf, axis=-1, keepdims=True) + EPS)

def modulate(h, shift, scale):
    return h * (1.0 + scale) + shift

def split_in(p):
    idx = np.cumsum(IN_SPLITS)[:-1].tolist()
    return jnp.split(p, idx, axis=-1)

def to_heads(t, n_heads):
    b, l, _ = t.shape
    return t.reshape(b, l, n_heads, -1).transpose(0, 2, 1, 3)

def from_heads(t):
    return t.transpose(0, 2, 1, 3)

def depthwise_conv2d(img, w):
    ch = img.shape[-1]
    return lax.conv_general_dilated(img, w[:, :, None, :].astype(img.dtype), window_strides=(1, 1), padding='SAME',
                                    dimension_numbers=('NHWC', 'HWIO', 'NHWC'), feature_group_count=ch)

def conv_latent(t, conv_w):
    b, l, ch = t.shape
    rows = l // GRID_W
    return depthwise_conv2d(t.reshape(b, rows, GRID_W, ch), conv_w).reshape(b, l, ch)

def conv_context(t, conv_w):
    mid = CONV_SIZE // 2
    return depthwise_conv2d(t[:, None], conv_w[mid:mid + 1])[:, 0]

def gated_delta_chunked(q, k, v, g, beta, s0):
    b, h, l, dk = q.shape
    dv = v.shape[-1]
    c = GDN_CHUNK
    n = l // c
    q = q.astype(F32).reshape(b, h, n, c, dk) * (dk ** -0.5)
    k = k.astype(F32).reshape(b, h, n, c, dk)
    v = v.astype(F32).reshape(b, h, n, c, dv)
    beta = beta.astype(F32).reshape(b, h, n, c)
    g = jnp.cumsum(g.astype(F32).reshape(b, h, n, c), axis=-1)
    incl = jnp.tril(jnp.ones((c, c), bool))
    strict = jnp.tril(jnp.ones((c, c), bool), -1)
    decay = jnp.exp(jnp.where(incl, g[..., :, None] - g[..., None, :], -jnp.inf))
    kb = k * beta[..., None]
    m = jnp.where(strict, jnp.einsum('bhnid,bhnjd->bhnij', kb, k) * decay, 0.0)
    a = m + jnp.eye(c, dtype=F32)
    rhs = jnp.concatenate([v * beta[..., None], kb * jnp.exp(g)[..., None]], axis=-1)
    sol = lax.linalg.triangular_solve(a, rhs, left_side=True, lower=True, unit_diagonal=True)
    u, w = sol[..., :dv], sol[..., dv:]
    attn = jnp.einsum('bhnid,bhnjd->bhnij', q, k) * decay
    qg = q * jnp.exp(g)[..., None]
    kd = k * jnp.exp(g[..., -1:] - g)[..., None]
    gl = jnp.exp(g[..., -1])
    xs = tuple(jnp.moveaxis(t, 2, 0) for t in (u, w, attn, qg, kd, gl))

    def step(s, xs_n):
        u_n, w_n, attn_n, qg_n, kd_n, gl_n = xs_n
        v_new = u_n - jnp.einsum('bhck,bhkv->bhcv', w_n, s)
        o_n = jnp.einsum('bhck,bhkv->bhcv', qg_n, s) + jnp.einsum('bhij,bhjv->bhiv', attn_n, v_new)
        s = s * gl_n[..., None, None] + jnp.einsum('bhck,bhcv->bhkv', kd_n, v_new)
        return s, o_n

    s, o = lax.scan(step, s0.astype(F32), xs)
    return jnp.moveaxis(o, 0, 2).reshape(b, h, l, dv), s

def gla_chunked(q, k, v, log_a, s0):
    b, h, l, dk = q.shape
    dv = v.shape[-1]
    c = GLA_CHUNK
    n = l // c
    q = q.astype(F32).reshape(b, h, n, c, dk) * (dk ** -0.5)
    k = k.astype(F32).reshape(b, h, n, c, dk)
    v = v.astype(F32).reshape(b, h, n, c, dv)
    gcum = jnp.cumsum(log_a.astype(F32).reshape(b, h, n, c, dk), axis=-2)
    ref = gcum[..., c // 2:c // 2 + 1, :]
    incl = jnp.tril(jnp.ones((c, c), bool))
    attn = jnp.einsum('bhnik,bhnjk->bhnij', q * jnp.exp(gcum - ref), k * jnp.exp(ref - gcum))
    attn = jnp.where(incl, attn, 0.0)
    intra = jnp.einsum('bhnij,bhnjv->bhniv', attn, v)
    qg = q * jnp.exp(gcum)
    kd = k * jnp.exp(gcum[..., -1:, :] - gcum)
    gl = jnp.exp(gcum[..., -1, :])
    xs = tuple(jnp.moveaxis(t, 2, 0) for t in (intra, qg, kd, v, gl))

    def step(s, xs_n):
        intra_n, qg_n, kd_n, v_n, gl_n = xs_n
        o_n = intra_n + jnp.einsum('bhck,bhkv->bhcv', qg_n, s)
        s = s * gl_n[..., :, None] + jnp.einsum('bhck,bhcv->bhkv', kd_n, v_n)
        return s, o_n

    s, o = lax.scan(step, s0.astype(F32), xs)
    return jnp.moveaxis(o, 0, 2).reshape(b, h, l, dv), s

def flip_seq(ts, flip):
    return tuple(jnp.flip(t, axis=2) for t in ts) if flip else tuple(ts)

def bidirectional_prefix_scan(scan_fn, ctx_shared, lat_shared, ctx_gates, lat_gates, s0, need_ctx):
    lat_outs, ctx_outs = [], []
    for direction, flip in enumerate((False, True)):
        o_c, s_c = scan_fn(*flip_seq(ctx_shared, flip), *flip_seq(ctx_gates[direction], flip), s0)
        o_l, _ = scan_fn(*flip_seq(lat_shared, flip), *flip_seq(lat_gates[direction], flip), s_c)
        lat_outs.append(flip_seq((o_l,), flip)[0])
        if need_ctx:
            ctx_outs.append(flip_seq((o_c,), flip)[0])
    o_lat = lat_outs[0] + lat_outs[1]
    o_ctx = ctx_outs[0] + ctx_outs[1] if need_ctx else None
    return o_lat, o_ctx

def gdn_inputs(parts, qkv, a_log_f, a_log_b, dt_bias_f, dt_bias_b):
    q, k, v = jnp.split(qkv, 3, axis=-1)
    q = l2_normalize(to_heads(q, GDN_HEADS))
    k = l2_normalize(to_heads(k, GDN_HEADS))
    v = to_heads(v, GDN_HEADS)
    beta = jax.nn.sigmoid(parts[4].astype(F32)).transpose(0, 2, 1)
    a = parts[5].astype(F32).transpose(0, 2, 1)
    hh = GDN_HEADS
    g_f = -jnp.exp(a_log_f.astype(F32))[:, None] * jax.nn.softplus(a[:, :hh] + dt_bias_f.astype(F32)[:, None])
    g_b = -jnp.exp(a_log_b.astype(F32))[:, None] * jax.nn.softplus(a[:, hh:] + dt_bias_b.astype(F32)[:, None])
    return (q, k, v), ((g_f, beta[:, :hh]), (g_b, beta[:, hh:]))

def gla_log_gate(z, w, bias):
    return to_heads(jax.nn.log_sigmoid((z @ w + bias).astype(F32)) / GLA_GATE_NORMALIZER, GLA_HEADS)

def gla_inputs(parts, w_f, w_b, b_f, b_b):
    q = to_heads(parts[6], GLA_HEADS)
    k = to_heads(parts[7], GLA_HEADS)
    v = to_heads(parts[8], GLA_HEADS)
    lr = parts[10]
    g_f = gla_log_gate(lr[..., :GLA_GATE_RANK], w_f, b_f)
    g_b = gla_log_gate(lr[..., GLA_GATE_RANK:], w_b, b_b)
    return (q, k, v), ((g_f,), (g_b,))

def merge_branches(parts, o_a, o_b, gdn_norm_g, gla_norm_g, w_out_a, w_out_b, w_out):
    dtype = parts[0].dtype
    bsz, l = parts[0].shape[:2]
    za = parts[3].reshape(bsz, l, GDN_HEADS, GDN_HEAD_DIM).astype(F32)
    ya = (rms_norm(from_heads(o_a), gdn_norm_g) * jax.nn.silu(za)).astype(dtype).reshape(bsz, l, GDN_WIDTH) @ w_out_a
    rb = parts[9].reshape(bsz, l, GLA_HEADS, GLA_DV).astype(F32)
    yb = (rms_norm(from_heads(o_b), gla_norm_g) * jax.nn.silu(rb)).astype(dtype).reshape(bsz, l, GLA_VALUE_DIM) @ w_out_b
    gates = jax.nn.sigmoid(parts[11])
    y = gates[..., :D_MODEL] * ya + gates[..., D_MODEL:] * yb
    return y @ w_out

def token_mixer(h_lat, h_ctx, need_ctx, w_in, conv_w, a_log_f, a_log_b, dt_bias_f, dt_bias_b, gdn_norm_g,
                gla_gate_w_f, gla_gate_w_b, gla_gate_b_f, gla_gate_b_b, gla_norm_g, w_out_a, w_out_b, w_out):
    p_lat = h_lat @ w_in
    p_ctx = h_ctx @ w_in
    parts_lat, parts_ctx = split_in(p_lat), split_in(p_ctx)
    bsz = h_lat.shape[0]
    qkv_lat = jax.nn.silu(conv_latent(p_lat[..., :3 * GDN_WIDTH], conv_w))
    qkv_ctx = jax.nn.silu(conv_context(p_ctx[..., :3 * GDN_WIDTH], conv_w))
    a_lat, a_lat_g = gdn_inputs(parts_lat, qkv_lat, a_log_f, a_log_b, dt_bias_f, dt_bias_b)
    a_ctx, a_ctx_g = gdn_inputs(parts_ctx, qkv_ctx, a_log_f, a_log_b, dt_bias_f, dt_bias_b)
    s0_a = jnp.zeros((bsz, GDN_HEADS, GDN_HEAD_DIM, GDN_HEAD_DIM), F32)
    o_a_lat, o_a_ctx = bidirectional_prefix_scan(gated_delta_chunked, a_ctx, a_lat, a_ctx_g, a_lat_g, s0_a, need_ctx)
    b_lat, b_lat_g = gla_inputs(parts_lat, gla_gate_w_f, gla_gate_w_b, gla_gate_b_f, gla_gate_b_b)
    b_ctx, b_ctx_g = gla_inputs(parts_ctx, gla_gate_w_f, gla_gate_w_b, gla_gate_b_f, gla_gate_b_b)
    s0_b = jnp.zeros((bsz, GLA_HEADS, GLA_DK, GLA_DV), F32)
    o_b_lat, o_b_ctx = bidirectional_prefix_scan(gla_chunked, b_ctx, b_lat, b_ctx_g, b_lat_g, s0_b, need_ctx)
    merge_w = (gdn_norm_g, gla_norm_g, w_out_a, w_out_b, w_out)
    y_lat = merge_branches(parts_lat, o_a_lat, o_b_lat, *merge_w)
    y_ctx = merge_branches(parts_ctx, o_a_ctx, o_b_ctx, *merge_w) if need_ctx else None
    return y_lat, y_ctx

def moe_ffn(h, w_router, b_router, w_gu, b_gu, w_down, b_down):
    t, d = h.shape
    n_assign = t * TOP_K
    n_blocks = -(-(n_assign + N_EXPERTS * (MOE_BLOCK - 1)) // MOE_BLOCK)
    logits = (h @ w_router + b_router).astype(F32)
    top_logit, top_idx = lax.top_k(logits, TOP_K)
    top_p = jax.nn.softmax(top_logit, axis=-1)
    flat_e = top_idx.reshape(-1).astype(jnp.int32)
    order = jnp.argsort(flat_e)
    sorted_e = flat_e[order]
    sorted_tok = (order // TOP_K).astype(jnp.int32)
    sorted_p = top_p.reshape(-1)[order]
    counts = jnp.bincount(flat_e, length=N_EXPERTS).astype(jnp.int32)
    start = jnp.cumsum(counts) - counts
    padded = (counts + MOE_BLOCK - 1) // MOE_BLOCK * MOE_BLOCK
    pad_end = jnp.cumsum(padded)
    pad_start = pad_end - padded
    dest = pad_start[sorted_e] + jnp.arange(n_assign, dtype=jnp.int32) - start[sorted_e]
    slot_tok = jnp.full((n_blocks * MOE_BLOCK,), t, jnp.int32).at[dest].set(sorted_tok)
    slot_p = jnp.zeros((n_blocks * MOE_BLOCK,), F32).at[dest].set(sorted_p)
    block_start = jnp.arange(n_blocks, dtype=jnp.int32) * MOE_BLOCK
    block_expert = jnp.minimum(jnp.searchsorted(pad_end, block_start, side='right'), N_EXPERTS - 1)
    h_pad = jnp.concatenate([h, jnp.zeros((1, d), h.dtype)], axis=0)

    def expert_block(args):
        tok, p, e = args
        xb = h_pad[tok]
        gu = xb @ w_gu[e] + b_gu[e]
        glu = jnp.minimum(gu[:, :D_EXPERT], SWIGLU_LIMIT)
        lin = jnp.clip(gu[:, D_EXPERT:], -SWIGLU_LIMIT, SWIGLU_LIMIT)
        act = glu * jax.nn.sigmoid(SWIGLU_ALPHA * glu) * (lin + 1.0)
        return (act @ w_down[e] + b_down[e]) * p[:, None].astype(h.dtype)

    yb = lax.map(expert_block, (slot_tok.reshape(n_blocks, MOE_BLOCK), slot_p.reshape(n_blocks, MOE_BLOCK), block_expert))
    y = jax.ops.segment_sum(yb.reshape(-1, d), slot_tok, num_segments=t + 1)
    return y[:t].astype(h.dtype)

def first_inputs(seed: int = 0) -> dict:
    key = jax.random.key(seed)
    ks = iter(jax.random.split(key, 40))
    nrm = lambda shape, s: jax.random.normal(next(ks), shape, F32) * s
    gain = lambda shape: 1.0 + nrm(shape, 0.02)
    dd = D_MODEL
    u_dt = jax.random.uniform(next(ks), (2, DEPTH, GDN_HEADS), F32)
    dt = jnp.exp(u_dt * (jnp.log(0.1) - jnp.log(1e-3)) + jnp.log(1e-3))
    dt_bias = dt + jnp.log(-jnp.expm1(-dt))
    a_log = jnp.log(jax.random.uniform(next(ks), (2, DEPTH, GDN_HEADS), F32, 1.0, 16.0))
    return {
        'x': nrm((BATCH, SEQ, dd), 1.0),
        'c': nrm((BATCH, dd), 1.0),
        'ctx': nrm((BATCH, CTX_LEN, dd), 1.0),
        'c_ctx': nrm((dd,), 1.0),
        'w_mod': nrm((DEPTH, dd, N_MOD * dd), 0.5 * dd ** -0.5),
        'b_mod': nrm((DEPTH, N_MOD * dd), 0.02),
        'norm_mix_g': gain((DEPTH, dd)),
        'norm_ffn_g': gain((DEPTH, dd)),
        'w_in': nrm((DEPTH, dd, D_IN), dd ** -0.5),
        'conv_w': nrm((DEPTH, CONV_SIZE, CONV_SIZE, 3 * GDN_WIDTH), 1.0 / CONV_SIZE),
        'a_log_f': a_log[0],
        'a_log_b': a_log[1],
        'dt_bias_f': dt_bias[0],
        'dt_bias_b': dt_bias[1],
        'gdn_norm_g': gain((DEPTH, GDN_HEAD_DIM)),
        'gla_gate_w_f': nrm((DEPTH, GLA_GATE_RANK, GLA_KEY_DIM), GLA_GATE_RANK ** -0.5),
        'gla_gate_w_b': nrm((DEPTH, GLA_GATE_RANK, GLA_KEY_DIM), GLA_GATE_RANK ** -0.5),
        'gla_gate_b_f': nrm((DEPTH, GLA_KEY_DIM), 0.1),
        'gla_gate_b_b': nrm((DEPTH, GLA_KEY_DIM), 0.1),
        'gla_norm_g': gain((DEPTH, GLA_DV)),
        'w_out_a': nrm((DEPTH, GDN_WIDTH, dd), GDN_WIDTH ** -0.5),
        'w_out_b': nrm((DEPTH, GLA_VALUE_DIM, dd), GLA_VALUE_DIM ** -0.5),
        'w_out': nrm((DEPTH, dd, dd), dd ** -0.5),
        'w_router': nrm((DEPTH, dd, N_EXPERTS), dd ** -0.5),
        'b_router': nrm((DEPTH, N_EXPERTS), 0.01),
        'w_gu': nrm((DEPTH, N_EXPERTS, dd, 2 * D_EXPERT), dd ** -0.5),
        'b_gu': nrm((DEPTH, N_EXPERTS, 2 * D_EXPERT), 0.01),
        'w_down': nrm((DEPTH, N_EXPERTS, D_EXPERT, dd), D_EXPERT ** -0.5),
        'b_down': nrm((DEPTH, N_EXPERTS, dd), 0.01),
        'final_norm_g': gain((dd,)),
    }

def first_block(x, c, ctx, c_ctx, w_mod, b_mod, norm_mix_g, norm_ffn_g, w_in, conv_w, a_log_f, a_log_b, dt_bias_f,
              dt_bias_b, gdn_norm_g, gla_gate_w_f, gla_gate_w_b, gla_gate_b_f, gla_gate_b_b, gla_norm_g, w_out_a,
              w_out_b, w_out, w_router, b_router, w_gu, b_gu, w_down, b_down, final_norm_g):
    for layer in range(DEPTH):
        need_ctx = layer < DEPTH - 1
        mod_lat = [m[:, None, :] for m in jnp.split(jax.nn.silu(c) @ w_mod[layer] + b_mod[layer], N_MOD, axis=-1)]
        mod_ctx = jnp.split(jax.nn.silu(c_ctx) @ w_mod[layer] + b_mod[layer], N_MOD, axis=-1)
        sh1, sc1, g1, sh2, sc2, g2 = mod_lat
        csh1, csc1, cg1, csh2, csc2, cg2 = mod_ctx
        h_lat = modulate(rms_norm(x, norm_mix_g[layer]), sh1, sc1)
        h_ctx = modulate(rms_norm(ctx, norm_mix_g[layer]), csh1, csc1)
        y_lat, y_ctx = token_mixer(h_lat, h_ctx, need_ctx, w_in[layer], conv_w[layer], a_log_f[layer], a_log_b[layer],
                                   dt_bias_f[layer], dt_bias_b[layer], gdn_norm_g[layer], gla_gate_w_f[layer],
                                   gla_gate_w_b[layer], gla_gate_b_f[layer], gla_gate_b_b[layer], gla_norm_g[layer],
                                   w_out_a[layer], w_out_b[layer], w_out[layer])
        x = x + g1 * y_lat
        h = modulate(rms_norm(x, norm_ffn_g[layer]), sh2, sc2).reshape(-1, D_MODEL)
        moe_w = (w_router[layer], b_router[layer], w_gu[layer], b_gu[layer], w_down[layer], b_down[layer])
        if need_ctx:
            ctx = ctx + cg1 * y_ctx
            hc = modulate(rms_norm(ctx, norm_ffn_g[layer]), csh2, csc2).reshape(-1, D_MODEL)
            n_lat = h.shape[0]
            y = moe_ffn(jnp.concatenate([h, hc], axis=0), *moe_w)
            x = x + g2 * y[:n_lat].reshape(x.shape)
            ctx = ctx + cg2 * y[n_lat:].reshape(ctx.shape)
        else:
            x = x + g2 * moe_ffn(h, *moe_w).reshape(x.shape)
    return rms_norm(x, final_norm_g)


_first_inputs = first_inputs


def first_inputs(seed=0):
    import zlib

    import numpy as np

    out = dict(_first_inputs(seed))
    spreads = {}
    factors = {'c_ctx': 3.039,
     'norm_mix_g': 5.809,
     'norm_ffn_g': 3.223,
     'a_log_f': 2.854,
     'a_log_b': 3.499,
     'gdn_norm_g': 8.0,
     'gla_gate_w_f': 3.757,
     'gla_gate_w_b': 3.743,
     'gla_gate_b_f': 8.0,
     'gla_gate_b_b': 7.736,
     'gla_norm_g': 8.0,
     'b_router': 5.315,
     'b_gu': 8.0,
     'b_down': 8.0,
     'final_norm_g': 3.12}
    for name, (base, spread) in spreads.items():
        noise = np.random.default_rng([zlib.crc32(name.encode()), seed]).standard_normal(out[name].shape)
        drawn = base * np.exp(spread * noise) if base else spread * noise
        out[name] = __import__('jax').numpy.asarray(drawn.astype(out[name].dtype))
    for name, factor in factors.items():
        out[name] = (out[name] * factor).astype(out[name].dtype)
    return out


_narrow_inputs = first_inputs


def first_inputs(seed=0):
    out = dict(_narrow_inputs(seed))
    wider = {'norm_ffn_g': 6.93,
     'gdn_norm_g': 4.42,
     'gla_norm_g': 4.4,
     'b_router': 12.0,
     'b_gu': 10.19,
     'b_down': 12.0,
     'final_norm_g': 3.54}
    for name, times in wider.items():
        mean = out[name].mean()
        out[name] = (mean + times * (out[name] - mean)).astype(out[name].dtype)
    return out


D_MIX = D_MODEL
N_HEADS_A = 8
HEAD_DIM_A = 64
DIL_CONFIGS = ((128, 1), (512, 4), (2048, 16))
Q_BLOCK = 128
N_HEADS_B = 8
QK_NOPE = 64
QK_ROPE = 32
V_DIM = 64
Q_LORA = 384
KV_LORA = 256
ROPE_BASE = 10000.0
D_FF = 2816
CONV_WIDTH = 3
NEG = -1e30

WIDTH_A = N_HEADS_A * HEAD_DIM_A
WIDTH_B = N_HEADS_B * V_DIM
IN_SIZES = (WIDTH_A, WIDTH_A, WIDTH_A, Q_LORA, KV_LORA, QK_ROPE)
D_IN_2 = sum(IN_SIZES)
SPLIT_POINTS = tuple(int(v) for v in np.cumsum(IN_SIZES)[:-1])


def _rmsnorm(x, g):
    xf = x.astype(jnp.float32)
    y = xf * lax.rsqrt(jnp.mean(xf * xf, axis=-1, keepdims=True) + EPS)
    return (y * g.astype(jnp.float32)).astype(x.dtype)

def _rope(x, cos, sin):
    xf = x.astype(jnp.float32)
    half = xf.shape[-1] // 2
    x1, x2 = xf[..., :half], xf[..., half:]
    out = jnp.concatenate([x1 * cos - x2 * sin, x2 * cos + x1 * sin], axis=-1)
    return out.astype(x.dtype)

def _dilated_branch(q, k, v, slopes, window, dilation):
    b, h, s, d = q.shape
    r = dilation
    half = window // (2 * dilation)
    L = s // r
    qb = min(Q_BLOCK, L)
    nblk = -(-L // qb)
    Lp = nblk * qb
    slab = qb + 2 * half

    def to_dilated(t):
        return t.reshape(b, h, L, r, d).transpose(0, 1, 3, 2, 4)

    qd, kd, vd = to_dilated(q), to_dilated(k), to_dilated(v)
    qd = jnp.pad(qd, ((0, 0), (0, 0), (0, 0), (0, Lp - L), (0, 0)))
    pad_kv = ((0, 0), (0, 0), (0, 0), (half, half + Lp - L), (0, 0))
    kd = jnp.pad(kd, pad_kv)
    vd = jnp.pad(vd, pad_kv)
    idx = jnp.arange(nblk)[:, None] * qb + jnp.arange(slab)[None, :]
    k_s = kd[:, :, :, idx, :].astype(jnp.float32)
    v_s = vd[:, :, :, idx, :].astype(jnp.float32)
    q_s = qd.reshape(b, h, r, nblk, qb, d).astype(jnp.float32)

    scores = jnp.einsum('bhcnqd,bhcnkd->bhcnqk', q_s, k_s) * (d ** -0.5)
    off = jnp.arange(slab)[None, :] - half - jnp.arange(qb)[:, None]
    key_pos = idx - half
    valid = (jnp.abs(off) <= half)[None, :, :] & ((key_pos >= 0) & (key_pos < L))[:, None, :]
    dist = (jnp.abs(off) * r).astype(jnp.float32)
    alibi = -slopes[:, None, None] * dist[None]
    scores = scores + alibi[None, :, None, None]
    scores = jnp.where(valid[None, None, None], scores, NEG)
    lse = jax.nn.logsumexp(scores, axis=-1)
    p = jnp.exp(scores - lse[..., None])
    o = jnp.einsum('bhcnqk,bhcnkd->bhcnqd', p, v_s)

    o = o.reshape(b, h, r, Lp, d)[:, :, :, :L].transpose(0, 1, 3, 2, 4).reshape(b, h, s, d)
    lse = lse.reshape(b, h, r, Lp)[:, :, :, :L].transpose(0, 1, 3, 2).reshape(b, h, s)
    return o, lse

def _dilated_attention(qa, ka, va):
    b, s, _ = qa.shape
    def heads(t):
        return t.reshape(b, s, N_HEADS_A, HEAD_DIM_A).transpose(0, 2, 1, 3)
    q, k, v = heads(qa), heads(ka), heads(va)
    slopes = jnp.exp2(-8.0 * jnp.arange(1, N_HEADS_A + 1, dtype=jnp.float32) / N_HEADS_A)
    outs, lses = [], []
    for window, dilation in DIL_CONFIGS:
        o, lse = _dilated_branch(q, k, v, slopes, window, dilation)
        outs.append(o)
        lses.append(lse)
    w = jax.nn.softmax(jnp.stack(lses, axis=0), axis=0)
    o = jnp.einsum('gbhs,gbhsd->bhsd', w, jnp.stack(outs, axis=0))
    return o.transpose(0, 2, 1, 3).reshape(b, s, WIDTH_A).astype(qa.dtype)

def _mla(c_q, c_kv, k_r, q_lat_norm, w_uq, kv_lat_norm, w_ukv):
    b, s, _ = c_q.shape
    pos = jnp.arange(s, dtype=jnp.float32)
    inv_freq = jnp.exp(-math.log(ROPE_BASE) * jnp.arange(0, QK_ROPE, 2, dtype=jnp.float32) / QK_ROPE)
    ang = pos[:, None] * inv_freq[None, :]
    cos, sin = jnp.cos(ang), jnp.sin(ang)

    q = (_rmsnorm(c_q, q_lat_norm) @ w_uq).reshape(b, s, N_HEADS_B, QK_NOPE + QK_ROPE)
    q_nope = q[..., :QK_NOPE]
    q_rope = _rope(q[..., QK_NOPE:], cos[:, None, :], sin[:, None, :])
    kv = (_rmsnorm(c_kv, kv_lat_norm) @ w_ukv).reshape(b, s, N_HEADS_B, QK_NOPE + V_DIM)
    k_nope = kv[..., :QK_NOPE].transpose(0, 2, 1, 3).astype(jnp.float32)
    v = kv[..., QK_NOPE:].transpose(0, 2, 1, 3).astype(jnp.float32)
    k_rope = _rope(k_r, cos, sin).astype(jnp.float32)
    scale = (QK_NOPE + QK_ROPE) ** -0.5

    nq = s // Q_BLOCK
    qn_blk = q_nope.reshape(b, nq, Q_BLOCK, N_HEADS_B, QK_NOPE).transpose(1, 0, 3, 2, 4)
    qr_blk = q_rope.reshape(b, nq, Q_BLOCK, N_HEADS_B, QK_ROPE).transpose(1, 0, 3, 2, 4)

    def block(args):
        qn, qr = args
        sc = (jnp.einsum('bhqd,bhkd->bhqk', qn.astype(jnp.float32), k_nope)
              + jnp.einsum('bhqr,bkr->bhqk', qr.astype(jnp.float32), k_rope)) * scale
        p = jax.nn.softmax(sc, axis=-1)
        return jnp.einsum('bhqk,bhkd->bhqd', p, v)

    o = lax.map(block, (qn_blk, qr_blk))
    return o.transpose(1, 0, 3, 2, 4).reshape(b, s, WIDTH_B).astype(c_q.dtype)

def _dwconv(u, w, bias):
    c = u.shape[-1]
    y = lax.conv_general_dilated(
        u, w[:, None, :].astype(u.dtype), window_strides=(1,),
        padding=((CONV_WIDTH // 2, CONV_WIDTH // 2),),
        dimension_numbers=('NWC', 'WIO', 'NWC'), feature_group_count=c)
    return y + bias.astype(u.dtype)

def second_inputs(seed: int = 0) -> dict:
    key = jax.random.key(seed)
    ks = jax.random.split(key, 17)
    f32 = jnp.float32

    def gain(k, n):
        return 1.0 + 0.1 * jax.random.normal(k, (DEPTH, n), f32)

    def dense(k, fan_in, fan_out):
        return jax.random.normal(k, (DEPTH, fan_in, fan_out), f32) * fan_in ** -0.5

    return {
        "x": jax.random.normal(ks[0], (BATCH, SEQ, D_MODEL), f32),
        "norm_mix_pre": gain(ks[1], D_MODEL),
        "w_in": dense(ks[2], D_MODEL, D_IN_2),
        "q_lat_norm": gain(ks[3], Q_LORA),
        "w_uq": dense(ks[4], Q_LORA, N_HEADS_B * (QK_NOPE + QK_ROPE)),
        "kv_lat_norm": gain(ks[5], KV_LORA),
        "w_ukv": dense(ks[6], KV_LORA, N_HEADS_B * (QK_NOPE + V_DIM)),
        "out_norm_a": gain(ks[7], WIDTH_A),
        "out_norm_b": gain(ks[8], WIDTH_B),
        "w_o": dense(ks[9], D_MIX, D_MODEL),
        "norm_mix_post": gain(ks[10], D_MODEL),
        "norm_ffn_pre": gain(ks[11], D_MODEL),
        "w_up": dense(ks[12], D_MODEL, 2 * D_FF),
        "conv_w": jax.random.normal(ks[13], (DEPTH, CONV_WIDTH, 2 * D_FF), f32) * CONV_WIDTH ** -0.5,
        "conv_b": 0.02 * jax.random.normal(ks[14], (DEPTH, 2 * D_FF), f32),
        "w_down": dense(ks[15], D_FF, D_MODEL),
        "norm_ffn_post": gain(ks[16], D_MODEL),
    }

def second_block(x, norm_mix_pre, w_in, q_lat_norm, w_uq, kv_lat_norm, w_ukv, out_norm_a,
              out_norm_b, w_o, norm_mix_post, norm_ffn_pre, w_up, conv_w, conv_b, w_down,
              norm_ffn_post):
    for l in range(DEPTH):
        h = _rmsnorm(x, norm_mix_pre[l])
        proj = h @ w_in[l]
        qa, ka, va, c_q, c_kv, k_r = jnp.split(proj, SPLIT_POINTS, axis=-1)
        ya = _dilated_attention(qa, ka, va)
        yb = _mla(c_q, c_kv, k_r, q_lat_norm[l], w_uq[l], kv_lat_norm[l], w_ukv[l])
        y = jnp.concatenate([_rmsnorm(ya, out_norm_a[l]), _rmsnorm(yb, out_norm_b[l])], axis=-1)
        y = y @ w_o[l]
        x = x + _rmsnorm(y, norm_mix_post[l])
        h = _rmsnorm(x, norm_ffn_pre[l])
        u = _dwconv(h @ w_up[l], conv_w[l], conv_b[l])
        g, v = u[..., :D_FF], u[..., D_FF:]
        y = (jax.nn.gelu(g, approximate=True) * v) @ w_down[l]
        x = x + _rmsnorm(y, norm_ffn_post[l])
    return x


def setup_inputs(seed=0):
    out = dict(first_inputs(seed))
    for name, value in second_inputs(seed + 1).items():
        if name != "x":
            out[name + "_2"] = value
    return out


def reference(
    x, c, ctx, c_ctx, w_mod, b_mod, norm_mix_g, norm_ffn_g, w_in, conv_w, a_log_f, a_log_b,
    dt_bias_f, dt_bias_b, gdn_norm_g, gla_gate_w_f, gla_gate_w_b, gla_gate_b_f, gla_gate_b_b,
    gla_norm_g, w_out_a, w_out_b, w_out, w_router, b_router, w_gu, b_gu, w_down, b_down,
    final_norm_g, norm_mix_pre_2, w_in_2, q_lat_norm_2, w_uq_2, kv_lat_norm_2, w_ukv_2,
    out_norm_a_2, out_norm_b_2, w_o_2, norm_mix_post_2, norm_ffn_pre_2, w_up_2, conv_w_2,
    conv_b_2, w_down_2, norm_ffn_post_2,
):
    x = first_block(
        x, c, ctx, c_ctx, w_mod, b_mod, norm_mix_g, norm_ffn_g, w_in, conv_w, a_log_f, a_log_b,
        dt_bias_f, dt_bias_b, gdn_norm_g, gla_gate_w_f, gla_gate_w_b, gla_gate_b_f,
        gla_gate_b_b, gla_norm_g, w_out_a, w_out_b, w_out, w_router, b_router, w_gu, b_gu,
        w_down, b_down, final_norm_g,
    )
    return second_block(
        x, norm_mix_pre_2, w_in_2, q_lat_norm_2, w_uq_2, kv_lat_norm_2, w_ukv_2, out_norm_a_2,
        out_norm_b_2, w_o_2, norm_mix_post_2, norm_ffn_pre_2, w_up_2, conv_w_2, conv_b_2,
        w_down_2, norm_ffn_post_2,
    )


_drawn_inputs = setup_inputs


def setup_inputs(seed=0):
    import zlib

    import numpy as np

    out = dict(_drawn_inputs(seed))
    spreads = {}
    factors = {'q_lat_norm_2': 4.714, 'conv_b_2': 6.953}
    for name, (base, spread) in spreads.items():
        noise = np.random.default_rng([zlib.crc32(name.encode()), seed]).standard_normal(out[name].shape)
        drawn = base * np.exp(spread * noise) if base else spread * noise
        out[name] = __import__('jax').numpy.asarray(drawn.astype(out[name].dtype))
    for name, factor in factors.items():
        out[name] = (out[name] * factor).astype(out[name].dtype)
    return out
```

```python
from contextlib import ExitStack

import numpy as np

import concourse.bass as bass
from concourse import mybir

P = 128
D = 1024
KT = D // P
L = 256
NTILE = 2 * L // P
EPS = 1e-6
NMOD = 6
HA = 8
HB = 4
GRID_W = 64
GC = 64
GATE_RANK = 16
GATE_NORM = 16.0
NE = 32
TOPK = 4
SLOTS = 64
LIMIT = 7.0
ALPHA = 1.702
UNIT = 256
HALF = 4
LEVELS = 7
NEG = -1e30
G_ZERO = -104.0

F32 = mybir.dt.float32
BF16 = mybir.dt.bfloat16
U32 = mybir.dt.uint32
I32 = mybir.dt.int32
ALU = mybir.AluOpType
ACT = mybir.ActivationFunctionType
AX = mybir.AxisListType.X


class Chain:

    def __init__(self, eng, sem, base=0):
        self.eng, self.sem, self.n = eng, sem, base

    def __call__(self, ins, n=1):
        ins.then_inc(self.sem, n)
        self.n += n
        self.eng.wait_ge(self.sem, self.n)
        return ins


class Scope:

    def __init__(self, nc, stage=""):
        self.nc, self.ctx, self.stage, self.used = nc, ExitStack(), stage, []

    def __enter__(self):
        self.ctx.__enter__()
        return self

    def __exit__(self, *a):
        if self.used and a[0] is None:
            self.nc.clear_and_free_semaphores(self.used)
            self.nc.all_engine_barrier()
        return self.ctx.__exit__(*a)

    def sb(self, name, shape, dt=F32):
        return self.ctx.enter_context(self.nc.sbuf_tensor(self.stage + name, shape, dt))

    def ps(self, name, shape, dt=F32):
        return self.ctx.enter_context(self.nc.psum_tensor(self.stage + name, shape, dt))

    def sem(self, name):
        self.used.append(self.nc.alloc_semaphore(name=self.stage + name))
        return self.used[-1]

    def sems(self, name, n):
        return [self.sem(f"{name}{i}") for i in range(n)]


def wide(ap, n):
    return ap.rearrange("p (o x) -> p o x", o=1).to_broadcast([ap.shape[0], n, ap.shape[1]])


def deep(ap, n):
    return ap.rearrange("p (x o) -> p x o", o=1).to_broadcast([ap.shape[0], ap.shape[1], n])


def modulate_stage(nc, A, C, S):
    NU = NMOD * D // 512
    RING = 3
    SMALL = 8
    with Scope(nc, "modulate_") as s:
        wm = s.sb("wm", [P, RING, KT, 512])
        ccol = s.sb("ccol", [P, KT, 2])
        ccolp = s.sb("ccolp", [P, KT, 32])
        modrow = s.sb("modrow", [P, NMOD * D])
        xc = s.sb("xc", [P, NTILE, D])
        xn = s.sb("xn", [P, 2, D])
        bcol = s.sb("bcol", [P, NMOD * KT])
        gmix = s.sb("gmix", [P, KT])
        gffn = s.sb("gffn", [P, KT])
        g1b = s.sb("g1b", [P, D])
        g2b = s.sb("g2b", [P, D])
        sel = s.sb("sel", [P, 2])
        selb = s.sb("selb", [P, P])
        junk = s.sb("junk", [P, D])
        ss = s.sb("ss", [P, NTILE])
        rstd = s.sb("rstd", [P, NTILE])
        a1 = s.sb("a1", [P, 2, KT])
        b1 = s.sb("b1", [P, 2, KT])
        mcol = s.sb("mcol", [P, NMOD * KT, 2])
        pm = s.ps("pm", [P, 2, 512])
        pt = s.ps("pt", [P, 4, 512])
        pc = s.ps("pc", [P, 512])

        s_small, s_w, s_x, s_c = s.sem("s_small"), s.sems("s_w", RING), s.sem("s_x"), s.sem("s_c")
        s_pe, s_row, s_col, s_colr = s.sem("s_pe"), s.sem("s_row"), s.sem("s_col"), s.sem("s_colr")
        s_ab, s_tr, s_ht, s_ss, s_rs = s.sem("s_ab"), s.sem("s_tr"), s.sem("s_ht"), s.sem("s_ss"), s.sem("s_rs")
        s_rv, s_xn, s_g, s_ge, s_z, s_d = s.sem("s_rv"), s.sem("s_xn"), s.sem("s_g"), s.sem("s_ge"), s.sem("s_z"), s.sem("s_d")
        xs = [xc[:, t, :] for t in range(NTILE)]
        COLS = [m * KT + k for m in (0, 1, 3, 4) for k in range(KT)]

        with nc.Block() as block:
            @block.sync
            def _(sp):
                sp.dma_start(C.const[:], A.consts).then_inc(s_small, 16)
                sp.dma_start(ccol[:], A.ccol).then_inc(s_small, 16)
                sp.dma_start(bcol[:], A.b_mod_col).then_inc(s_small, 16)
                sp.dma_start(gmix[:], A.norm_mix_col).then_inc(s_small, 16)
                sp.dma_start(gffn[:], A.norm_ffn_col).then_inc(s_small, 16)
                sp.dma_start(xc[:], A.xall.rearrange("t p d -> p t d")).then_inc(s_x, 16)
                for u in range(NU):
                    if u >= RING:
                        sp.wait_ge(s_pe, u - RING + 1)
                    sp.dma_start(wm[:, u % RING], A.w_mod[:, u * 512:(u + 1) * 512]
                                 .rearrange("(k p) n -> p k n", p=P)).then_inc(s_w[u % RING], 16)
                    if u == 2:
                        sp.dma_start(g1b[:], A.b_mod[:, 2 * D:3 * D].to_broadcast([P, D])).then_inc(s_small, 16)
                        sp.dma_start(g2b[:], A.b_mod[:, 5 * D:6 * D].to_broadcast([P, D])).then_inc(s_small, 16)
                        sp.dma_start(sel[:], A.sel).then_inc(s_small, 16)

            @block.scalar
            def _(act):
                act.wait_ge(s_small, 16 * SMALL)
                act.wait_ge(s_z, 1)
                act.activation(ccolp[:, :, 0:2], ccol[:], ACT.Silu).then_inc(s_c, 1)
                act.wait_ge(s_x, 16)
                for t in range(NTILE):
                    act.activation(junk[:], xs[t], ACT.Square, accum_out=ss[:, t:t + 1]).then_inc(s_ss, 1)
                    act.wait_ge(s_ss, t + 1)
                act.wait_ge(s_rv, 2)
                act.activation(rstd[:], ss[:], ACT.Sqrt).then_inc(s_rs, 1)
                for u in range(NU):
                    act.wait_ge(s_pe, u + 1)
                    act.activation(modrow[:, u * 512:(u + 1) * 512], pm[:, u % 2, :], ACT.Copy).then_inc(s_row, 1)

            @block.tensor
            def _(pe):
                pe.wait_ge(s_c, 1)
                for u in range(NU):
                    pe.wait_ge(s_w[u % RING], 16 * (u // RING + 1))
                    if u >= 2:
                        pe.wait_ge(s_row, u - 1)
                    for r in range(2):
                        for q in range(4):
                            k = 4 * r + q
                            m = pe.matmul(pm[32 * q:32 * q + 32, u % 2, :], ccolp[:, k, :], wm[:, u % RING, k, :],
                                          start=(r == 0), stop=(r == 1))
                    m.then_inc(s_pe, 1)
                pe.wait_ge(s_row, NU)
                for n, j in enumerate(COLS):
                    m = pe.matmul(pc[:, 2 * n:2 * n + 2], modrow[:, j * P:(j + 1) * P], sel[:], start=True, stop=True)
                m.then_inc(s_col, 1)
                pe.wait_ge(s_z, 2)
                for n, base in enumerate((2 * D, 5 * D)):
                    for h in range(2):
                        m = pe.matmul(pt[:, 2 * n + h, :], selb[:], modrow[:, base + 512 * h:base + 512 * h + 512],
                                      start=True, stop=True)
                m.then_inc(s_g, 1)
                for t in range(NTILE):
                    pe.wait_ge(s_xn, t + 1)
                    for h in range(2):
                        if t < 2:
                            pe.wait_ge(s_ge, 1 if (t, h) < (1, 0) else 2)
                        else:
                            pe.wait_ge(s_ht, (t - 2) * 2 + h + 1)
                        for k in range(4):
                            m = pe.transpose(pt[:, 2 * (t % 2) + h, k * P:(k + 1) * P],
                                             xn[:, t % 2, (4 * h + k) * P:(4 * h + k + 1) * P], C.ident)
                        m.then_inc(s_tr, 1)

            @block.vector
            def _(v):
                link = Chain(v, s_d)
                v.memset(ccolp[:], 0.0).then_inc(s_z, 1)
                v.wait_ge(s_small, 16 * SMALL)
                v.wait_ge(s_z, 1)
                v.tensor_copy(selb[:], sel[:, 0:1].to_broadcast([P, P])).then_inc(s_z, 1)
                v.wait_ge(s_ss, NTILE)
                v.tensor_scalar(ss[:], ss[:], 1.0 / D, EPS, ALU.mult, ALU.add).then_inc(s_rv, 1)
                v.wait_ge(s_rv, 1)
                v.reciprocal(ss[:], ss[:]).then_inc(s_rv, 1)
                v.wait_ge(s_rs, 1)
                for t in range(2):
                    v.tensor_scalar(xn[:, t, :], xs[t], rstd[:, t:t + 1], None, ALU.mult).then_inc(s_xn, 1)
                v.wait_ge(s_col, 1)
                for n, m in enumerate((0, 1, 3, 4)):
                    link(v.tensor_tensor(mcol[:, m * KT:(m + 1) * KT, :],
                                         pc[:, 16 * n:16 * n + 16].rearrange("p (k t) -> p k t", t=2),
                                         deep(bcol[:, m * KT:(m + 1) * KT], 2), ALU.add))
                for q in range(2):
                    link(v.scalar_tensor_tensor(a1[:, q, :], mcol[:, KT:2 * KT, q], 1.0, gmix[:], ALU.add, ALU.mult))
                    link(v.tensor_copy(b1[:, q, :], mcol[:, 0:KT, q]))
                link(v.scalar_tensor_tensor(S.a2[:], mcol[:, 4 * KT:5 * KT, 0], 1.0, gffn[:], ALU.add, ALU.mult))
                link(v.tensor_copy(S.b2[:], mcol[:, 3 * KT:4 * KT, 0]))
                v.wait_ge(s_g, 1)
                for n, (dst, row) in enumerate(((S.g1, g1b), (S.g2, g2b))):
                    for h in range(2):
                        m = v.tensor_tensor(dst[:, 512 * h:512 * h + 512], pt[:, 2 * n + h, :],
                                            row[:, 512 * h:512 * h + 512], ALU.add)
                    m.then_inc(s_ge, 1)
                for t in range(NTILE):
                    q = 1 if t < 2 else 0
                    for h in range(2):
                        v.wait_ge(s_tr, 2 * t + h + 1)
                        for k in range(4):
                            kk = 4 * h + k
                            m = v.tensor_scalar(S.hT[:, kk, t * P:(t + 1) * P], pt[:, 2 * (t % 2) + h, k * P:(k + 1) * P],
                                                a1[:, q, kk:kk + 1], b1[:, q, kk:kk + 1], ALU.mult, ALU.add)
                        m.then_inc(s_ht, 1)
                    if t < 2:
                        v.tensor_scalar(xn[:, t, :], xs[t + 2], rstd[:, t + 2:t + 3], None, ALU.mult).then_inc(s_xn, 1)


class Projector:

    def __init__(self, s, A, S, name="pj"):
        self.A, self.S = A, S
        self.ring = s.sb(name + "ring", [P, 2, KT, UNIT])
        self.bank = s.ps(name + "bank", [P, 2, 2, 512])
        self.w_in = s.sems(name + "w_landed", 2)
        self.done = s.sems(name + "unit_done", 2)
        self.out = s.sems(name + "bank_free", 2)
        self.pairs = {"sp": 0, "pe": 0, "act": 0}

    def load(self, sp, unit0, pairs):
        g0 = self.pairs["sp"]
        with sp.Fori(0, pairs) as i:
            for z in range(2):
                sp.wait_ge(self.done[z], i + (g0 + 1))
                sp.dma_start(self.ring[:, z], self.A.w_in_units[bass.ds(i * 2 + (unit0 + z), 1)]
                             .rearrange("u p k n -> p (u k) n")).then_inc(self.w_in[z], 16)
        self.pairs["sp"] += pairs

    def credit_pe(self, pe):
        for z in range(2):
            pe.sem_inc(self.done[z], 1)

    def credit_act(self, act):
        for z in range(2):
            act.sem_inc(self.out[z], 1)

    def multiply(self, pe, pairs, tok0, ntok):
        g0 = self.pairs["pe"]
        with pe.Fori(0, pairs) as i:
            for z in range(2):
                pe.wait_ge(self.w_in[z], i * 16 + 16 * (g0 + 1))
                pe.wait_ge(self.out[z], i + (g0 + 1))
                for j in range(2):
                    for k in range(KT):
                        m = pe.matmul(self.bank[:, z, j, 0:ntok], self.ring[:, z, k, j * P:(j + 1) * P],
                                      self.S.hT[:, k, tok0:tok0 + ntok], start=(k == 0), stop=(k == KT - 1))
                m.then_inc(self.done[z], 1)
        self.pairs["pe"] += pairs

    def evacuate(self, act, pairs, dst, tile0, ntok, sem=None):
        g0 = self.pairs["act"]
        with act.Fori(0, pairs) as i:
            for z in range(2):
                act.wait_ge(self.done[z], i + (g0 + 2))
                for j in range(2):
                    m = act.activation(dst[:, bass.ds(i * 4 + (tile0 + 2 * z + j), 1), :],
                                       self.bank[:, z, j:j + 1, 0:ntok], ACT.Copy)
                m.then_inc(self.out[z], 1)
                if sem is not None:
                    act.wait_ge(self.out[z], i + (g0 + 2))
                    act.sem_inc(sem, 1)
        self.pairs["act"] += pairs


def delta_project_stage(nc, A, C, S):
    with Scope(nc, "delta_project_") as s:
        pj = Projector(s, A, S)
        ws = s.sb("ws", [P, KT, 64])
        cw = s.sb("cw", [P, 24, 9])
        acc = s.sb("acc", [P, 2, 512])
        ssm = s.ps("ssm", [P, 2, 512])
        s_in, s_sm, s_pj = s.sem("s_in"), s.sem("s_sm"), s.sem("s_pj")
        s_k = s.sem("s_k")
        s_se = s.sem("s_se")

        with nc.Block() as block:
            @block.sync
            def _(sp):
                sp.dma_start(ws[:], A.w_small).then_inc(s_in, 16)
                sp.dma_start(cw[:], A.conv_w_col).then_inc(s_in, 16)
                pj.load(sp, 0, 2)
                pj.load(sp, 4, 4)

            @block.tensor
            def _(pe):
                pj.credit_pe(pe)
                pe.wait_ge(s_in, 32)
                for n, (c0, w) in enumerate(SMALL_COLS):
                    q, b = n % 3, n // 3
                    for k in range(KT):
                        m = pe.matmul(ssm[32 * q:32 * q + w, b, :], ws[:, k, c0:c0 + w], S.hT[:, k, :],
                                      start=(k == 0), stop=(k == KT - 1))
                m.then_inc(s_sm, 1)
                pj.multiply(pe, 2, L, L)
                pj.multiply(pe, 4, 0, 2 * L)

            @block.scalar
            def _(act):
                pj.credit_act(act)
                act.wait_ge(s_sm, 1)
                for n, ((c0, w), dst) in enumerate(zip(SMALL_COLS, (S.bf, S.bb, S.af, S.ab, S.lf, S.lb))):
                    q, b = n % 3, n // 3
                    m = act.activation(dst[:], ssm[32 * q:32 * q + w, b, :], ACT.Copy)
                m.then_inc(s_se, 1)
                pj.evacuate(act, 2, S.pq, 0, L, s_pj)
                pj.evacuate(act, 4, S.pkv, 0, 2 * L, s_pj)
                act.wait_ge(s_se, 1)

            @block.vector
            def _(v):
                def taps(dst, src, w, image, base):
                    n = 1
                    v.tensor_scalar(dst, src, w(4), None, ALU.mult).then_inc(s_k, 1)
                    for dr in (-1, 0, 1):
                        for dc in (-1, 0, 1):
                            if (dr, dc) == (0, 0) or (not image and dr):
                                continue
                            width = GRID_W if image else L
                            rows = L // width
                            o = dst.rearrange("p (r c) -> p r c", c=width)
                            x = src.rearrange("p (r c) -> p r c", c=width)
                            r0, r1 = max(0, -dr), min(rows, rows - dr)
                            c0, c1 = max(0, -dc), min(width, width - dc)
                            oo, xx = o[:, r0:r1, c0:c1], x[:, r0 + dr:r1 + dr, c0 + dc:c1 + dc]
                            v.wait_ge(s_k, base + n)
                            v.scalar_tensor_tensor(oo, xx, w(3 * (dr + 1) + dc + 1), oo,
                                                   ALU.mult, ALU.add).then_inc(s_k, 1)
                            n += 1
                    return n

                v.wait_ge(s_in, 32)
                for t0, buf, units, first, per, base0 in ((0, S.pq, 4, 0, 10, 1), (8, S.pkv, 8, 4, 13, 81)):
                    with v.Fori(0, units) as i:
                        v.wait_ge(s_pj, i + (first + 1))
                        for z in range(2):
                            base = i * (2 * per) + (z * per + base0)
                            src = buf[:, bass.ds(i * 2 + z, 1), :].rearrange("p o n -> p (o n)")
                            w = lambda j: cw[:, bass.ds(i * 2 + (z + t0), 1), j:j + 1].rearrange("p o n -> p (o n)")
                            v.wait_ge(s_k, base)
                            if t0 == 0:
                                n = taps(acc[:, z, L:2 * L], src, w, True, base)
                                span = (L, 2 * L)
                            else:
                                n = taps(acc[:, z, L:2 * L], src[:, L:2 * L], w, True, base)
                                n += taps(acc[:, z, 0:L], src[:, 0:L], w, False, base + n)
                                span = (0, 2 * L)
                            v.wait_ge(s_k, base + n)
                            v.tensor_scalar(src, acc[:, z, span[0]:span[1]], 1.0, None, ALU.mult).then_inc(s_k, 1)
                            assert n + 1 == per

            @block.gpsimd
            def _(g):
                g.sem_inc(s_k, 1)


SMALL_COLS = ((0, 8), (8, 8), (16, 8), (24, 8), (32, 16), (48, 16))


def delta_gate_stage(nc, A, C, S):
    with Scope(nc, "delta_gate_") as s:
        sm = s.sb("sm", [HA, 2, 2 * L])
        al, dtb = s.sb("al", [HA, 2]), s.sb("dtb", [HA, 2])
        x = s.sb("x_", [HA, 4, 2 * L])
        nx = s.sb("nx", [HA, 4, 2 * L])
        u = s.sb("u", [HA, 4, 2 * L])
        w = s.sb("w", [HA, 4, 2 * L])
        r = s.sb("r", [HA, 4, 2 * L])
        m = s.sb("m", [HA, 4, 2 * L])
        g = s.sb("g", [HA, 2, 2 * L])
        rows = s.sb("rows", [HA, 2, 2, 2 * L])
        quant = s.sb("quant", [P, 2, 2 * L])
        pt = s.ps("pt", [P, 2, 512])
        s_in, s_v, s_a, s_o, s_t = s.sem("s_in"), s.sem("s_v"), s.sem("s_a"), s.sem("s_o"), s.sem("s_t")
        V = {}
        with nc.Block() as block:
            @block.sync
            def _(sp):
                sp.dma_start(sm[:], A.scan_masks[0:HA, 0:2]).then_inc(s_in, 16)
                sp.dma_start(al[:], A.a_log).then_inc(s_in, 16)
                sp.dma_start(dtb[:], A.dt_bias).then_inc(s_in, 16)
                sp.wait_ge(s_v, 23)
                for d in range(2):
                    for k in range(2):
                        sp.dma_start(A.row_scratch[d, :, k].rearrange("t h n -> h t n"),
                                     rows[:, d, k, :].rearrange("h (t n) -> h t n", n=P)).then_inc(s_o, 16)
                sp.wait_ge(s_o, 64)

            @block.vector
            def _(v):
                link = Chain(v, s_v)
                v.wait_ge(s_in, 48)
                for d, a in enumerate((S.af, S.ab)):
                    link(v.tensor_scalar(x[:, d, :], a[:], dtb[:, d:d + 1], None, ALU.add))
                for d, b in enumerate((S.bf, S.bb)):
                    link(v.tensor_copy(x[:, 2 + d, :], b[:]))
                link(v.tensor_scalar(nx[:], x[:], -1.0, None, ALU.mult))
                link(v.tensor_tensor(nx[:], nx[:], x[:], ALU.min))
                v.wait_ge(s_a, 1)
                link(v.tensor_scalar(w[:], u[:], 1.0, None, ALU.add))
                link(v.tensor_scalar(m[:], w[:], 1.0, None, ALU.is_equal))
                link(v.scalar_tensor_tensor(nx[:], w[:], -1.0, m[:], ALU.add, ALU.add))
                link(v.reciprocal(nx[:], nx[:]))
                link(v.tensor_tensor(nx[:], nx[:], u[:], ALU.mult))
                link(v.tensor_tensor(m[:], m[:], u[:], ALU.mult))
                v.wait_ge(s_a, 2)
                link(v.tensor_tensor(r[:], r[:], nx[:], ALU.mult))
                link(v.tensor_tensor(r[:], r[:], m[:], ALU.add))
                link(v.scalar_tensor_tensor(u[:, 0:2, :], x[:, 0:2, :], 0.0, r[:, 0:2, :], ALU.max, ALU.add))
                link(v.scalar_tensor_tensor(u[:, 2:4, :], x[:, 2:4, :], 0.0, r[:, 2:4, :], ALU.min, ALU.subtract))
                v.wait_ge(s_a, 3)
                for d in range(2):
                    link(v.tensor_scalar(g[:, d, :], u[:, d, :], al[:, d:d + 1], -1.0, ALU.mult, ALU.mult))
                link(v.tensor_scalar(g[:], g[:], G_ZERO, None, ALU.max))
                link(v.tensor_tensor_scan(rows[:, 0, 1, :], sm[:, 0, :], g[:, 0, :], 0.0, ALU.mult, ALU.add))
                link(v.tensor_tensor_scan(rows[:, 1, 1, ::-1], sm[:, 1, ::-1], g[:, 1, ::-1], 0.0, ALU.mult, ALU.add))
                for d in range(2):
                    link(v.tensor_tensor(rows[:, d, 0, :], rows[:, d, 1, :], u[:, 2 + d, :], ALU.add))
                link(v.memset(quant[:], 0.0))
                for d in range(2):
                    gc = rows[:, d, 1, :].rearrange("h (t n) -> h t n", n=P)
                    end = P - 1 if d == 0 else 0
                    link(v.tensor_scalar(quant[0:HA, d, :], rows[:, d, 1, :], -1.0, None, ALU.mult))
                    link(v.tensor_tensor(w[:, d, :].rearrange("h (t n) -> h t n", n=P),
                                         gc[:, :, end:end + 1].to_broadcast([HA, NTILE, P]), gc, ALU.subtract))
                v.wait_ge(s_a, 4)
                for d in range(2):
                    link(v.scalar_tensor_tensor(m[:, d, :], u[:, d, :], -1.0, x[:, 2 + d, :], ALU.mult, ALU.mult))
                for d in range(2):
                    link(v.tensor_copy(quant[64:64 + HA, d, :], m[:, d, :]))
                for d in range(2):
                    v.wait_ge(s_t, d + 1)
                    link(v.tensor_copy(S.tokq[:, d], pt[:, d, :].rearrange("p (t n) -> p t n", n=P)))

            @block.scalar
            def _(act):
                act.wait_ge(s_v, 6)
                act.activation(u[:], nx[:], ACT.Exp).then_inc(s_a, 1)
                act.wait_ge(s_v, 7)
                act.activation(r[:], w[:], ACT.Ln).then_inc(s_a, 1)
                act.wait_ge(s_in, 48)
                act.activation(al[:], al[:], ACT.Exp).then_inc(s_a, 1)
                act.wait_ge(s_v, 28)
                for d in range(2):
                    i = act.activation(u[:, d, :], rows[:, d, 1, :], ACT.Exp)
                for d in range(2):
                    i = act.activation(quant[96:96 + HA, d, :], w[:, d, :], ACT.Exp)
                for d in range(2):
                    i = act.activation(x[:, 2 + d, :], x[:, 2 + d, :], ACT.Sigmoid)
                i.then_inc(s_a, 1)
                act.wait_ge(s_a, 4)
                for d in range(2):
                    i = act.activation(quant[32:32 + HA, d, :], x[:, 2 + d, :], ACT.Copy)
                i.then_inc(s_a, 1)

            @block.tensor
            def _(pe):
                pe.wait_ge(s_v, 32)
                pe.wait_ge(s_a, 5)
                for d in range(2):
                    for t in range(NTILE):
                        i = pe.transpose(pt[:, d, t * P:(t + 1) * P], quant[:, d, t * P:(t + 1) * P], C.ident)
                    i.then_inc(s_t, 1)


def delta_scan_stage(nc, A, C, S):
    G = HA // HALF
    W = HALF * P
    DK = float(P) ** -0.5
    with Scope(nc, "delta_scan_") as s:
        lvl = s.sb("lvl", [P, 2, LEVELS, P])
        strict = s.sb("strict", [P, 2, 2, P])
        ksl = s.sb("ksl", [P, HALF, 2 * L])
        qsl = s.sb("qsl", [P, HALF, L])
        tmp = s.sb("tmp", [P, HALF, 2 * L])
        ktok = s.sb("ktok", [P, NTILE, HALF, P])
        vtok = s.sb("vtok", [P, NTILE, HALF, P])
        tq = s.sb("tq", [P, 2, NTILE, 4, HALF])
        d2 = range(2)
        rw = [s.sb(f"rw{d}", [P, 2, HALF, P]) for d in d2]
        eg = [s.sb(f"eg{d}", [P, HALF, P]) for d in d2]
        egl = [s.sb(f"egl{d}", [P, 2, HALF]) for d in d2]
        mt = [s.sb(f"mt{d}", [P, HALF, P]) for d in d2]
        ms = [s.sb(f"ms{d}", [P, 3, HALF, P]) for d in d2]
        tt = [s.sb(f"tt{d}", [P, HALF, P]) for d in d2]
        t_ = [s.sb(f"t{d}", [P, HALF, P]) for d in d2]
        y = [s.sb(f"y{d}", [P, HALF, P]) for d in d2]
        at = [s.sb(f"at{d}", [P, HALF, P]) for d in d2]
        qg = [s.sb(f"qg{d}", [P, 2, HALF, P]) for d in d2]
        vb = [s.sb(f"vb{d}", [P, HALF, P]) for d in d2]
        kd = [s.sb(f"kd{d}", [P, HALF, P]) for d in d2]
        rr = [s.sb(f"rr{d}", [P, HALF, P]) for d in d2]
        vn = [s.sb(f"vn{d}", [P, HALF, P]) for d in d2]
        st = [s.sb(f"st{d}", [P, HALF, P]) for d in d2]
        bank = [[s.ps(f"bank{d}{b}", [P, HALF, P]) for b in range(4)] for d in d2]
        pa, pb, pc, pd = ([bank[d][b] for d in d2] for b in range(4))
        allbank = [bank[d][b] for d in d2 for b in range(4)]

        s_in = s.sem("s_in")
        s_si, s_sq, s_ss, s_rv, s_rt, s_nm = (s.sem(n) for n in ("s_si", "s_sq", "s_ss", "s_rv", "s_rt", "s_nm"))
        s_kt, s_ktc, s_vs, s_vt, s_vtc, s_tq = (s.sem(n) for n in ("s_kt", "s_ktc", "s_vs", "s_vt", "s_vtc", "s_tq"))
        rowsem, s_v0 = s.sems("rows_in", 2), s.sem("sums_read")
        (s_eg, s_dm, s_vk, s_g, s_mt, s_ms, s_m1, s_t0, s_y, s_yc, s_dl, s_t, s_ks, s_r, s_vn, s_vnc, s_o,
         s_oc, s_kv, s_s, s_mk, s_qg) = (s.sems(n, 2) for n in (
             "eg_done", "decay_done", "vk_scaled", "gram_done", "mt_done", "masked", "m1_done", "t_start",
             "y_done", "y_copied", "delta_done", "t_updated", "ks_done", "r_done", "vnew_done", "vnew_copied",
             "o_done", "o_copied", "kv_done", "state_done", "mask_added", "qg_done"))

        def tile(d, n):
            return n if d == 0 else (n ^ 1)

        with nc.Block() as block:
            @block.sync
            def _(sp):
                sp.dma_start(lvl[:], A.level_masks).then_inc(s_in, 16)
                sp.dma_start(strict[:], A.tri_masks).then_inc(s_in, 16)
                with sp.Fori(0, G) as i:
                    for n in range(NTILE):
                        for d in d2:
                            sp.wait_ge(s_mt[d], i * NTILE + (n + 1))
                            sp.dma_start(rw[d][:], A.row_scratch[d, tile(d, n)]
                                         [:, bass.ds(i * HALF, HALF), :].rearrange("(o k) h n -> o k h n", o=1)
                                         .to_broadcast([P, 2, HALF, P])).then_inc(rowsem[d], 16)

            @block.scalar
            def _(act):
                act.wait_ge(s_in, 32)

                def prep(n):
                    for d in d2:
                        lat = n >= 2
                        act.wait_ge(rowsem[d], i * (16 * NTILE) + 16 * (n + 1))
                        act.wait_ge(s_qg[d], i * NTILE + (n + 1))
                        act.activation(eg[d][:], rw[d][:, 1], ACT.Exp).then_inc(s_eg[d], 1)
                        act.wait_ge(s_mk[d], i * NTILE + (n + 1))
                        for k in range(2 if lat else 1):
                            for h in range(HALF):
                                m = act.activation(rw[d][:, k, h, :], rw[d][:, k, h, :], ACT.Exp,
                                                   bias=tq[:, d, tile(d, n), 0, h:h + 1])
                        m.then_inc(s_dm[d], 1)

                with act.Fori(0, G) as i:
                    act.wait_ge(s_vn[0], i * NTILE + 1)
                    act.wait_ge(s_vn[1], i * NTILE + 1)
                    act.wait_ge(s_qg[0], i * NTILE + 1)
                    act.wait_ge(s_qg[1], i * NTILE + 1)
                    act.activation(ksl[:], S.pkv[:, bass.ds(i * HALF, HALF), :], ACT.Silu)
                    act.activation(qsl[:], S.pq[:, bass.ds(i * HALF, HALF), :], ACT.Silu).then_inc(s_si, 1)
                    act.wait_ge(s_rv, i * 2 + 1)
                    act.activation(tmp[:], tmp[:], ACT.Sqrt).then_inc(s_rt, 1)
                    act.wait_ge(s_rv, i * 2 + 2)
                    act.activation(tmp[:, :, 0:L], tmp[:, :, 0:L], ACT.Sqrt).then_inc(s_rt, 1)
                    act.wait_ge(s_nm, i * 2 + 2)
                    act.activation(tmp[:], S.pkv[:, bass.ds(i * HALF + HA, HALF), :], ACT.Silu).then_inc(s_vs, 1)
                    for b in range(4):
                        act.wait_ge(s_kt, i * 4 + (b + 1))
                        act.activation(ktok[:, b], bank[0][b][:], ACT.Copy).then_inc(s_ktc, 1)
                    for b in range(4):
                        act.wait_ge(s_vt, i * 4 + (b + 1))
                        act.activation(vtok[:, b], bank[1][b][:], ACT.Copy).then_inc(s_vtc, 1)
                    act.wait_ge(s_tq, i + 1)
                    act.wait_ge(s_vtc, i * 4 + 4)
                    act.wait_ge(s_ktc, i * 4 + 4)
                    prep(0)
                    for n in range(NTILE):
                        for l in range(1, LEVELS):
                            for d in d2:
                                act.wait_ge(s_y[d], i * (6 * NTILE) + (6 * n + l))
                                act.activation(y[d][:], pa[d][:], ACT.Copy).then_inc(s_yc[d], 1)
                            if l == 2:
                                for d in d2:
                                    act.wait_ge(s_r[d], i * NTILE + (n + 1))
                                    if n > 0:
                                        act.wait_ge(s_kv[d], i * 3 + n)
                                    for h in range(HALF):
                                        act.activation(vb[d][:, h, :], vtok[:, tile(d, n), h, :], ACT.Copy,
                                                       scale=tq[:, d, tile(d, n), 1, h:h + 1])
                                    for h in range(HALF):
                                        m = act.activation(kd[d][:, h, :], ktok[:, tile(d, n), h, :], ACT.Copy,
                                                           scale=tq[:, d, tile(d, n), 3, h:h + 1])
                                    m.then_inc(s_vk[d], 1)
                            if l == 4 and n + 1 < NTILE:
                                prep(n + 1)
                        for d in d2:
                            act.wait_ge(s_vn[d], i * NTILE + (n + 2))
                            act.activation(vn[d][:], pc[d][:], ACT.Copy).then_inc(s_vnc[d], 1)

            @block.gpsimd
            def _(g):
                for d in d2:
                    for q in (s_mt, s_qg, s_r, s_vn, s_s, s_oc):
                        g.sem_inc(q[d], 1)
                g.wait_ge(s_in, 32)

                def prep(n):
                    for d in d2:
                        end = P - 1 if d == 0 else 0
                        g.wait_ge(s_eg[d], i * NTILE + (n + 1))
                        for k in range(2 if n >= 2 else 1):
                            m = g.tensor_tensor(rw[d][:, k], rw[d][:, k], wide(strict[:, d, k, :], HALF), ALU.add)
                        m.then_inc(s_mk[d], 1)
                        if n >= 2:
                            t0 = (tile(d, n) - 2) * P
                            g.tensor_tensor(qg[d][:, n % 2], eg[d][:], qsl[:, :, t0:t0 + P], ALU.mult)
                        g.tensor_copy(egl[d][:, n % 2, :], eg[d][:, :, end]).then_inc(s_qg[d], 1)

                with g.Fori(0, G) as i:
                    g.wait_ge(s_si, i + 1)
                    g.tensor_tensor(tmp[:], ksl[:], ksl[:], ALU.mult).then_inc(s_sq, 1)
                    g.wait_ge(s_nm, i * 2 + 1)
                    g.tensor_tensor(tmp[:, :, 0:L], qsl[:], qsl[:], ALU.mult).then_inc(s_sq, 1)
                    g.wait_ge(s_nm, i * 2 + 2)
                    prep(0)
                    for n in range(NTILE):
                        for l in range(LEVELS):
                            for d in d2:
                                g.wait_ge(s_mt[d], i * NTILE + (n + 2))
                                if l >= 3:
                                    g.wait_ge(s_y[d] if l > 3 else s_t0[d],
                                              i * (6 * NTILE) + (6 * n + l - 3) if l > 3 else i * NTILE + (n + 1))
                                g.tensor_tensor(ms[d][:, l % 3], mt[d][:], wide(lvl[:, d, l, :], HALF),
                                                ALU.mult).then_inc(s_ms[d], 1)
                            if l == 5 and n + 1 < NTILE:
                                prep(n + 1)

            @block.vector
            def _(v):
                v.wait_ge(s_in, 32)
                with v.Fori(0, G) as i:
                    for d in d2:
                        for k in range(4):
                            m = v.tensor_copy(tq[:, d, :, k, :], S.tokq[:, d, :, bass.ds(i * HALF + 32 * k, HALF)])
                    m.then_inc(s_tq, 1)
                    for h in range(HALF):
                        v.wait_ge(s_ss, i * 8 + (h + 1))
                        m = v.tensor_scalar(tmp[:, h, :], allbank[h][:].rearrange("p a n -> p (a n)"), EPS, None, ALU.add)
                    m.then_inc(s_v0, 1)
                    v.wait_ge(s_v0, i * 2 + 1)
                    v.reciprocal(tmp[:], tmp[:]).then_inc(s_rv, 1)
                    v.wait_ge(s_rt, i * 2 + 1)
                    v.tensor_tensor(ksl[:], ksl[:], tmp[:], ALU.mult).then_inc(s_nm, 1)
                    for h in range(HALF):
                        v.wait_ge(s_ss, i * 8 + (4 + h + 1))
                        m = v.tensor_scalar(tmp[:, h, 0:L], allbank[4 + h][:].rearrange("p a n -> p (a n)")[:, 0:L],
                                            EPS, None, ALU.add)
                    m.then_inc(s_v0, 1)
                    v.wait_ge(s_v0, i * 2 + 2)
                    v.reciprocal(tmp[:, :, 0:L], tmp[:, :, 0:L]).then_inc(s_rv, 1)
                    v.wait_ge(s_rt, i * 2 + 2)
                    v.scalar_tensor_tensor(qsl[:], qsl[:], DK, tmp[:, :, 0:L], ALU.mult, ALU.mult).then_inc(s_nm, 1)
                    for n in range(NTILE):
                        lat = n >= 2
                        for d in d2:
                            v.wait_ge(s_dm[d], i * NTILE + (n + 1))
                            v.wait_ge(s_g[d], i * NTILE + (n + 1))
                            m = v.scalar_tensor_tensor(mt[d][:], pa[d][:], -1.0, rw[d][:, 0], ALU.mult, ALU.mult)
                            if lat:
                                m = v.tensor_tensor(at[d][:], pb[d][:], rw[d][:, 1], ALU.mult)
                            m.then_inc(s_mt[d], 1)
                        for d in d2:
                            v.wait_ge(s_m1[d], i * NTILE + (n + 1))
                            v.tensor_tensor(tt[d][:], ms[d][:, 0], wide(C.ident, HALF), ALU.add)
                            v.tensor_tensor(t_[d][:], pc[d][:], wide(C.ident, HALF), ALU.add).then_inc(s_t0[d], 1)
                        for l in range(1, LEVELS):
                            for d in d2:
                                v.wait_ge(s_dl[d], i * (6 * NTILE) + (6 * n + l))
                                m = v.tensor_tensor(tt[d][:], tt[d][:], pc[d][:], ALU.add)
                                if l < LEVELS - 1:
                                    m = v.tensor_tensor(t_[d][:], t_[d][:], pb[d][:], ALU.add)
                                m.then_inc(s_t[d], 1)
                        for d in d2:
                            v.wait_ge(s_vk[d], i * NTILE + (n + 1))
                            if n == 0:
                                v.tensor_copy(rr[d][:], vb[d][:]).then_inc(s_r[d], 1)
                            else:
                                v.wait_ge(s_ks[d], i * 3 + n)
                                for h in range(HALF):
                                    m = v.scalar_tensor_tensor(rr[d][:, h, :], pb[d][:, h, :],
                                                               tq[:, d, tile(d, n), 2, h:h + 1], vb[d][:, h, :],
                                                               ALU.mult, ALU.add)
                                m.then_inc(s_r[d], 1)
                        for d in d2:
                            if n < NTILE - 1:
                                v.wait_ge(s_kv[d], i * 3 + (n + 1))
                                if n == 0:
                                    m = v.tensor_copy(st[d][:], pa[d][:])
                                else:
                                    for h in range(HALF):
                                        m = v.scalar_tensor_tensor(st[d][:, h, :], st[d][:, h, :],
                                                                   egl[d][:, n % 2, h:h + 1], pa[d][:, h, :],
                                                                   ALU.mult, ALU.add)
                                m.then_inc(s_s[d], 1)
                        if lat:
                            for d in d2:
                                v.wait_ge(s_o[d], i * 2 + (n - 1))
                                t0 = (tile(d, n) - 2) * P
                                dst = S.oa[:, bass.ds(i * HALF, HALF), t0:t0 + P]
                                if n == 2:
                                    m = v.tensor_copy(dst, pd[d][:])
                                else:
                                    m = v.tensor_tensor(dst, dst, pd[d][:], ALU.add)
                                m.then_inc(s_oc[d], 1)

            @block.tensor
            def _(pe):
                with pe.Fori(0, G) as i:
                    for d in d2:
                        pe.wait_ge(s_oc[d], i * 2 + 1)
                    for h in range(HALF):
                        if h == 0:
                            pe.wait_ge(s_sq, i * 2 + 1)
                        pe.matmul(allbank[h][:].rearrange("p a n -> p (a n)"), C.ones, tmp[:, h, :],
                                  start=True, stop=True).then_inc(s_ss, 1)
                    for h in range(HALF):
                        if h == 0:
                            pe.wait_ge(s_sq, i * 2 + 2)
                        pe.matmul(allbank[4 + h][:].rearrange("p a n -> p (a n)")[:, 0:L], C.ones, tmp[:, h, 0:L],
                                  start=True, stop=True).then_inc(s_ss, 1)
                    pe.wait_ge(s_nm, i * 2 + 2)
                    for t in range(NTILE):
                        for h in range(HALF):
                            m = pe.transpose(bank[0][t][:, h, :], ksl[:, h, t * P:(t + 1) * P], C.ident)
                        m.then_inc(s_kt, 1)
                    pe.wait_ge(s_vs, i + 1)
                    for t in range(NTILE):
                        for h in range(HALF):
                            m = pe.transpose(bank[1][t][:, h, :], tmp[:, h, t * P:(t + 1) * P], C.ident)
                        m.then_inc(s_vt, 1)
                    pe.wait_ge(s_ktc, i * 4 + 4)
                    pe.wait_ge(s_vtc, i * 4 + 4)
                    for n in range(NTILE):
                        lat = n >= 2
                        for d in d2:
                            t0 = tile(d, n) * P
                            if 0 < n:
                                pe.wait_ge(s_s[d], i * 3 + (n + 1))
                                pe.wait_ge(s_r[d], i * NTILE + (n + 1))
                            for h in range(HALF):
                                m = pe.matmul(pa[d][:, h, :], ksl[:, h, t0:t0 + P], ksl[:, h, t0:t0 + P],
                                              start=True, stop=True)
                            if lat:
                                for h in range(HALF):
                                    m = pe.matmul(pb[d][:, h, :], ksl[:, h, t0:t0 + P],
                                                  qsl[:, h, t0 - L:t0 - L + P], start=True, stop=True)
                            m.then_inc(s_g[d], 1)
                        for d in d2:
                            pe.wait_ge(s_ms[d], i * (LEVELS * NTILE) + (LEVELS * n + 1))
                            if n > 0:
                                pe.wait_ge(s_vnc[d], i * NTILE + n)
                            for h in range(HALF):
                                m = pe.transpose(pc[d][:, h, :], ms[d][:, 0, h, :], C.ident)
                            m.then_inc(s_m1[d], 1)
                        for l in range(1, LEVELS):
                            for d in d2:
                                pe.wait_ge(s_ms[d], i * (LEVELS * NTILE) + (LEVELS * n + l + 1))
                                if l == 1:
                                    pe.wait_ge(s_t0[d], i * NTILE + (n + 1))
                                else:
                                    pe.wait_ge(s_t[d], i * (6 * NTILE) + (6 * n + l - 1))
                                for h in range(HALF):
                                    m = pe.matmul(pa[d][:, h, :], ms[d][:, l % 3, h, :], t_[d][:, h, :],
                                                  start=True, stop=True)
                                m.then_inc(s_y[d], 1)
                            for d in d2:
                                pe.wait_ge(s_yc[d], i * (6 * NTILE) + (6 * n + l))
                                for h in range(HALF):
                                    if l < LEVELS - 1:
                                        pe.matmul(pb[d][:, h, :], tt[d][:, h, :], y[d][:, h, :],
                                                  start=True, stop=True)
                                    m = pe.matmul(pc[d][:, h, :], y[d][:, h, :], tt[d][:, h, :],
                                                  start=True, stop=True)
                                m.then_inc(s_dl[d], 1)
                        if n > 0:
                            for d in d2:
                                t0 = tile(d, n) * P
                                pe.wait_ge(s_t[d], i * (6 * NTILE) + (6 * n + LEVELS - 2))
                                for h in range(HALF):
                                    m = pe.matmul(pb[d][:, h, :], ksl[:, h, t0:t0 + P], st[d][:, h, :],
                                                  start=True, stop=True)
                                m.then_inc(s_ks[d], 1)
                        for d in d2:
                            pe.wait_ge(s_t[d], i * (6 * NTILE) + (6 * n + LEVELS - 1))
                            pe.wait_ge(s_r[d], i * NTILE + (n + 2))
                            for h in range(HALF):
                                m = pe.matmul(pc[d][:, h, :], tt[d][:, h, :], rr[d][:, h, :], start=True, stop=True)
                            m.then_inc(s_vn[d], 1)
                        for d in d2:
                            pe.wait_ge(s_vnc[d], i * NTILE + (n + 1))
                            if lat:
                                pe.wait_ge(s_oc[d], i * 2 + (n - 1))
                                for h in range(HALF):
                                    pe.matmul(pd[d][:, h, :], vn[d][:, h, :], at[d][:, h, :],
                                              start=True, stop=False)
                                    m = pe.matmul(pd[d][:, h, :], st[d][:, h, :], qg[d][:, n % 2, h, :],
                                                  start=False, stop=True)
                                m.then_inc(s_o[d], 1)
                            if n < NTILE - 1:
                                for h in range(HALF):
                                    m = pe.matmul(pa[d][:, h, :], kd[d][:, h, :], vn[d][:, h, :],
                                                  start=True, stop=True)
                                m.then_inc(s_kv[d], 1)


def linear_attention_stage(nc, A, C, S):
    d2 = range(2)
    DK = float(P) ** -0.5
    IG = 1.0 / GATE_NORM
    NH = HB
    DV2 = 2
    with Scope(nc, "linear_") as s:
        gq = s.sb("gq", [P, NH, L])
        gkv = s.sb("gkv", [P, NH + NH * DV2, 2 * L])
        with Scope(nc, "linear_project_") as q:
            pj = Projector(q, A, S)
            with nc.Block() as block:
                @block.sync
                def _(sp):
                    pj.load(sp, 12, 1)
                    pj.load(sp, 14, 3)

                @block.tensor
                def _(pe):
                    pj.credit_pe(pe)
                    pj.multiply(pe, 1, L, L)
                    pj.multiply(pe, 3, 0, 2 * L)

                @block.scalar
                def _(act):
                    pj.credit_act(act)
                    pj.evacuate(act, 1, gq, 0, L)
                    pj.evacuate(act, 3, gkv, 0, 2 * L)

        gk, gv = gkv[:, 0:NH, :], gkv[:, NH:, :]
        wg = s.sb("wg", [GATE_RANK, 2, NH * P])
        bg = s.sb("bg", [P, 2, NH])
        sm = s.sb("sm", [P, 4, 2 * L])
        pick = s.sb("pick", [P, 2, 2, P], I32)
        z = s.sb("z", [P, NH, 2 * L])
        gc = s.sb("gc", [P, NH, 2 * L])
        gt = s.sb("gt", [P, NH, 2 * L])
        w = s.sb("w", [P, NH, 2 * L])
        qa, ka, qc, kc = (s.sb(n, [P, NH, L]) for n in ("qa", "ka", "qc", "kc"))
        qt = [s.sb(f"qt{d}", [P, NH, L]) for d in d2]
        ktd = [s.sb(f"ktd{d}", [P, NTILE, NH, P]) for d in d2]
        at = [s.sb(f"at{d}", [P, 2, NH, P]) for d in d2]
        egl = s.sb("egl", [P, 2, NH, NTILE])
        vt = s.sb("vt", [P, NTILE, NH * DV2, P])
        st = [[s.sb(f"st{d}{n}", [P, NH, DV2 * P]) for n in range(3)] for d in d2]
        bank = [s.ps(f"bank{b}", [P, 4, P]) for b in range(8)]
        (s_in, s_zp, s_z, s_ab, s_ln, s_l, s_gc, s_d, s_ex, s_m, s_att, s_at, s_ktp, s_kt, s_vtp, s_vt, s_kv, s_st,
         s_o, s_oc, s_zero, s_gl, s_sum) = (s.sem(n) for n in (
             "in", "z_done", "z_biased", "exp_abs", "softplus", "log_gate", "cumsum", "exponent", "exped", "scaled",
             "att_done", "att_picked", "kd_turned", "kd_copied", "v_turned", "v_copied", "kv_done", "state_done",
             "o_done", "o_copied", "cleared", "end_decay", "att_summed"))

        def chunks(ap):
            return ap.rearrange("p h (c n) -> p (h c) n", n=GC)

        def tiles(ap):
            return ap.rearrange("p h (c n) -> p (h c) n", n=P)

        with nc.Block() as block:
            @block.sync
            def _(sp):
                sp.dma_start(wg[:], A.gate_w).then_inc(s_in, 16)
                sp.dma_start(bg[:], A.gate_b).then_inc(s_in, 16)
                sp.dma_start(sm[:], A.scan_masks).then_inc(s_in, 16)
                sp.dma_start(pick[:], A.pick_masks).then_inc(s_in, 16)

            @block.gpsimd
            def _(g):
                for d in d2:
                    m = g.memset(at[d][:], 0.0)
                m.then_inc(s_zero, 1)

            @block.tensor
            def _(pe):
                pe.wait_ge(s_in, 64)

                def gates(d):
                    lr = (S.lf, S.lb)[d]
                    if d:
                        pe.wait_ge(s_at, 4)
                    for h in range(NH):
                        m = pe.matmul(bank[h][:].rearrange("p a n -> p (a n)"), wg[:, d, h * P:(h + 1) * P], lr[:],
                                      start=True, stop=True)
                    m.then_inc(s_zp, 1)

                gates(0)
                for t in range(NTILE):
                    for u in range(2):
                        b = 2 * t + u
                        if b >= 4:
                            pe.wait_ge(s_vt, b - 3)
                        for j in range(4):
                            m = pe.transpose(bank[4 + b % 4][:, j, :], gv[:, 4 * u + j, t * P:(t + 1) * P], C.ident)
                        m.then_inc(s_vtp, 1)
                pe.wait_ge(s_vt, 8)
                for d in d2:
                    if d:
                        gates(1)
                    pe.wait_ge(s_z, NH * (d + 1))
                    pe.wait_ge(s_m, 6 * d + 4)
                    for t in range(2):
                        for c, (kk, qq) in enumerate(((ka, qa), (kc, qc))):
                            for h in range(NH):
                                m = pe.matmul(bank[2 * t + c][:, h, :], kk[:, h, t * P:(t + 1) * P],
                                              qq[:, h, t * P:(t + 1) * P], start=True, stop=True)
                            m.then_inc(s_att, 1)
                    pe.wait_ge(s_m, 6 * d + 6)
                    if d:
                        pe.wait_ge(s_kt, 4)
                    for t in range(NTILE):
                        for h in range(NH):
                            m = pe.transpose(bank[4 + t][:, h, :], w[:, h, t * P:(t + 1) * P], C.ident)
                        m.then_inc(s_ktp, 1)
                for n in range(3):
                    for d in d2:
                        t = n ^ d
                        pe.wait_ge(s_kt, 4 * d + 4)
                        if n == 0:
                            pe.wait_ge(s_at, 8)
                        else:
                            pe.wait_ge(s_st, 2 * (n - 1) + d + 1)
                        for h in range(NH):
                            o = bank[2 * d + h // 2][:].rearrange("p a n -> p (a n)")[:, 256 * (h % 2):256 * (h % 2) + 256]
                            m = pe.matmul(o, ktd[d][:, t, h, :], vt[:, t, 2 * h:2 * h + 2, :].rearrange("p a n -> p (a n)"),
                                          start=True, stop=True)
                        m.then_inc(s_kv, 1)
                pe.wait_ge(s_sum, 1)
                pe.wait_ge(s_kt, 8)
                pe.wait_ge(s_st, 6)
                for t in range(2):
                    sf, sb = st[0][1 + t], st[1][2 - t]
                    for u in range(2):
                        for j in range(4):
                            c = 4 * u + j
                            h, e = c // 2, c % 2
                            o = bank[4 + 2 * t + u][:, j, :]
                            pe.matmul(o, vt[:, 2 + t, c, :], at[0][:, t, h, :], start=True, stop=False)
                            pe.matmul(o, sf[:, h, e * P:(e + 1) * P], qt[0][:, h, t * P:(t + 1) * P],
                                      start=False, stop=False)
                            m = pe.matmul(o, sb[:, h, e * P:(e + 1) * P], qt[1][:, h, t * P:(t + 1) * P],
                                          start=False, stop=True)
                        m.then_inc(s_o, 1)

            @block.scalar
            def _(act):
                for d in d2:
                    act.wait_ge(s_z, NH * (d + 1))
                    act.activation(w[:], z[:], ACT.Abs).then_inc(s_ab, 1)
                    act.wait_ge(s_ab, 2 * d + 1)
                    act.activation(w[:], w[:], ACT.Exp, scale=-1.0).then_inc(s_ab, 1)
                    act.wait_ge(s_ab, 2 * d + 2)
                    act.activation(w[:], w[:], ACT.Ln, bias=1.0).then_inc(s_ln, 1)
                    if d == 0:
                        for b in range(8):
                            t, u = b // 2, b % 2
                            act.wait_ge(s_vtp, b + 1)
                            act.activation(vt[:, t, 4 * u:4 * u + 4, :], bank[4 + b % 4][:], ACT.Copy).then_inc(s_vt, 1)
                    act.wait_ge(s_gc, d + 1)
                    end = P - 1 if d == 0 else 0
                    act.activation(egl[:, d], gt[:].rearrange("p h (t n) -> p h t n", n=P)[:, :, :, end],
                                   ACT.Exp, scale=IG).then_inc(s_gl, 1)
                    for e, (src, cols, sc) in enumerate((
                            (w, slice(L, 2 * L), IG), (w, slice(L, 2 * L), -IG), (gc, slice(L, 2 * L), IG),
                            (w, slice(L, 2 * L), IG), (gt, slice(L, 2 * L), IG), (w, slice(0, 2 * L), IG))):
                        act.wait_ge(s_d, 3 * d + (0, 1, 1, 2, 2, 3)[e] + (1 if e == 0 else 0))
                        if e:
                            act.wait_ge(s_m, 6 * d + e)
                        n = cols.stop - cols.start
                        act.activation(z[:, :, 0:n], src[:, :, cols], ACT.Exp, scale=sc).then_inc(s_ex, 1)
                    for t in range(NTILE):
                        act.wait_ge(s_ktp, 4 * d + t + 1)
                        act.activation(ktd[d][:, t], bank[4 + t][:], ACT.Copy).then_inc(s_kt, 1)
                for b in range(4):
                    t, u = b // 2, b % 2
                    act.wait_ge(s_o, b + 1)
                    act.activation(S.ob[:, 4 * u:4 * u + 4, t * P:(t + 1) * P], bank[4 + b][:], ACT.Copy).then_inc(s_oc, 1)
                act.wait_ge(s_oc, 4)

            @block.vector
            def _(v):
                v.wait_ge(s_in, 64)
                for d in d2:
                    v.wait_ge(s_zp, d + 1)
                    if d:
                        v.wait_ge(s_m, 6)
                    for h in range(NH):
                        v.tensor_scalar(z[:, h, :], bank[h][:].rearrange("p a n -> p (a n)"), bg[:, d, h:h + 1], None,
                                        ALU.add).then_inc(s_z, 1)
                    v.wait_ge(s_ln, d + 1)
                    v.scalar_tensor_tensor(z[:], z[:], 0.0, w[:], ALU.min, ALU.subtract).then_inc(s_l, 1)
                    v.wait_ge(s_l, d + 1)
                    for mk, dst in ((2, gc), (0, gt)):
                        for h in range(NH):
                            o, l, k = dst[:, h, :], z[:, h, :], sm[:, mk + d, :]
                            if d:
                                o, l, k = dst[:, h, ::-1], z[:, h, ::-1], sm[:, mk + d, ::-1]
                            m = v.tensor_tensor_scan(o, k, l, 0.0, ALU.mult, ALU.add)
                    m.then_inc(s_gc, 1)
                    v.wait_ge(s_gc, d + 1)
                    lat = slice(L, 2 * L)
                    mid = GC // 2 if d == 0 else GC - 1 - GC // 2
                    cend, tend = (GC - 1, P - 1) if d == 0 else (0, 0)
                    gcl, wl = gc[:, :, lat], w[:, :, lat]

                    def less(dst, src, at_, n, flip):
                        c = src.rearrange("p h (c n) -> p h c n", n=n)
                        o = dst.rearrange("p h (c n) -> p h c n", n=n)
                        r = c[:, :, :, at_:at_ + 1].to_broadcast(list(c.shape))
                        for h in range(NH):
                            a, b = (r[:, h], c[:, h]) if flip else (c[:, h], r[:, h])
                            m = v.tensor_tensor(o[:, h], a, b, ALU.subtract)
                        m.then_inc(s_d, 1)

                    less(wl, gcl, mid, GC, False)
                    def times(dst, x, n, sc, e):
                        v.wait_ge(s_ex, 6 * d + e + 1)
                        if e == 5 and d:
                            pass
                        v.scalar_tensor_tensor(dst, z[:, :, 0:n], sc, x, ALU.mult, ALU.mult).then_inc(s_m, 1)
                    if d:
                        v.wait_ge(s_att, 4)
                    times(qa[:], gq[:], L, DK, 0)
                    times(ka[:], gk[:, :, lat], L, 1.0, 1)
                    less(wl, gcl, cend, GC, True)
                    times(qc[:], gq[:], L, DK, 2)
                    times(kc[:], gk[:, :, lat], L, 1.0, 3)
                    less(w[:], gt[:], tend, P, True)
                    times(qt[d][:], gq[:], L, DK, 4)
                    times(w[:], gk, 2 * L, 1.0, 5)
                    if d == 0:
                        v.wait_ge(s_zero, 1)
                    for t in range(2):
                        for c in range(2):
                            v.wait_ge(s_att, 4 * d + 2 * t + c + 1)
                            v.copy_predicated(at[d][:, t], wide(pick[:, d, c, :], NH), bank[2 * t + c][:]).then_inc(s_at, 1)
                            v.wait_ge(s_at, 4 * d + 2 * t + c + 1)
                v.wait_ge(s_at, 8)
                v.tensor_tensor(at[0][:], at[0][:], at[1][:], ALU.add).then_inc(s_sum, 1)
                v.wait_ge(s_gl, 2)
                for n in range(3):
                    for d in d2:
                        t = n ^ d
                        v.wait_ge(s_kv, 2 * n + d + 1)
                        for h in range(NH):
                            o = bank[2 * d + h // 2][:].rearrange("p a n -> p (a n)")[:, 256 * (h % 2):256 * (h % 2) + 256]
                            if n == 0:
                                m = v.tensor_copy(st[d][n][:, h, :], o)
                            else:
                                m = v.scalar_tensor_tensor(st[d][n][:, h, :], st[d][n - 1][:, h, :],
                                                           egl[:, d, h, t:t + 1], o, ALU.mult, ALU.add)
                        m.then_inc(s_st, 1)
                        v.wait_ge(s_st, 2 * n + d + 1)


def merge_stage(nc, A, C, S):
    with Scope(nc, "merge_") as s:
        pz = s.sb("pz", [P, 4 * HA, L])
        with Scope(nc, "merge_project_") as q:
            pj = Projector(q, A, S)
            with nc.Block() as block:
                @block.sync
                def _(sp):
                    pj.load(sp, 20, 8)

                @block.tensor
                def _(pe):
                    pj.credit_pe(pe)
                    pj.multiply(pe, 8, L, L)

                @block.scalar
                def _(act):
                    pj.credit_act(act)
                    pj.evacuate(act, 8, pz, 0, L)

        w = [s.sb(f"w{n}", [P, KT, D]) for n in range(2)]
        sq = s.sb("sq", [P, HA, L])
        ra, rb = s.sb("ra", [P, HA, L]), s.sb("rb", [P, HB, L])
        gain = s.sb("gain", [P, 3])
        y = s.sb("y", [P, HA, L])
        junk = s.sb("junk", [P, D])
        ss, rstd = s.sb("ss", [P, 2]), s.sb("rstd", [P, 2])
        bank = [s.ps(f"bank{b}", [P, 2, L]) for b in range(8)]
        (s_in, s_wo, s_x, s_sq, s_ss, s_v, s_rt, s_sil, s_ya, s_pa, s_t, s_y, s_z, s_xs, s_n, s_tr, s_h) = (
            s.sem(n) for n in ("in", "wo_in", "x_in", "squared", "sums", "chain", "rooted", "silu", "gated",
                               "branch", "mixed", "y_done", "out_done", "x_squares", "norm", "turned", "h_done"))
        with nc.Block() as block:
            @block.sync
            def _(sp):
                sp.dma_start(gain[:], A.head_gains).then_inc(s_in, 16)
                sp.dma_start(w[0][:], A.w_out_a.rearrange("(k p) n -> p k n", p=P)).then_inc(s_in, 16)
                sp.dma_start(w[1][:], A.w_out_b.rearrange("(k p) n -> p k n", p=P)).then_inc(s_in, 16)
                sp.dma_start(S.x[:], A.xall[2:4].rearrange("t p d -> p t d")).then_inc(s_x, 16)
                sp.wait_ge(s_pa, 1)
                sp.dma_start(w[0][:], A.w_out.rearrange("(k p) n -> p k n", p=P)).then_inc(s_wo, 16)

            @block.gpsimd
            def _(g):
                g.tensor_tensor(sq[:], S.oa[:], S.oa[:], ALU.mult).then_inc(s_sq, 1)
                g.wait_ge(s_ss, 1)
                g.tensor_tensor(sq[:], S.ob[:], S.ob[:], ALU.mult).then_inc(s_sq, 1)

            @block.scalar
            def _(act):
                act.activation(pz[:, 0:16, :], pz[:, 0:16, :], ACT.Silu)
                act.activation(pz[:, 16:32, :], pz[:, 16:32, :], ACT.Sigmoid).then_inc(s_sil, 1)
                act.wait_ge(s_v, 2)
                act.activation(ra[:], ra[:], ACT.Sqrt).then_inc(s_rt, 1)
                act.wait_ge(s_v, 4)
                act.activation(rb[:], rb[:], ACT.Sqrt).then_inc(s_rt, 1)
                for t in range(2):
                    act.wait_ge(s_z, t + 1)
                    act.activation(junk[:], S.x[:, t, :], ACT.Square, accum_out=ss[:, t:t + 1]).then_inc(s_xs, 1)
                    act.wait_ge(s_xs, t + 1)
                act.wait_ge(s_n, 2)
                act.activation(rstd[:], ss[:], ACT.Sqrt).then_inc(s_n, 1)

            @block.tensor
            def _(pe):
                flat = lambda b: bank[b][:].rearrange("p a n -> p (a n)")
                pe.wait_ge(s_sq, 1)
                for b in range(4):
                    m = pe.matmul(flat(b), C.ones, sq[:, 2 * b:2 * b + 2, :].rearrange("p a n -> p (a n)"),
                                  start=True, stop=True)
                m.then_inc(s_ss, 1)
                pe.wait_ge(s_sq, 2)
                for h in range(HB):
                    for e in range(2):
                        m = pe.matmul(bank[4 + h // 2][:, h % 2, :], C.ones, sq[:, 2 * h + e, :],
                                      start=(e == 0), stop=(e == 1))
                m.then_inc(s_ss, 1)
                pe.wait_ge(s_in, 48)
                for n, src in enumerate((S.oa, S.ob)):
                    pe.wait_ge(s_ya, n + 1)
                    if n == 1:
                        pe.wait_ge(s_v, 3)
                    for o in range(KT):
                        for k in range(KT):
                            m = pe.matmul(bank[4 * n + o // 2][:, o % 2, :], w[n][:, k, o * P:(o + 1) * P],
                                          src[:, k, :], start=(k == 0), stop=(k == KT - 1))
                    m.then_inc(s_pa, 1)
                pe.wait_ge(s_wo, 16)
                pe.wait_ge(s_y, 1)
                for t in range(2):
                    for h in range(2):
                        for k in range(KT):
                            m = pe.matmul(flat(2 * t + h), y[:, k, t * P:(t + 1) * P],
                                          w[0][:, k, 512 * h:512 * h + 512], start=(k == 0), stop=(k == KT - 1))
                        m.then_inc(s_t, 1)
                for t in range(2):
                    pe.wait_ge(s_h, 1 + t)
                    for k in range(KT):
                        b = 4 + 2 * t + k // 4
                        m = pe.transpose(flat(b)[:, (k % 4) * P:(k % 4 + 1) * P], S.xn[:, t, k * P:(k + 1) * P], C.ident)
                    m.then_inc(s_tr, 1)

            @block.vector
            def _(v):
                link = Chain(v, s_v)
                v.wait_ge(s_ss, 1)
                for b in range(4):
                    m = v.tensor_scalar(ra[:, 2 * b:2 * b + 2, :], bank[b][:], 1.0 / P, EPS, ALU.mult, ALU.add)
                link(m)
                link(v.reciprocal(ra[:], ra[:]))
                v.wait_ge(s_ss, 2)
                for b in range(2):
                    m = v.tensor_scalar(rb[:, 2 * b:2 * b + 2, :], bank[4 + b][:], 1.0 / (2 * P), EPS, ALU.mult, ALU.add)
                link(m)
                link(v.reciprocal(rb[:], rb[:]))
                v.wait_ge(s_in, 48)
                v.wait_ge(s_rt, 1)
                v.wait_ge(s_sil, 1)
                link(v.scalar_tensor_tensor(S.oa[:], S.oa[:], gain[:, 0:1], ra[:], ALU.mult, ALU.mult))
                v.tensor_tensor(S.oa[:], S.oa[:], pz[:, 0:HA, :], ALU.mult).then_inc(s_ya, 1)
                v.wait_ge(s_rt, 2)
                for c in range(HA):
                    m = v.scalar_tensor_tensor(S.ob[:, c, :], S.ob[:, c, :], gain[:, 1 + c % 2:2 + c % 2],
                                               rb[:, c // 2, :], ALU.mult, ALU.mult)
                link(m)
                v.tensor_tensor(S.ob[:], S.ob[:], pz[:, HA:2 * HA, :], ALU.mult).then_inc(s_ya, 1)
                v.wait_ge(s_pa, 1)
                for b in range(4):
                    m = v.tensor_tensor(y[:, 2 * b:2 * b + 2, :], bank[b][:], pz[:, 16 + 2 * b:18 + 2 * b, :], ALU.mult)
                link(m)
                v.wait_ge(s_pa, 2)
                for b in range(4):
                    m = v.tensor_tensor(sq[:, 2 * b:2 * b + 2, :], bank[4 + b][:], pz[:, 24 + 2 * b:26 + 2 * b, :], ALU.mult)
                link(m)
                v.tensor_tensor(y[:], y[:], sq[:], ALU.add).then_inc(s_y, 1)
                v.wait_ge(s_x, 16)
                for t in range(2):
                    for h in range(2):
                        c = slice(512 * h, 512 * h + 512)
                        v.wait_ge(s_t, 2 * t + h + 1)
                        link(v.tensor_tensor(S.xn[:, t, c], bank[2 * t + h][:].rearrange("p a n -> p (a n)"),
                                             S.g1[:, c], ALU.mult))
                        m = v.tensor_tensor(S.x[:, t, c], S.x[:, t, c], S.xn[:, t, c], ALU.add)
                    m.then_inc(s_z, 1)
                v.wait_ge(s_xs, 2)
                v.tensor_scalar(ss[:], ss[:], 1.0 / D, EPS, ALU.mult, ALU.add).then_inc(s_n, 1)
                v.wait_ge(s_n, 1)
                v.reciprocal(ss[:], ss[:]).then_inc(s_n, 1)
                v.wait_ge(s_n, 3)
                for t in range(2):
                    v.tensor_scalar(S.xn[:, t, :], S.x[:, t, :], rstd[:, t:t + 1], None, ALU.mult).then_inc(s_h, 1)
                for t in range(2):
                    v.wait_ge(s_tr, t + 1)
                    for k in range(KT):
                        v.tensor_scalar(S.h2T[:, k, t * P:(t + 1) * P],
                                        bank[4 + 2 * t + k // 4][:].rearrange("p a n -> p (a n)")
                                        [:, (k % 4) * P:(k % 4 + 1) * P],
                                        S.a2[:, k:k + 1], S.b2[:, k:k + 1], ALU.mult, ALU.add)


def router_stage(nc, A, C, S):
    with Scope(nc, "router_") as s:
        wr = s.sb("wr", [P, KT, NE])
        br = s.sb("br", [P, NE])
        tri, iota = s.sb("tri", [P, P]), s.sb("iota", [P, NE])
        lg = s.sb("lg", [P, 2, NE])
        top = s.sb("top", [P, 2, 8])
        idx = s.sb("idx", [P, 2, 8], U32)
        idf = s.sb("idf", [P, 2, 8])
        ex, tot, nmax = s.sb("ex", [P, 2, TOPK]), s.sb("tot", [P, 2]), s.sb("nmax", [P, 2])
        one = s.sb("one", [P, 2, NE])
        most = s.sb("most", [P, 1])
        pl = s.ps("pl", [P, 2, NE])
        pp = s.ps("pp", [P, 3, NE])
        s_in, s_l, s_v, s_e, s_p = (s.sem(n) for n in ("in", "logits", "chain", "exped", "placed"))
        with nc.Block() as block:
            @block.sync
            def _(sp):
                sp.dma_start(wr[:], A.w_router.rearrange("(k p) n -> p k n", p=P)).then_inc(s_in, 16)
                sp.dma_start(br[:], A.b_router.to_broadcast([P, NE])).then_inc(s_in, 16)
                sp.dma_start(tri[:], A.before_mask).then_inc(s_in, 16)
                sp.dma_start(iota[:], A.iota[:, 0:NE]).then_inc(s_in, 16)

            @block.tensor
            def _(pe):
                pe.wait_ge(s_in, 64)
                for t in range(2):
                    for k in range(KT):
                        m = pe.matmul(pl[:, t, :], S.h2T[:, k, t * P:(t + 1) * P], wr[:, k, :],
                                      start=(k == 0), stop=(k == KT - 1))
                m.then_inc(s_l, 1)
                pe.wait_ge(s_v, PLACE_AT)
                pe.matmul(pp[:, 0, :], tri[:], S.mask[:, 0, 0:NE], start=True, stop=True)
                pe.matmul(pp[:, 1, :], C.ones, S.mask[:, 0, 0:NE], start=True, stop=False)
                pe.matmul(pp[:, 1, :], tri[:], S.mask[:, 1, 0:NE], start=False, stop=True)
                pe.matmul(pp[:, 2, :], C.ones, S.mask[:, 0, 0:NE], start=True, stop=False)
                pe.matmul(pp[:, 2, :], C.ones, S.mask[:, 1, 0:NE], start=False, stop=True).then_inc(s_p, 1)

            @block.scalar
            def _(act):
                act.wait_ge(s_v, 12)
                for t in range(2):
                    m = act.activation(ex[:, t, :], top[:, t, 0:TOPK], ACT.Exp, bias=nmax[:, t:t + 1],
                                       accum_out=tot[:, t:t + 1])
                m.then_inc(s_e, 1)

            @block.vector
            def _(v):
                link = Chain(v, s_v)
                v.wait_ge(s_in, 64)
                v.wait_ge(s_l, 1)
                link(v.tensor_tensor(lg[:], pl[:], wide(br[:], 2), ALU.add))
                for t in range(2):
                    link(v.max(top[:, t, :], lg[:, t, :]))
                    link(v.max_index(idx[:, t, :], top[:, t, :], lg[:, t, :]))
                link(v.tensor_copy(idf[:], idx[:]))
                link(v.tensor_scalar(nmax[:], top[:, :, 0], -1.0, None, ALU.mult))
                for b in (S.wgt, S.mask, S.pos):
                    link(v.memset(b[:], 0.0))
                link(v.memset(one[:], 0.0))
                link(v.tensor_copy(S.posp[:], S.pos[:]))
                v.wait_ge(s_e, 1)
                link(v.reciprocal(tot[:], tot[:]))
                for t in range(2):
                    link(v.tensor_scalar(ex[:, t, :], ex[:, t, :], tot[:, t:t + 1], None, ALU.mult))
                for r in range(TOPK):
                    for t in range(2):
                        for dst, val in ((S.wgt, ex[:, t, r:r + 1]), (S.mask, 1.0)):
                            link(v.tensor_scalar(one[:, t, :], iota[:], idf[:, t, r:r + 1], val,
                                                 ALU.is_equal, ALU.mult))
                            link(v.tensor_tensor(dst[:, t, 0:NE], dst[:, t, 0:NE], one[:, t, :], ALU.add))
                assert link.n == PLACE_AT
                v.wait_ge(s_p, 1)
                link(v.tensor_copy(S.pos[:, :, 0:NE], pp[:, 0:2, :]))
                link(v.tensor_copy(S.posp[:], S.pos[:]))
                link(v.tensor_reduce(most[:], pp[:, 2, :], AX, ALU.max))
                link(v.tensor_copy(S.count[:], most[:]))


PLACE_AT = 12 + 1 + 2 + TOPK * 2 * 2 * 2


def expert_stage(nc, A, C, S):
    RING = 12
    GU, DN = KT, 4
    PER = 2 * (GU + DN)
    PAIRS = NE // 2
    F = D
    with Scope(nc, "expert_") as s:
        bparts = s.sb("bparts", [3 * NE, 3 * D], BF16)
        pick = s.sb("pick", [3 * NE, NE * SLOTS])
        bsel = s.sb("bsel", [3 * NE, 2 * SLOTS], BF16)
        iota = s.sb("iota", [P, SLOTS])
        sel = s.sb("sel", [P, 2, 2, SLOTS])
        selw = s.sb("selw", [P, 2, 3, SLOTS])
        put = S.put[:].rearrange("p (e h x) n -> p e h (x n)", e=2, h=2)[:, :, :, 0:L]
        xT = S.work[:, 0:KT * P].rearrange("p (k n) -> p k n", k=KT)
        glu, lin, sig, hid, hidT, ysb = (S.work[:, KT * P + 512 * n:KT * P + 512 * (n + 1)] for n in range(6))
        hidT = hidT.rearrange("p (c n) -> p c n", c=4)
        gb, lb = s.ps("gb", [P, 512]), s.ps("lb", [P, 512])
        tb, yb = s.ps("tb", [P, 4, P]), s.ps("yb", [P, 512])
        xb = [s.ps(f"xb{n}", [P, 4, P]) for n in range(2)]
        ob = [s.ps(f"ob{n}", [P, 512]) for n in range(2)]
        landed = s.sems("landed", RING)
        shift = s.sb("shift", [P, L // SLOTS])
        (s_in, s_used, s_sel, s_gx, s_xT, s_selw, s_pt, s_put, s_glu, s_lin, s_sig, s_hid, s_tr, s_trc,
         s_yc, s_sc, s_ac, s_bs, s_c, s_z, s_shift) = (s.sem(n) for n in (
             "in", "unit_used", "picks", "gathered", "x_ready", "weights", "put_turned", "put_ready",
             "glu_done", "lin_done", "sig_done", "hid_done", "hid_turned", "hid_copied", "y_copied",
             "spread", "added", "bias_pick", "chain", "zeroed", "shifted"))

        def up_done(it, j):
            return it * PER + (RING + j * (GU + DN) + GU)

        def down_done(it, j):
            return it * PER + (RING + (j + 1) * (GU + DN))

        with Scope(nc, "expert_bias_") as q:
            bias = q.sb("bias", [NE, 3 * D])
            back = q.sb("back", [NE, 3 * D])
            with nc.Block() as block:
                @block.sync
                def _(sp):
                    sp.dma_start(bias[:, 0:2 * D], A.b_gu).then_inc(s_in, 16)
                    sp.dma_start(bias[:, 2 * D:3 * D], A.b_down).then_inc(s_in, 16)
                    sp.dma_start(pick[:], A.bias_pick).then_inc(s_in, 16)
                    sp.dma_start(iota[:], A.iota[:, 0:SLOTS]).then_inc(s_in, 16)
                    sp.dma_start(shift[:], A.pass_start).then_inc(s_in, 16)

                @block.vector
                def _(v):
                    link = Chain(v, s_c)
                    v.wait_ge(s_in, 80)
                    for n in range(3):
                        part = bparts[n * NE:(n + 1) * NE, :]
                        link(v.tensor_copy(part, bias[:]))
                        if n < 2:
                            link(v.tensor_copy(back[:], part))
                            link(v.tensor_tensor(bias[:], bias[:], back[:], ALU.subtract))

        ring = s.sb("ring", [P, RING, 2 * F])

        def passes(eng, body):
            count = eng.value_load(S.count[0:1, 0:1], min_val=0, max_val=L)
            with eng.Fori(0, L // SLOTS) as p:
                with eng.If(count > p * SLOTS):
                    body(p)

        with nc.Block() as block:
            @block.sync
            def _(sp):
                def body(p):
                    with sp.Fori(0, PAIRS) as i:
                        it = p * PAIRS + i
                        u = 0
                        for j in range(2):
                            for n in range(GU + DN):
                                z = u % RING
                                sp.wait_ge(s_used, it * PER + (u + 1))
                                if n < GU:
                                    src = A.w_gu[bass.ds(i * 2 + j, 1), n * P:(n + 1) * P, :].rearrange("e p n -> (e p) n")
                                    sp.dma_start(ring[:, z, :], src).then_inc(landed[z], 16)
                                else:
                                    m = n - GU
                                    src = A.w_down[bass.ds(i * 2 + j, 1), 2 * m * P:2 * (m + 1) * P, :] \
                                        .rearrange("e (a p) n -> p (e a) n", p=P)
                                    sp.dma_start(ring[:, z, :].rearrange("p (a n) -> p a n", a=2), src) \
                                        .then_inc(landed[z], 16)
                                u += 1
                passes(sp, body)

            @block.gpsimd
            def _(g):
                g.sem_inc(s_used, RING)
                g.sem_inc(s_ac, 2)
                g.memset(put, 0.0).then_inc(s_z, 1)
                g.memset(S.acc, 0.0).then_inc(s_z, 1)

                def body(p):
                    with g.Fori(0, PAIRS) as i:
                        it = p * PAIRS + i
                        for j in range(2):
                            g.wait_ge(s_used, it * PER + (1 if j == 0 else RING))
                            g.tensor_copy(bsel[:, j * SLOTS:(j + 1) * SLOTS],
                                          pick[:, bass.ds(i * (2 * SLOTS) + j * SLOTS, SLOTS)]).then_inc(s_bs, 1)
                passes(g, body)

            @block.vector
            def _(v):
                def picks(e):
                    for t in range(2):
                        for j in range(2):
                            m = v.tensor_scalar(sel[:, t, j, :], iota[:], S.posp[:, t, bass.ds(e + j, 1)],
                                                S.mask[:, t, bass.ds(e + j, 1)], ALU.is_equal, ALU.mult)
                    m.then_inc(s_sel, 1)

                def body(p):
                    v.tensor_scalar(S.posp[:], S.pos[:], shift[:, bass.ds(p, 1)], None, ALU.subtract).then_inc(s_shift, 1)
                    v.wait_ge(s_shift, p + 1)
                    picks(0)
                    with v.Fori(0, PAIRS) as i:
                        it = p * PAIRS + i
                        gth = it + p
                        for t in range(2):
                            for c in range(3):
                                e = i * 2 + (c % 2)
                                m = v.tensor_scalar(selw[:, t, c, :], iota[:], S.posp[:, t, bass.ds(e, 1)],
                                                    S.wgt[:, t, bass.ds(e, 1)], ALU.is_equal, ALU.mult)
                        m.then_inc(s_selw, 1)
                        v.wait_ge(s_gx, gth + 1)
                        picks(i * 2 + 2)
                        for j in range(2):
                            v.wait_ge(s_used, up_done(it, j))
                            v.tensor_scalar(glu, gb[:], LIMIT, None, ALU.min).then_inc(s_glu, 1)
                            v.tensor_scalar(lin, lb[:], LIMIT, -LIMIT, ALU.min, ALU.max).then_inc(s_lin, 1)
                            v.wait_ge(s_glu, it * 2 + (j + 1))
                            v.wait_ge(s_lin, it * 4 + (2 * j + 1))
                            v.scalar_tensor_tensor(lin, lin, 1.0, glu, ALU.add, ALU.mult).then_inc(s_lin, 1)
                            v.wait_ge(s_lin, it * 4 + (2 * j + 2))
                            v.wait_ge(s_sig, it * 2 + (j + 1))
                            v.tensor_tensor(hid, lin, sig, ALU.mult).then_inc(s_hid, 1)
                        for j in range(2):
                            v.wait_ge(s_ac, it * 8 + (4 * j + 2))
                            for q in range(4):
                                v.wait_ge(s_sc, it * 8 + (4 * j + q + 1))
                                a = S.acc[:, q // 2, 512 * (q % 2):512 * (q % 2) + 512]
                                v.tensor_tensor(a, a, ob[q % 2][:], ALU.add).then_inc(s_ac, 1)
                v.wait_ge(s_z, 2)
                passes(v, body)

            @block.scalar
            def _(act):
                act.wait_ge(s_z, 2)

                def take():
                    for k in range(KT):
                        m = act.activation(xT[:, k, :], xb[k // 4][:, k % 4, :], ACT.Identity,
                                           scale=S.a2[:, k:k + 1], bias=S.b2[:, k:k + 1])
                    m.then_inc(s_xT, 1)

                def body(p):
                    act.wait_ge(s_gx, p * (PAIRS + 1) + 1)
                    take()
                    with act.Fori(0, PAIRS) as i:
                        it = p * PAIRS + i
                        gth = it + p
                        act.wait_ge(s_pt, it + 1)
                        for w in range(2):
                            lo, hi = w, 1 - w
                            act.activation(put[0:SLOTS, lo, 0, :].rearrange("p (t n) -> p t n", n=P),
                                           tb[0:SLOTS, 2 * w:2 * w + 2, :], ACT.Copy)
                            m = act.activation(put[SLOTS:P, hi, 1, :].rearrange("p (t n) -> p t n", n=P),
                                               tb[SLOTS:P, 2 * w:2 * w + 2, :], ACT.Copy)
                        m.then_inc(s_put, 1)
                        for j in range(2):
                            act.wait_ge(s_glu, it * 2 + (j + 1))
                            act.activation(sig, glu, ACT.Sigmoid, scale=ALPHA).then_inc(s_sig, 1)
                            if j == 1:
                                act.wait_ge(s_gx, gth + 2)
                                take()
                            act.wait_ge(s_tr, it * 2 + (j + 1))
                            act.activation(hidT, tb[:], ACT.Copy).then_inc(s_trc, 1)
                            act.wait_ge(s_used, down_done(it, j))
                            act.activation(ysb, yb[:], ACT.Copy).then_inc(s_yc, 1)
                passes(act, body)

            @block.tensor
            def _(pe):
                halves = (slice(0, SLOTS), slice(SLOTS, P))

                def spread(it, j):
                    pe.wait_ge(s_yc, it * 2 + (j + 1))
                    for q in range(4):
                        pe.wait_ge(s_ac, it * 8 + (4 * j + q + 1))
                        t, h = q // 2, q % 2
                        pe.matmul(ob[h][:], put[:, j, h, t * P:(t + 1) * P], ysb,
                                  start=True, stop=True).then_inc(s_sc, 1)

                def gather():
                    for k in range(KT):
                        for t in range(2):
                            m = pe.matmul(xb[k // 4][:, k % 4, :], S.xn[:, t, k * P:(k + 1) * P],
                                          sel[:, t].rearrange("p j n -> p (j n)"), start=(t == 0), stop=(t == 1))
                    m.then_inc(s_gx, 1)

                def body(p):
                    pe.wait_ge(s_sel, p * (PAIRS + 1) + 1)
                    gather()
                    with pe.Fori(0, PAIRS) as i:
                        it = p * PAIRS + i
                        gth = it + p
                        pe.wait_ge(s_xT, gth + 1)
                        u = 0
                        for j in range(2):
                            x = slice(j * SLOTS, (j + 1) * SLOTS)
                            pe.wait_ge(s_bs, it * 2 + (j + 1))
                            for b, c0 in ((gb, 0), (lb, F)):
                                for h in range(2):
                                    pe.matmul(b[halves[h], :], bsel[:, x], bparts[:, c0 + 512 * h:c0 + 512 * h + 512],
                                              start=True, stop=False)
                            for k in range(GU):
                                z = u % RING
                                pe.wait_ge(landed[z], it * 32 + 16 * (u // RING + 1))
                                for b, c0 in ((gb, 0), (lb, F)):
                                    for h in range(2):
                                        m = pe.matmul(b[halves[h], :], xT[:, k, x],
                                                      ring[:, z, c0 + 512 * h:c0 + 512 * h + 512],
                                                      start=False, stop=(k == GU - 1))
                                m.then_inc(s_used, 1)
                                u += 1
                            if j == 0:
                                pe.wait_ge(s_selw, it + 1)
                                for w in range(2):
                                    for t in range(2):
                                        m = pe.transpose(tb[:, 2 * w + t, :],
                                                         selw[:, t, w:w + 2, :].rearrange("p j n -> p (j n)"), C.ident)
                                m.then_inc(s_pt, 1)
                                pe.wait_ge(s_sel, gth + 2)
                                gather()
                                pe.wait_ge(s_put, it + 1)
                            else:
                                spread(it, 0)
                            pe.wait_ge(s_hid, it * 2 + (j + 1))
                            for c in range(4):
                                m = pe.transpose(tb[:, c, :], hid[:, c * P:(c + 1) * P], C.ident)
                            m.then_inc(s_tr, 1)
                            for h in range(2):
                                pe.matmul(yb[halves[h], :], bsel[:, x],
                                          bparts[:, 2 * F + 512 * h:2 * F + 512 * h + 512], start=True, stop=False)
                            pe.wait_ge(s_trc, it * 2 + (j + 1))
                            for n in range(DN):
                                z = u % RING
                                pe.wait_ge(landed[z], it * 32 + 16 * (u // RING + 1))
                                for a in range(2):
                                    f = 2 * n + a
                                    c, hh = f % 4, f // 4
                                    for h in range(2):
                                        m = pe.matmul(yb[halves[h], :], hidT[:, c, hh * SLOTS:(hh + 1) * SLOTS],
                                                      ring[:, z, a * F + 512 * h:a * F + 512 * h + 512],
                                                      start=False, stop=(f == 7))
                                m.then_inc(s_used, 1)
                                u += 1
                        spread(it, 1)
                passes(pe, body)


def close_first_stage(nc, A, C, S):
    with Scope(nc, "close_") as s:
        gf = s.sb("gf", [P, D])
        junk = s.sb("junk", [P, D])
        ss, rstd = s.sb("ss", [P, 2]), s.sb("rstd", [P, 2])
        s_in, s_v, s_a = s.sem("in"), s.sem("chain"), s.sem("act")
        with nc.Block() as block:
            @block.sync
            def _(sp):
                sp.dma_start(gf[:], A.final_norm_g.to_broadcast([P, D])).then_inc(s_in, 16)

            @block.scalar
            def _(act):
                for t in range(2):
                    act.wait_ge(s_v, 3 + t)
                    act.activation(junk[:], S.x[:, t, :], ACT.Square, accum_out=ss[:, t:t + 1]).then_inc(s_a, 1)
                    act.wait_ge(s_a, t + 1)
                act.wait_ge(s_v, 6)
                act.activation(rstd[:], ss[:], ACT.Sqrt).then_inc(s_a, 1)

            @block.vector
            def _(v):
                link = Chain(v, s_v)
                for t in range(2):
                    link(v.tensor_tensor(S.acc[:, t, :], S.acc[:, t, :], S.g2, ALU.mult))
                for t in range(2):
                    link(v.tensor_tensor(S.x[:, t, :], S.x[:, t, :], S.acc[:, t, :], ALU.add))
                v.wait_ge(s_a, 2)
                link(v.tensor_scalar(ss[:], ss[:], 1.0 / D, EPS, ALU.mult, ALU.add))
                link(v.reciprocal(ss[:], ss[:]))
                v.wait_ge(s_a, 3)
                v.wait_ge(s_in, 16)
                for t in range(2):
                    v.scalar_tensor_tensor(S.g[:, t, :], S.x[:, t, :], rstd[:, t:t + 1], gf[:], ALU.mult, ALU.mult)


H2 = 8
HD = 64
NOPE, ROPE = 64, 32
QL, KVL = 384, 256
WA = H2 * HD
FF = 2816
FT = FF // P
IN2 = 3 * WA + QL + KVL + ROPE


def attend_stage(nc, A, C, S):
    HQ = NOPE + ROPE
    with Scope(nc, "attend_") as s:
        proj = s.sb("proj", [P, 2, IN2])
        gcol = s.sb("gcol", [P, KT + 3 + 2 + KT])
        s_in, s_w = s.sem("in"), s.sems("w_in", 3)
        stat, rstd, junk = s.sb("stat", [P, 12]), s.sb("rstd", [P, 12]), s.sb("junk", [P, D])
        COLS = [(c, min(512, IN2 - c)) for c in range(0, IN2, 512)]
        with Scope(nc, "attend_in_") as q:
            wi = q.sb("wi", [P, 3, KT, 512])
            xn, hT = q.sb("xn", [P, 2, D]), q.sb("hT", [P, KT, L])
            pt = [q.ps(f"pt{n}", [P, 4, P]) for n in range(4)]
            pj = [q.ps(f"pj{n}", [P, 512]) for n in range(4)]
            s_a, s_v, s_t, s_h, s_p, s_c = (q.sem(n) for n in ("act", "chain", "turned", "hT_done", "projected", "copied"))
            with nc.Block() as block:
                @block.sync
                def _(sp):
                    sp.dma_start(gcol[:], A.gains2_col).then_inc(s_in, 16)
                    for u, (c, n) in enumerate(COLS):
                        if u >= 3:
                            sp.wait_ge(s_p, 2 * (u - 2))
                        sp.dma_start(wi[:, u % 3, :, 0:n], A.w_in_2[:, c:c + n]
                                     .rearrange("(k p) n -> p k n", p=P)).then_inc(s_w[u % 3], 16)

                @block.scalar
                def _(act):
                    for t in range(2):
                        act.activation(junk[:], S.x[:, t, :], ACT.Square, accum_out=stat[:, t:t + 1]).then_inc(s_a, 1)
                        act.wait_ge(s_a, t + 1)
                    act.wait_ge(s_v, 2)
                    act.activation(rstd[:, 0:2], stat[:, 0:2], ACT.Sqrt).then_inc(s_a, 1)
                    for u, (c, n) in enumerate(COLS):
                        for t in range(2):
                            b = 2 * u + t
                            act.wait_ge(s_p, b + 1)
                            act.activation(proj[:, t, c:c + n], pj[b % 4][:, 0:n], ACT.Copy).then_inc(s_c, 1)

                @block.vector
                def _(v):
                    link = Chain(v, s_v)
                    v.wait_ge(s_a, 2)
                    link(v.tensor_scalar(stat[:, 0:2], stat[:, 0:2], 1.0 / D, EPS, ALU.mult, ALU.add))
                    link(v.reciprocal(stat[:, 0:2], stat[:, 0:2]))
                    v.wait_ge(s_a, 3)
                    for t in range(2):
                        link(v.tensor_scalar(xn[:, t, :], S.x[:, t, :], rstd[:, t:t + 1], None, ALU.mult))
                    v.wait_ge(s_in, 16)
                    for b in range(4):
                        t, h = b // 2, b % 2
                        v.wait_ge(s_t, b + 1)
                        for k in range(4):
                            kk = 4 * h + k
                            m = v.tensor_scalar(hT[:, kk, t * P:(t + 1) * P], pt[b][:, k, :], gcol[:, kk:kk + 1], None,
                                                ALU.mult)
                        m.then_inc(s_h, 1)

                @block.tensor
                def _(pe):
                    for b in range(4):
                        t, h = b // 2, b % 2
                        pe.wait_ge(s_v, 3 + t)
                        for k in range(4):
                            m = pe.transpose(pt[b][:, k, :], xn[:, t, (4 * h + k) * P:(4 * h + k + 1) * P], C.ident)
                        m.then_inc(s_t, 1)
                    pe.wait_ge(s_h, 4)
                    for u, (c, n) in enumerate(COLS):
                        pe.wait_ge(s_w[u % 3], 16 * (u // 3 + 1))
                        for t in range(2):
                            b = 2 * u + t
                            if b >= 4:
                                pe.wait_ge(s_c, b - 3)
                            for k in range(KT):
                                m = pe.matmul(pj[b % 4][:, 0:n], hT[:, k, t * P:(t + 1) * P], wi[:, u % 3, k, 0:n],
                                              start=(k == 0), stop=(k == KT - 1))
                            m.then_inc(s_p, 1)

        qz = s.sb("qz", [P, H2, L])
        ka = s.sb("ka", [P, H2 // 2, L])
        qb, kb = s.sb("qb", [HQ, H2, L]), s.sb("kb", [HQ, H2, L])
        vb = s.sb("vb", [P, 2, H2, HD])
        bias = s.sb("bias", [P, H2, 2, L])
        wo = s.sb("wo", [P, KT, D])
        gpost = s.sb("gpost", [P, D])
        s_wo = s.sem("wo_in")
        with Scope(nc, "attend_latent_") as q:
            cn = q.sb("cn", [P, 2, QL + KVL])
            cT = q.sb("cT", [P, 5, L])
            wuq, wukv = q.sb("wuq", [P, 3, H2 * HQ]), q.sb("wukv", [P, 2, 2 * WA])
            rope = q.sb("rope", [P, 2, 2, ROPE // 2])
            qc, kc = q.sb("qc", [P, 2, H2, HQ]), q.sb("kc", [P, 2, H2, HQ])
            t1, t2 = q.sb("t1", [P, H2, ROPE // 2]), q.sb("t2", [P, H2, ROPE // 2])
            r1 = q.sb("r1", [P, 4, ROPE // 2])
            bank = [q.ps(f"bank{n}", [P, 4, P]) for n in range(8)]
            s_in, s_a, s_v, s_t, s_u, s_e, s_d, s_z, s_q, s_te = (q.sem(n) for n in (
                "in", "act", "chain", "turned", "up_done", "copied", "dve", "zeroed", "q_turned", "q_copied"))
            flat = lambda b: bank[b][:].rearrange("p a n -> p (a n)")
            with nc.Block() as block:
                @block.sync
                def _(sp):
                    sp.dma_start(wuq[:], A.w_uq.rearrange("(k p) n -> p k n", p=P)).then_inc(s_in, 16)
                    sp.dma_start(wukv[:], A.w_ukv.rearrange("(k p) n -> p k n", p=P)).then_inc(s_in, 16)
                    sp.dma_start(rope[:], A.rope).then_inc(s_in, 16)
                    sp.dma_start(bias[:], A.key_bias).then_inc(s_wo, 16)
                    sp.dma_start(wo[:], A.w_o.rearrange("(k p) n -> p k n", p=P)).then_inc(s_wo, 16)
                    sp.dma_start(gpost[:], A.norm_mix_post.to_broadcast([P, D])).then_inc(s_wo, 16)

                @block.gpsimd
                def _(g):
                    g.memset(qz[:], 0.0).then_inc(s_z, 1)

                @block.scalar
                def _(act):
                    for t in range(2):
                        act.activation(junk[:, 0:QL], proj[:, t, 3 * WA:3 * WA + QL], ACT.Square,
                                       accum_out=stat[:, 2 + t:3 + t]).then_inc(s_a, 1)
                        act.wait_ge(s_a, 2 * t + 1)
                        act.activation(junk[:, 0:KVL], proj[:, t, 3 * WA + QL:3 * WA + QL + KVL], ACT.Square,
                                       accum_out=stat[:, 4 + t:5 + t]).then_inc(s_a, 1)
                        act.wait_ge(s_a, 2 * t + 2)
                    act.wait_ge(s_v, 3)
                    act.activation(rstd[:, 2:6], stat[:, 2:6], ACT.Sqrt).then_inc(s_a, 1)
                    act.wait_ge(s_z, 1)
                    for t in range(2):
                        act.wait_ge(s_q, 2 * t + 1)
                        for c in range(4):
                            for r in range(2):
                                m = act.activation(qz[r * HD:(r + 1) * HD, 2 * c + r, t * P:(t + 1) * P],
                                                   bank[2 * t][r * HD:(r + 1) * HD, c, :], ACT.Copy)
                        m.then_inc(s_te, 1)
                        act.wait_ge(s_q, 2 * t + 2)
                        act.activation(ka[:, :, t * P:(t + 1) * P], bank[2 * t + 1][:], ACT.Copy).then_inc(s_te, 1)
                    for n in range(8):
                        x, t, g = n // 4, (n // 2) % 2, n % 2
                        act.wait_ge(s_q, 4 + n + 1)
                        act.activation((qb, kb)[x][:, 4 * g:4 * g + 4, t * P:(t + 1) * P], bank[n][0:HQ, :, :],
                                       ACT.Copy).then_inc(s_te, 1)

                @block.vector
                def _(v):
                    link = Chain(v, s_v)
                    v.wait_ge(s_a, 4)
                    link(v.tensor_scalar(stat[:, 2:4], stat[:, 2:4], 1.0 / QL, EPS, ALU.mult, ALU.add))
                    link(v.tensor_scalar(stat[:, 4:6], stat[:, 4:6], 1.0 / KVL, EPS, ALU.mult, ALU.add))
                    link(v.reciprocal(stat[:, 2:6], stat[:, 2:6]))
                    v.wait_ge(s_a, 5)
                    for t in range(2):
                        v.tensor_scalar(cn[:, t, 0:QL], proj[:, t, 3 * WA:3 * WA + QL], rstd[:, 2 + t:3 + t], None, ALU.mult)
                        link(v.tensor_scalar(cn[:, t, QL:], proj[:, t, 3 * WA + QL:3 * WA + QL + KVL],
                                             rstd[:, 4 + t:5 + t], None, ALU.mult))
                    for k in range(5):
                        v.wait_ge(s_t, k + 1)
                        m = v.tensor_scalar(cT[:, k, :], flat(4 + k % 4)[:, 0:L], gcol[:, KT + k:KT + k + 1], None, ALU.mult)
                        link(m)
                    v.wait_ge(s_in, 48)
                    for t in range(2):
                        cos, sin = rope[:, 0, t, :], rope[:, 1, t, :]
                        v.wait_ge(s_u, 2 * t + 1)
                        for g in range(2):
                            src = flat(4 * t + g)[:, 0:4 * HQ].rearrange("p (h n) -> p h n", n=HQ)
                            m = v.tensor_copy(qc[:, t, 4 * g:4 * g + 4, :], src)
                        link(m)
                        v.wait_ge(s_u, 2 * t + 2)
                        for g in range(2):
                            src = flat(4 * t + 2 + g).rearrange("p (h n) -> p h n", n=NOPE + HD)
                            v.tensor_copy(kc[:, t, 4 * g:4 * g + 4, 0:NOPE], src[:, :, 0:NOPE])
                            m = v.tensor_copy(vb[:, t, 4 * g:4 * g + 4, :], src[:, :, NOPE:])
                        link(m)

                        def turn(dst, x1, x2, c, s_, a, b):
                            h = ROPE // 2
                            v.tensor_tensor(a, x2, s_, ALU.mult)
                            link(v.tensor_tensor(b, x1, s_, ALU.mult))
                            v.tensor_tensor(dst[..., 0:h], x1, c, ALU.mult)
                            link(v.tensor_tensor(dst[..., h:], x2, c, ALU.mult))
                            v.tensor_tensor(dst[..., 0:h], dst[..., 0:h], a, ALU.subtract)
                            link(v.tensor_tensor(dst[..., h:], dst[..., h:], b, ALU.add))

                        h = ROPE // 2
                        kr = proj[:, t, IN2 - ROPE:]
                        kd = r1[:, 2:4, :].rearrange("p a n -> p (a n)")
                        turn(kd, kr[:, 0:h], kr[:, h:], cos, sin, r1[:, 0, :], r1[:, 1, :])
                        link(v.tensor_copy(kc[:, t, :, NOPE:], wide(kd, H2)))
                        x1, x2 = qc[:, t, :, NOPE:NOPE + h], qc[:, t, :, NOPE + h:]
                        cw, sw = wide(cos, H2), wide(sin, H2)
                        v.tensor_tensor(t1[:], x2, sw, ALU.mult)
                        link(v.tensor_tensor(t2[:], x1, sw, ALU.mult))
                        v.tensor_tensor(x1, x1, cw, ALU.mult)
                        link(v.tensor_tensor(x2, x2, cw, ALU.mult))
                        v.tensor_tensor(x1, x1, t1[:], ALU.subtract)
                        link(v.tensor_tensor(x2, x2, t2[:], ALU.add))
                        v.sem_inc(s_d, 1)
                    assert link.n == 10 + 2 * 9

                @block.tensor
                def _(pe):
                    for t in range(2):
                        for x in range(2):
                            for c in range(4):
                                m = pe.transpose(bank[2 * t + x][:, c, :],
                                                 proj[:, t, x * WA + c * P:x * WA + (c + 1) * P], C.ident)
                            m.then_inc(s_q, 1)
                    pe.wait_ge(s_v, 5)
                    for k in range(5):
                        if k == 4:
                            pe.wait_ge(s_v, 6)
                        for t in range(2):
                            m = pe.transpose(bank[4 + k % 4][:, t, :], cn[:, t, k * P:(k + 1) * P], C.ident)
                        m.then_inc(s_t, 1)
                    pe.wait_ge(s_v, 10)
                    pe.wait_ge(s_te, 4)
                    pe.wait_ge(s_in, 48)
                    for t in range(2):
                        for g in range(2):
                            for k in range(3):
                                m = pe.matmul(flat(4 * t + g)[:, 0:4 * HQ], cT[:, k, t * P:(t + 1) * P],
                                              wuq[:, k, 4 * HQ * g:4 * HQ * (g + 1)], start=(k == 0), stop=(k == 2))
                        m.then_inc(s_u, 1)
                        for g in range(2):
                            for k in range(2):
                                m = pe.matmul(flat(4 * t + 2 + g), cT[:, 3 + k, t * P:(t + 1) * P],
                                              wukv[:, k, 512 * g:512 * (g + 1)], start=(k == 0), stop=(k == 1))
                        m.then_inc(s_u, 1)
                    pe.wait_ge(s_v, 28)
                    for n in range(8):
                        x, t, g = n // 4, (n // 2) % 2, n % 2
                        for h in range(4):
                            m = pe.transpose(bank[n][0:HQ, h, :], (qc, kc)[x][:, t, 4 * g + h, :], C.ident)
                        m.then_inc(s_q, 1)

        sc = s.sb("sc", [P, 2, 2, L])
        mx = s.sb("mx", [P, 2, 2])
        pr = s.sb("pr", [P, 2, 2, L])
        prT = s.sb("prT", [P, 2, 4, P])
        rs = s.sb("rs", [P, 2, 2, H2])
        y = s.sb("y", [P, 2, 2, WA])
        yT = s.sb("yT", [P, KT, L])
        with Scope(nc, "attend_soft_") as q:
            pS = [q.ps(f"pS{n}", [P, 2, L]) for n in range(2)]
            pT = [q.ps(f"pT{n}", [P, 4, P]) for n in range(2)]
            pO = [q.ps(f"pO{n}", [P, H2, HD]) for n in range(2)]
            pY = [q.ps(f"pY{n}", [P, 512]) for n in range(2)]
            (s_s, s_b, s_m, s_e, s_pt, s_pc, s_o, s_r, s_y, s_a, s_v, s_t, s_tc, s_f, s_x) = (q.sem(n) for n in (
                "scores", "biased", "negmax", "exped", "turned", "turned_copied", "o_done", "recip", "y_done",
                "act", "chain", "y_turned", "y_copied", "out_done", "x_done"))
            STEPS = [(a, t, c) for a in range(2) for t in range(2) for c in range(H2 // 2)]
            with nc.Block() as block:
                @block.tensor
                def _(pe):
                    def scores(n):
                        a, t, c = STEPS[n]
                        if n >= 2:
                            pe.wait_ge(s_e, n - 1)
                        for r in range(2):
                            h = 2 * c + r
                            if a == 0:
                                m = pe.matmul(pS[n % 2][:, r, :], qz[:, h, t * P:(t + 1) * P], ka[:, c, :],
                                              start=True, stop=True)
                            else:
                                m = pe.matmul(pS[n % 2][:, r, :], qb[:, h, t * P:(t + 1) * P], kb[:, h, :],
                                              start=True, stop=True)
                        m.then_inc(s_s, 1)

                    def turn(n):
                        pe.wait_ge(s_e, n + 1)
                        if n >= 2:
                            pe.wait_ge(s_pc, n - 1)
                        for r in range(2):
                            for k in range(2):
                                m = pe.transpose(pT[n % 2][:, 2 * r + k, :], pr[:, n % 2, r, k * P:(k + 1) * P], C.ident)
                        m.then_inc(s_pt, 1)

                    def values(n):
                        a, t, c = STEPS[n]
                        pe.wait_ge(s_pc, n + 1)
                        if c == 0 and n >= 8:
                            pe.wait_ge(s_y, n // 4 - 1)
                        for r in range(2):
                            h = 2 * c + r
                            for k in range(2):
                                val = proj[:, k, 2 * WA + h * HD:2 * WA + (h + 1) * HD] if a == 0 else vb[:, k, h, :]
                                m = pe.matmul(pO[(n // 4) % 2][:, h, :], prT[:, n % 2, 2 * r + k, :], val,
                                              start=(k == 0), stop=(k == 1))
                        m.then_inc(s_o, 1)

                    pe.wait_ge(s_wo, 48)
                    for n in range(len(STEPS) + 2):
                        if n < len(STEPS):
                            scores(n)
                        if 1 <= n <= len(STEPS):
                            turn(n - 1)
                        if n >= 2:
                            values(n - 2)
                    for b in range(4):
                        t, a = b // 2, b % 2
                        bk = pT[b % 2]
                        pe.wait_ge(s_v, 3 + t)
                        if b >= 2:
                            pe.wait_ge(s_tc, b - 1)
                        for k in range(4):
                            m = pe.transpose(bk[:, k, :], y[:, t, a, k * P:(k + 1) * P], C.ident)
                        m.then_inc(s_t, 1)
                    pe.wait_ge(s_tc, 4)
                    for b in range(4):
                        t, h = b // 2, b % 2
                        if b >= 2:
                            pe.wait_ge(s_f, b - 1)
                        for k in range(KT):
                            m = pe.matmul(pY[h][:], yT[:, k, t * P:(t + 1) * P], wo[:, k, 512 * h:512 * h + 512],
                                          start=(k == 0), stop=(k == KT - 1))
                        m.then_inc(s_x, 1)

                def copy_turned(act, n):
                    act.wait_ge(s_pt, n + 1)
                    if n >= 2:
                        act.wait_ge(s_o, n - 1)
                    act.activation(prT[:, n % 2], pT[n % 2][:], ACT.Copy).then_inc(s_pc, 1)

                @block.scalar
                def _(act):
                    for n, (a, t, c) in enumerate(STEPS):
                        act.wait_ge(s_m, n + 1)
                        if n >= 2:
                            act.wait_ge(s_pt, n - 1)
                        scale = 1.0 if a == 0 else HQ ** -0.5
                        src = sc[:, n % 2] if a == 0 else pS[n % 2][:]
                        for r in range(2):
                            m = act.activation(pr[:, n % 2, r, :], src[:, r, :], ACT.Exp, bias=mx[:, n % 2, r:r + 1],
                                               scale=scale, accum_out=rs[:, a, t, 2 * c + r:2 * c + r + 1])
                        m.then_inc(s_e, 1)
                        if n >= 1:
                            copy_turned(act, n - 1)
                    copy_turned(act, len(STEPS) - 1)
                    for t in range(2):
                        for a in range(2):
                            act.wait_ge(s_y, 4)
                            act.activation(junk[:, 0:WA], y[:, t, a, :], ACT.Square,
                                           accum_out=stat[:, 6 + 2 * t + a:7 + 2 * t + a]).then_inc(s_a, 1)
                            act.wait_ge(s_a, 2 * t + a + 1)
                    act.wait_ge(s_v, 2)
                    act.activation(rstd[:, 6:10], stat[:, 6:10], ACT.Sqrt).then_inc(s_a, 1)
                    for t in range(2):
                        for h in range(2):
                            b = 2 * t + h
                            act.wait_ge(s_x, b + 1)
                            act.activation(y[:, t, h, :], pY[h][:], ACT.Copy).then_inc(s_f, 1)
                            act.wait_ge(s_f, b + 1)
                        act.activation(junk[:], y[:, t].rearrange("p a n -> p (a n)"), ACT.Square,
                                       accum_out=stat[:, 10 + t:11 + t]).then_inc(s_a, 1)
                        act.wait_ge(s_a, 6 + t)
                    act.wait_ge(s_v, 6)
                    act.activation(rstd[:, 10:12], stat[:, 10:12], ACT.Sqrt).then_inc(s_a, 1)

                @block.vector
                def _(v):
                    link = Chain(v, s_v)
                    v.wait_ge(s_wo, 48)

                    def take(g):
                        a, t = g // 2, g % 2
                        v.wait_ge(s_o, 4 * g + 4)
                        v.reciprocal(rs[:, a, t, :], rs[:, a, t, :]).then_inc(s_r, 1)
                        v.wait_ge(s_r, g + 1)
                        v.tensor_tensor(y[:, t, a, :].rearrange("p (h n) -> p h n", n=HD), pO[g % 2][:],
                                        deep(rs[:, a, t, :], HD), ALU.mult).then_inc(s_y, 1)

                    nb = 0
                    for n, (a, t, c) in enumerate(STEPS):
                        v.wait_ge(s_s, n + 1)
                        if n >= 2:
                            v.wait_ge(s_e, n - 1)
                        if a == 0:
                            v.scalar_tensor_tensor(sc[:, n % 2], pS[n % 2][:], HD ** -0.5, bias[:, 2 * c:2 * c + 2, t, :],
                                                   ALU.mult, ALU.add).then_inc(s_b, 1)
                            nb += 1
                            v.wait_ge(s_b, nb)
                            src, neg = sc[:, n % 2], -1.0
                        else:
                            src, neg = pS[n % 2][:], -HQ ** -0.5
                        v.tensor_reduce(mx[:, n % 2, :], src, AX, ALU.max).then_inc(s_b, 1)
                        nb += 1
                        v.wait_ge(s_b, nb)
                        v.tensor_scalar(mx[:, n % 2, :], mx[:, n % 2, :], neg, None, ALU.mult).then_inc(s_m, 1)
                        if n % 4 == 3 and n >= 7:
                            take(n // 4 - 1)
                    take(3)
                    v.wait_ge(s_a, 4)
                    link(v.tensor_scalar(stat[:, 6:10], stat[:, 6:10], 1.0 / WA, EPS, ALU.mult, ALU.add))
                    link(v.reciprocal(stat[:, 6:10], stat[:, 6:10]))
                    v.wait_ge(s_a, 5)
                    for t in range(2):
                        for a in range(2):
                            m = v.tensor_scalar(y[:, t, a, :], y[:, t, a, :], rstd[:, 6 + 2 * t + a:7 + 2 * t + a], None,
                                                ALU.mult)
                        link(m)
                    for b in range(4):
                        t, a = b // 2, b % 2
                        v.wait_ge(s_t, b + 1)
                        for k in range(4):
                            kk = 4 * a + k
                            m = v.tensor_scalar(yT[:, kk, t * P:(t + 1) * P], pT[b % 2][:, k, :],
                                                gcol[:, KT + 5 + kk:KT + 6 + kk], None, ALU.mult)
                        m.then_inc(s_tc, 1)
                    v.wait_ge(s_a, 7)
                    link(v.tensor_scalar(stat[:, 10:12], stat[:, 10:12], 1.0 / D, EPS, ALU.mult, ALU.add))
                    link(v.reciprocal(stat[:, 10:12], stat[:, 10:12]))
                    v.wait_ge(s_a, 8)
                    for t in range(2):
                        row = y[:, t].rearrange("p a n -> p (a n)")
                        link(v.scalar_tensor_tensor(row, row, rstd[:, 10 + t:11 + t], gpost[:], ALU.mult, ALU.mult))
                        v.tensor_tensor(S.x[:, t, :], S.x[:, t, :], row, ALU.add)


def feed_forward_stage(nc, A, C, S, out):
    with Scope(nc, "ffn_") as s:
        xn, hT = s.sb("xn", [P, 2, D]), s.sb("hT", [P, KT, L])
        gcol, gpost = s.sb("gcol", [P, KT]), s.sb("gpost", [P, D])
        stat, rstd, junk = s.sb("stat", [P, 4]), s.sb("rstd", [P, 4]), s.sb("junk", [P, D])
        wu = s.sb("wu", [P, 2, KT, 2 * P])
        wd = s.sb("wd", [P, 2, D])
        cw = s.sb("cw", [P, FT, 8])
        cv = s.sb("cv", [P, 2, 2, L])
        ge = s.sb("ge", [P, 2, L])
        ac = s.sb("ac", [P, 2, L])
        y = s.sb("y", [P, 2, D])
        pu = [s.ps(f"pu{n}", [P, 2, L]) for n in range(2)]
        py = [s.ps(f"py{n}", [P, 512]) for n in range(4)]
        pt = [s.ps(f"pt{n}", [P, 4, P]) for n in range(2)]
        zero = s.sb("zero", [P, 512], BF16)
        landed = s.sems("landed", 2)
        free = s.sems("free", 2)
        up, conv, gel, hid = s.sems("up_done", 2), s.sems("conv_done", 2), s.sems("gelu_done", 2), s.sems("hid_done", 2)
        (s_in, s_a, s_v, s_t, s_h, s_k, s_z, s_y, s_c, s_out) = (s.sem(n) for n in (
            "in", "act", "chain", "turned", "hT_done", "taps", "zeroed", "down_done", "y_copied", "out"))
        with nc.Block() as block:
            @block.sync
            def _(sp):
                sp.dma_start(gcol[:], A.norm_ffn_pre_col).then_inc(s_in, 16)
                sp.dma_start(cw[:], A.conv_2_col).then_inc(s_in, 16)
                sp.dma_start(gpost[:], A.norm_ffn_post.to_broadcast([P, D])).then_inc(s_in, 16)
                with sp.Fori(0, FT // 2) as i:
                    for z in range(2):
                        sp.wait_ge(free[z], i + 1)
                        sp.dma_start(wu[:, z], A.w_up_units[bass.ds(i * 2 + z, 1)]
                                     .rearrange("u p k n -> p (u k) n")).then_inc(landed[z], 16)
                        sp.dma_start(wd[:, z, :], A.w_down_2[bass.ds(i * (2 * P) + z * P, P), :]).then_inc(landed[z], 16)
                for t in range(2):
                    sp.wait_ge(s_v, 8 + 2 * t)
                    sp.dma_start(out[0, t * P:(t + 1) * P, :], y[:, t, :]).then_inc(s_out, 16)
                sp.wait_ge(s_out, 32)

            @block.gpsimd
            def _(g):
                for z in range(2):
                    g.sem_inc(free[z], 1)
                g.memset(zero[:], 0.0).then_inc(s_z, 1)

            @block.scalar
            def _(act):
                for t in range(2):
                    act.activation(junk[:], S.x[:, t, :], ACT.Square, accum_out=stat[:, t:t + 1]).then_inc(s_a, 1)
                    act.wait_ge(s_a, t + 1)
                act.wait_ge(s_v, 2)
                act.activation(rstd[:, 0:2], stat[:, 0:2], ACT.Sqrt).then_inc(s_a, 1)
                with act.Fori(0, FT // 2) as i:
                    for z in range(2):
                        act.wait_ge(conv[z], i + 1)
                        act.activation(ge[:, z, :], cv[:, z, 0, :], ACT.Gelu_apprx_tanh).then_inc(gel[z], 1)
                for b in range(4):
                    act.wait_ge(s_y, 1)
                    act.activation(y[:, b // 2, 512 * (b % 2):512 * (b % 2) + 512], py[b][:], ACT.Copy).then_inc(s_c, 1)
                    act.wait_ge(s_c, b + 1)
                    if b % 2:
                        t = b // 2
                        act.activation(junk[:], y[:, t, :], ACT.Square, accum_out=stat[:, 2 + t:3 + t]).then_inc(s_a, 1)
                        act.wait_ge(s_a, 4 + t)
                act.wait_ge(s_v, 6)
                act.activation(rstd[:, 2:4], stat[:, 2:4], ACT.Sqrt).then_inc(s_a, 1)

            @block.tensor
            def _(pe):
                for b in range(4):
                    t, h = b // 2, b % 2
                    pe.wait_ge(s_v, 3 + t)
                    if b >= 2:
                        pe.wait_ge(s_h, b - 1)
                    for k in range(4):
                        m = pe.transpose(pt[b % 2][:, k, :], xn[:, t, (4 * h + k) * P:(4 * h + k + 1) * P], C.ident)
                    m.then_inc(s_t, 1)
                pe.wait_ge(s_z, 1)
                for b in range(4):
                    pe.matmul(py[b][:], zero[:, 0:P], zero[:], start=True, stop=False)
                pe.wait_ge(s_h, 4)
                with pe.Fori(0, FT // 2) as i:
                    for z in range(2):
                        pe.wait_ge(landed[z], i * 32 + 32)
                        for g in range(2):
                            for k in range(KT):
                                m = pe.matmul(pu[z][:, g, :], wu[:, z, k, g * P:(g + 1) * P], hT[:, k, :],
                                              start=(k == 0), stop=(k == KT - 1))
                        m.then_inc(up[z], 1)
                    for z in range(2):
                        pe.wait_ge(hid[z], i + 1)
                        for b in range(4):
                            t, h = b // 2, b % 2
                            m = pe.matmul(py[b][:], ac[:, z, t * P:(t + 1) * P], wd[:, z, 512 * h:512 * h + 512],
                                          start=False, stop=False, skip_group_check=True)
                        m.then_inc(free[z], 1)
                for b in range(4):
                    m = pe.matmul(py[b][:], zero[:, 0:P], zero[:], start=False, stop=True)
                m.then_inc(s_y, 1)

            @block.vector
            def _(v):
                link = Chain(v, s_v)
                v.wait_ge(s_a, 2)
                link(v.tensor_scalar(stat[:, 0:2], stat[:, 0:2], 1.0 / D, EPS, ALU.mult, ALU.add))
                link(v.reciprocal(stat[:, 0:2], stat[:, 0:2]))
                v.wait_ge(s_a, 3)
                for t in range(2):
                    link(v.tensor_scalar(xn[:, t, :], S.x[:, t, :], rstd[:, t:t + 1], None, ALU.mult))
                v.wait_ge(s_in, 48)
                for b in range(4):
                    t, h = b // 2, b % 2
                    v.wait_ge(s_t, b + 1)
                    for k in range(4):
                        kk = 4 * h + k
                        m = v.tensor_scalar(hT[:, kk, t * P:(t + 1) * P], pt[b % 2][:, k, :], gcol[:, kk:kk + 1], None,
                                            ALU.mult)
                    m.then_inc(s_h, 1)
                with v.Fori(0, FT // 2) as i:
                    for z in range(2):
                        v.wait_ge(up[z], i + 1)
                        w = lambda j: cw[:, bass.ds(i * 2 + z, 1), j:j + 1].rearrange("p o n -> p (o n)")
                        base = i * 12 + 6 * z
                        for g in range(2):
                            v.tensor_scalar(cv[:, z, g, :], pu[z][:, g, :], w(4 * g + 1), w(4 * g + 3),
                                            ALU.mult, ALU.add).then_inc(s_k, 1)
                        for g in range(2):
                            v.wait_ge(s_k, base + (1 + g))
                            v.scalar_tensor_tensor(cv[:, z, g, 1:], pu[z][:, g, :L - 1], w(4 * g), cv[:, z, g, 1:],
                                                   ALU.mult, ALU.add).then_inc(s_k, 1)
                        for g in range(2):
                            v.wait_ge(s_k, base + (3 + g))
                            m = v.scalar_tensor_tensor(cv[:, z, g, :L - 1], pu[z][:, g, 1:], w(4 * g + 2),
                                                       cv[:, z, g, :L - 1], ALU.mult, ALU.add).then_inc(s_k, 1)
                        v.wait_ge(s_k, base + 6)
                        v.sem_inc(conv[z], 1)
                        v.wait_ge(gel[z], i + 1)
                        v.tensor_tensor(ac[:, z, :], ge[:, z, :], cv[:, z, 1, :], ALU.mult).then_inc(hid[z], 1)
                v.wait_ge(s_a, 5)
                link(v.tensor_scalar(stat[:, 2:4], stat[:, 2:4], 1.0 / D, EPS, ALU.mult, ALU.add))
                link(v.reciprocal(stat[:, 2:4], stat[:, 2:4]))
                v.wait_ge(s_a, 6)
                for t in range(2):
                    link(v.scalar_tensor_tensor(y[:, t, :], y[:, t, :], rstd[:, 2 + t:3 + t], gpost[:], ALU.mult, ALU.mult))
                    link(v.tensor_tensor(y[:, t, :], S.x[:, t, :], y[:, t, :], ALU.add))


class Bag:
    pass


def build(nc, A, out):
    with Scope(nc) as s:
        C, S = Bag(), Bag()
        C.const = s.sb("const", [P, 2, P])
        C.ident, C.ones = C.const[:, 0, :], C.const[:, 1, :]
        S.a2, S.b2 = s.sb("a2", [P, KT]), s.sb("b2", [P, KT])
        S.g = s.sb("gates", [P, 2, D])
        S.g1, S.g2 = S.g[:, 0, :], S.g[:, 1, :]
        with Scope(nc) as mix:
            S.hT = mix.sb("hT", [P, KT, 2 * L])
            modulate_stage(nc, A, C, S)
            S.lf, S.lb = mix.sb("lf", [GATE_RANK, 2 * L]), mix.sb("lb", [GATE_RANK, 2 * L])
            S.oa = mix.sb("oa", [P, HA, L])
            with Scope(nc) as da:
                S.tokq = da.sb("tokq", [P, 2, NTILE, P])
                S.pq, S.pkv = da.sb("pq", [P, HA, L]), da.sb("pkv", [P, 2 * HA, 2 * L])
                with Scope(nc) as ga:
                    S.bf, S.bb, S.af, S.ab = (ga.sb(n, [HA, 2 * L]) for n in ("bf", "bb", "af", "ab"))
                    delta_project_stage(nc, A, C, S)
                    delta_gate_stage(nc, A, C, S)
                delta_scan_stage(nc, A, C, S)
            S.ob = mix.sb("ob", [P, HB * 2, L])
            linear_attention_stage(nc, A, C, S)
            S.x, S.xn, S.h2T = (mix.sb(n, [P, 2, D]) for n in ("x", "xn", "h2T"))
            S.h2T = S.h2T[:].rearrange("p a (b n) -> p (a b) n", n=L)
            merge_stage(nc, A, C, S)
            S.wgt, S.mask, S.pos, S.posp = (mix.sb(n, [P, 2, NE + 2]) for n in ("wgt", "mask", "pos", "posp"))
            S.count = mix.sb("count", [P, 1], I32)
            router_stage(nc, A, C, S)
            S.acc = S.oa[:].rearrange("p (a b) n -> p a (b n)", a=2)
            S.put, S.work = S.ob, S.hT[:].rearrange("p k n -> p (k n)")
            expert_stage(nc, A, C, S)
            close_first_stage(nc, A, C, S)
        S.x = S.g
        attend_stage(nc, A, C, S)
        feed_forward_stage(nc, A, C, S, out)


def layouts(x):
    f = lambda a: np.ascontiguousarray(a)
    col = lambda a, n: f(np.asarray(a).reshape(n, P).T)
    w_in = x["w_in"][0]
    W = 4 * D
    cuts = np.cumsum([0, D, D, D, D, 16, 16, 512, 512, D, D, 32, 2 * D])
    part = lambda i: w_in[:, cuts[i]:cuts[i + 1]]
    cols = np.concatenate([part(0), part(1), part(2), part(6), part(7), part(8), part(3), part(9), part(11)], axis=1)
    a = {
        "xall": f(np.concatenate([x["ctx"][0], x["x"][0]], axis=0).reshape(NTILE, P, D)),
        "ccol": f(np.stack([x["c"][0], x["c_ctx"]]).reshape(2, KT, P).transpose(2, 1, 0)),
        "w_mod": f(x["w_mod"][0]),
        "b_mod": f(x["b_mod"]),
        "b_mod_col": col(x["b_mod"], NMOD * KT),
        "norm_mix_col": col(x["norm_mix_g"], KT),
        "norm_ffn_col": col(x["norm_ffn_g"], KT),
        "w_in_units": f(cols.reshape(KT, P, -1, UNIT).transpose(2, 1, 0, 3)),
        "w_small": f(np.concatenate([part(4), part(5), part(10)], axis=1).reshape(KT, P, 64).transpose(1, 0, 2)),
        "conv_w_col": f(x["conv_w"][0].reshape(9, 24, P).transpose(2, 1, 0)),
        "w_out_a": f(x["w_out_a"][0]), "w_out_b": f(x["w_out_b"][0]), "w_out": f(x["w_out"][0]),
        "head_gains": f(np.concatenate([col(x["gdn_norm_g"], 1), col(x["gla_norm_g"], 2)], axis=1)),
        "w_router": f(x["w_router"][0]), "b_router": f(x["b_router"]),
        "w_gu": f(x["w_gu"][0]), "b_gu": f(x["b_gu"][0]), "w_down": f(x["w_down"][0]), "b_down": f(x["b_down"][0]),
        "final_norm_g": f(x["final_norm_g"][None]),
        "w_in_2": f(x["w_in_2"][0]), "w_uq": f(x["w_uq_2"][0]), "w_ukv": f(x["w_ukv_2"][0]), "w_o": f(x["w_o_2"][0]),
        "gains2_col": f(np.concatenate([col(x["norm_mix_pre_2"], KT), col(x["q_lat_norm_2"], 3), col(x["kv_lat_norm_2"], 2),
                                        col(x["out_norm_a_2"], 4), col(x["out_norm_b_2"], 4)], axis=1)),
        "norm_mix_post": f(x["norm_mix_post_2"]), "norm_ffn_post": f(x["norm_ffn_post_2"]),
        "norm_ffn_pre_col": col(x["norm_ffn_pre_2"], KT),
        "w_up_units": f(x["w_up_2"][0].reshape(KT, P, 2, FT, P).transpose(3, 1, 0, 2, 4).reshape(FT, P, KT, 2 * P)),
        "w_down_2": f(x["w_down_2"][0]),
        "conv_2_col": f(np.concatenate([x["conv_w_2"][0], x["conv_b_2"]]).reshape(4, 2, FT, P)
                        .transpose(3, 2, 1, 0).reshape(P, FT, 8)),
        "gate_w": f(np.stack([x["gla_gate_w_f"][0], x["gla_gate_w_b"][0]], axis=1)),
        "gate_b": f(np.stack([x["gla_gate_b_f"][0], x["gla_gate_b_b"][0]]).reshape(2, HB, P).transpose(2, 0, 1)),
        "a_log": f(np.stack([x["a_log_f"][0], x["a_log_b"][0]], axis=1)),
        "dt_bias": f(np.stack([x["dt_bias_f"][0], x["dt_bias_b"][0]], axis=1)),
    }
    return a


def tables():
    i = np.arange(P)
    f = lambda a: np.ascontiguousarray(a, dtype=np.float32)
    lev = np.zeros((P, 2, LEVELS, P))
    for l in range(LEVELS):
        b = 1 << l
        same = (i[:, None] // (2 * b)) == (i[None, :] // (2 * b))
        fw = same & ((i[:, None] // b) % 2 == 0) & ((i[None, :] // b) % 2 == 1)
        lev[:, 0, l], lev[:, 1, l] = fw, fw.T
    tri = np.zeros((P, 2, 2, P))
    for d in range(2):
        after = (i[None, :] > i[:, None]) if d == 0 else (i[None, :] < i[:, None])
        tri[:, d, 0] = np.where(after, 0, NEG)
        tri[:, d, 1] = np.where(after | (i[None, :] == i[:, None]), 0, NEG)
    same = (i[:, None] // GC) == (i[None, :] // GC)
    pick = np.zeros((P, 2, 2, P), np.int32)
    for d in range(2):
        upto = (i[None, :] >= i[:, None]) if d == 0 else (i[None, :] <= i[:, None])
        pick[:, d, 0], pick[:, d, 1] = upto & same, upto & ~same
    t = np.arange(2 * L)
    scan = np.stack([t % P != 0, t % P != P - 1, t % GC != 0, t % GC != GC - 1])
    sel = np.zeros((P, 2))
    sel[0::32, 0] = 1
    sel[1::32, 1] = 1
    q, k = np.arange(L)[:, None], np.arange(L)[None, :]
    count = (abs(q - k) <= 64).astype(np.float64) + ((q - k) % 4 == 0) + ((q - k) % 16 == 0)
    logc = np.where(count > 0, np.log(np.maximum(count, 1)), NEG)
    key_bias = np.stack([logc - 2.0 ** -(h + 1) * abs(q - k) for h in range(H2)])
    ang = np.arange(L, dtype=np.float32)[:, None] * np.exp(
        -np.log(np.float32(10000.0)) * np.arange(0, ROPE, 2, dtype=np.float32) / ROPE)[None, :]
    rope = np.stack([np.cos(ang), np.sin(ang)]).reshape(2, 2, P, ROPE // 2).transpose(2, 0, 1, 3)
    pb = np.zeros((3 * NE, NE, SLOTS), np.float32)
    for e in range(NE):
        pb[e::NE, e] = 1
    return {
        "key_bias": f(key_bias.reshape(H2, 2, P, L).transpose(2, 0, 1, 3)), "rope": f(rope),
        "bias_pick": pb.reshape(3 * NE, NE * SLOTS),
        "iota": f(np.broadcast_to(i, (P, P))), "before_mask": f(i[:, None] < i[None, :]),
        "pass_start": f(np.broadcast_to(np.arange(L // SLOTS) * SLOTS, (P, L // SLOTS))),
        "consts": f(np.stack([np.eye(P), np.ones((P, P))], axis=1)),
        "pick_masks": pick, "level_masks": f(lev), "tri_masks": f(tri), "sel": f(sel),
        "scan_masks": f(np.broadcast_to(scan[None], (P, 4, 2 * L))),
    }


def kernel(**inputs):
    import concourse.bacc as _bacc
    from concourse.bass_utils import run_bass_kernel_spmd as _run

    nc = _bacc.Bacc("TRN2", target_bir_lowering=False, num_devices=1)
    arrays = {**layouts(inputs), **tables()}
    A = Bag()
    for name, a in arrays.items():
        A.__dict__[name] = nc.dram_tensor("in_" + name, a.shape, mybir.dt.from_np(a.dtype), kind="ExternalInput").ap()
    A.row_scratch = nc.dram_tensor("row_scratch", (2, NTILE, 2, HA, P), F32).ap()
    out = nc.dram_tensor("out", (1, L, D), F32, kind="ExternalOutput").ap()
    build(nc, A, out)
    r = _run(nc, [{"in_" + n: a for n, a in arrays.items()}], core_ids=[0])
    return r.results[0]["out"]
```

```python
from contextlib import ExitStack

import numpy as np

import concourse.bass as bass
from concourse import mybir

P = 128
D = 1024
KT = D // P
L = 256
NTILE = 2 * L // P
EPS = 1e-6
NMOD = 6
HA = 8
HB = 4
GRID_W = 64
GC = 64
GATE_RANK = 16
GATE_NORM = 16.0
NE = 32
TOPK = 4
EXPERT_RING = 12
SLOTS = 64
LIMIT = 7.0
ALPHA = 1.702
UNIT = 256
FILL = 24
EARLY = 12
HALF = 4
LEVELS = 7
NEG = -1e30
G_ZERO = -104.0

F32 = mybir.dt.float32
BF16 = mybir.dt.bfloat16
U32 = mybir.dt.uint32
I32 = mybir.dt.int32
ALU = mybir.AluOpType
ACT = mybir.ActivationFunctionType
AX = mybir.AxisListType.X


class Chain:

    def __init__(self, eng, sem, base=0):
        self.eng, self.sem, self.n = eng, sem, base

    def __call__(self, ins, n=1):
        ins.then_inc(self.sem, n)
        self.n += n
        self.eng.wait_ge(self.sem, self.n)
        return ins


class Scope:

    def __init__(self, nc, stage=""):
        self.nc, self.ctx, self.stage, self.used = nc, ExitStack(), stage, []

    def __enter__(self):
        self.ctx.__enter__()
        return self

    def __exit__(self, *a):
        if self.used and a[0] is None:
            self.nc.clear_and_free_semaphores(self.used)
            self.nc.all_engine_barrier()
        return self.ctx.__exit__(*a)

    def sb(self, name, shape, dt=F32):
        return self.ctx.enter_context(self.nc.sbuf_tensor(self.stage + name, shape, dt))

    def ps(self, name, shape, dt=F32):
        return self.ctx.enter_context(self.nc.psum_tensor(self.stage + name, shape, dt))

    def sem(self, name):
        self.used.append(self.nc.alloc_semaphore(name=self.stage + name))
        return self.used[-1]

    def sems(self, name, n):
        return [self.sem(f"{name}{i}") for i in range(n)]


def wide(ap, n):
    return ap.rearrange("p (o x) -> p o x", o=1).to_broadcast([ap.shape[0], n, ap.shape[1]])


def deep(ap, n):
    return ap.rearrange("p (x o) -> p x o", o=1).to_broadcast([ap.shape[0], ap.shape[1], n])


def modulate_stage(nc, A, C, S):
    NU = NMOD * D // 512
    RING = 3
    SMALL = 5
    with Scope(nc, "modulate_") as s:
        wm = s.sb("wm", [P, RING, KT, 512])
        ccol = s.sb("ccol", [P, KT, 2])
        ccolp = s.sb("ccolp", [P, KT, 32])
        modrow = s.sb("modrow", [P, NMOD * D])
        xc = s.sb("xc", [P, NTILE, D])
        xn = s.sb("xn", [P, 2, D])
        bcol = s.sb("bcol", [P, NMOD * KT])
        gmix = s.sb("gmix", [P, KT])
        gffn = s.sb("gffn", [P, KT])
        g1b = s.sb("g1b", [P, D])
        g2b = s.sb("g2b", [P, D])
        sel = s.sb("sel", [P, 2])
        selb = s.sb("selb", [P, P])
        junk = s.sb("junk", [P, D])
        ss = s.sb("ss", [P, NTILE])
        rstd = s.sb("rstd", [P, NTILE])
        a1 = s.sb("a1", [P, 2, KT])
        b1 = s.sb("b1", [P, 2, KT])
        mcol = s.sb("mcol", [P, NMOD * KT, 2])
        pm = s.ps("pm", [P, 2, 512])
        pt = s.ps("pt", [P, 4, 512])
        pc = s.ps("pc", [P, 512])

        s_small, s_w, s_x, s_c = s.sem("small_in"), s.sems("w_mod_in", RING), s.sem("x_in"), s.sem("condition_ready")
        s_pe, s_row, s_col = s.sem("unit_done"), s.sem("row_copied"), s.sem("columns_done")
        s_tr, s_ht, s_ss, s_rs = s.sem("turned"), s.sem("hT_done"), s.sem("squares_summed"), s.sem("rooted")
        s_rv, s_xn, s_g, s_z, s_d = s.sem("mean_squares"), s.sem("normed"), s.sem("gates_done"), s.sem("cleared"), s.sem("chain")
        s_cc, s_gb = s.sem("cond_in"), s.sem("gate_bias_in")
        xs = [xc[:, t, :] for t in range(NTILE)]
        COLS = [m * KT + k for m in (0, 1, 3, 4) for k in range(KT)]

        with nc.Block() as block:
            @block.sync
            def _(sp):
                sp.dma_start(ccol[:], A.ccol).then_inc(s_cc, 16)
                for u in range(NU):
                    if u >= RING:
                        sp.wait_ge(s_pe, u - RING + 1)
                    sp.dma_start(wm[:, u % RING], A.w_mod[:, u * 512:(u + 1) * 512]
                                 .rearrange("(k p) n -> p k n", p=P)).then_inc(s_w[u % RING], 16)
                    if u == 0:
                        for dst, src in ((C.const, A.consts), (bcol, A.b_mod_col), (gmix, A.norm_mix_col),
                                         (gffn, A.norm_ffn_col), (sel, A.sel)):
                            sp.dma_start(dst[:], src).then_inc(s_small, 16)
                    if u == 1:
                        sp.dma_start(xc[:], A.xall.rearrange("t p d -> p t d")).then_inc(s_x, 16)
                    if u == 5:
                        sp.dma_start(g1b[:], A.b_mod[:, 2 * D:3 * D].to_broadcast([P, D])).then_inc(s_gb, 16)
                        sp.dma_start(g2b[:], A.b_mod[:, 5 * D:6 * D].to_broadcast([P, D])).then_inc(s_gb, 16)

            @block.scalar
            def _(act):
                act.wait_ge(s_cc, 16)
                act.wait_ge(s_z, 1)
                act.activation(ccolp[:, :, 0:2], ccol[:], ACT.Silu).then_inc(s_c, 1)
                for u in range(NU):
                    if u == 2:
                        act.wait_ge(s_x, 16)
                        for t in range(NTILE):
                            act.activation(junk[:], xs[t], ACT.Square, accum_out=ss[:, t:t + 1]).then_inc(s_ss, 1)
                            act.wait_ge(s_ss, t + 1)
                        act.wait_ge(s_rv, 2)
                        act.activation(rstd[:], ss[:], ACT.Sqrt).then_inc(s_rs, 1)
                    act.wait_ge(s_pe, u + 1)
                    act.activation(modrow[:, u * 512:(u + 1) * 512], pm[:, u % 2, :], ACT.Copy).then_inc(s_row, 1)

            @block.tensor
            def _(pe):
                def columns(half):
                    for n in range(16 * half, 16 * half + 16):
                        j = COLS[n]
                        m = pe.matmul(pc[:, 2 * n:2 * n + 2], modrow[:, j * P:(j + 1) * P], sel[:], start=True, stop=True)
                    m.then_inc(s_col, 1)

                pe.wait_ge(s_c, 1)
                for u in range(NU):
                    pe.wait_ge(s_w[u % RING], 16 * (u // RING + 1))
                    if u >= 2:
                        pe.wait_ge(s_row, u - 1)
                    for r in range(2):
                        for q in range(4):
                            k = 4 * r + q
                            m = pe.matmul(pm[32 * q:32 * q + 32, u % 2, :], ccolp[:, k, :], wm[:, u % RING, k, :],
                                          start=(r == 0), stop=(r == 1))
                    m.then_inc(s_pe, 1)
                    if u == 4:
                        pe.wait_ge(s_row, 4)
                        pe.wait_ge(s_small, 16 * SMALL)
                        columns(0)
                    if 5 <= u < 5 + NTILE:
                        t = u - 5
                        pe.wait_ge(s_xn, t + 1)
                        for h in range(2):
                            if t >= 2:
                                pe.wait_ge(s_ht, (t - 2) * 2 + h + 1)
                            for k in range(4):
                                m = pe.transpose(pt[:, 2 * (t % 2) + h, k * P:(k + 1) * P],
                                                 xn[:, t % 2, (4 * h + k) * P:(4 * h + k + 1) * P], C.ident)
                            m.then_inc(s_tr, 1)
                pe.wait_ge(s_row, NU)
                pe.wait_ge(s_ht, 2 * NTILE)
                columns(1)
                pe.wait_ge(s_z, 2)
                for n, base in enumerate((2 * D, 5 * D)):
                    for h in range(2):
                        m = pe.matmul(pt[:, 2 * n + h, :], selb[:], modrow[:, base + 512 * h:base + 512 * h + 512],
                                      start=True, stop=True)
                m.then_inc(s_g, 1)

            @block.vector
            def _(v):
                link = Chain(v, s_d)
                v.memset(ccolp[:], 0.0).then_inc(s_z, 1)
                v.memset(C.eps[:], EPS)
                v.wait_ge(s_small, 16 * SMALL)
                v.wait_ge(s_z, 1)
                v.tensor_copy(selb[:], sel[:, 0:1].to_broadcast([P, P])).then_inc(s_z, 1)
                v.wait_ge(s_ss, NTILE)
                v.tensor_scalar(ss[:], ss[:], 1.0 / D, EPS, ALU.mult, ALU.add).then_inc(s_rv, 1)
                v.wait_ge(s_rv, 1)
                v.reciprocal(ss[:], ss[:]).then_inc(s_rv, 1)
                v.wait_ge(s_rs, 1)
                for t in range(2):
                    v.tensor_scalar(xn[:, t, :], xs[t], rstd[:, t:t + 1], None, ALU.mult).then_inc(s_xn, 1)
                v.wait_ge(s_col, 1)
                def take(half):
                    for n, m in ((2 * half, 3 * half), (2 * half + 1, 3 * half + 1)):
                        link(v.tensor_tensor(mcol[:, m * KT:(m + 1) * KT, :],
                                             pc[:, 16 * n:16 * n + 16].rearrange("p (k t) -> p k t", t=2),
                                             deep(bcol[:, m * KT:(m + 1) * KT], 2), ALU.add))

                take(0)
                for q in range(2):
                    link(v.scalar_tensor_tensor(a1[:, q, :], mcol[:, KT:2 * KT, q], 1.0, gmix[:], ALU.add, ALU.mult))
                    link(v.tensor_copy(b1[:, q, :], mcol[:, 0:KT, q]))
                for t in range(NTILE):
                    q = 1 if t < 2 else 0
                    for h in range(2):
                        v.wait_ge(s_tr, 2 * t + h + 1)
                        for k in range(4):
                            kk = 4 * h + k
                            m = v.tensor_scalar(S.hT[:, kk, t * P:(t + 1) * P], pt[:, 2 * (t % 2) + h, k * P:(k + 1) * P],
                                                a1[:, q, kk:kk + 1], b1[:, q, kk:kk + 1], ALU.mult, ALU.add)
                        m.then_inc(s_ht, 1)
                    if t < 2:
                        v.tensor_scalar(xn[:, t, :], xs[t + 2], rstd[:, t + 2:t + 3], None, ALU.mult).then_inc(s_xn, 1)
                v.wait_ge(s_col, 2)
                take(1)
                link(v.scalar_tensor_tensor(S.a2[:], mcol[:, 4 * KT:5 * KT, 0], 1.0, gffn[:], ALU.add, ALU.mult))
                link(v.tensor_copy(S.b2[:], mcol[:, 3 * KT:4 * KT, 0]))
                v.wait_ge(s_g, 1)
                v.wait_ge(s_gb, 32)
                for n, (dst, row) in enumerate(((S.g1, g1b), (S.g2, g2b))):
                    for h in range(2):
                        v.tensor_tensor(dst[:, 512 * h:512 * h + 512], pt[:, 2 * n + h, :],
                                        row[:, 512 * h:512 * h + 512], ALU.add)


class Projector:

    def __init__(self, s, A, S, name="pj"):
        self.A, self.S = A, S
        self.ring = s.sb(name + "ring", [P, 2, KT, UNIT])
        self.bank = s.ps(name + "bank", [P, 2, 2, 512])
        self.w_in = s.sems(name + "w_landed", 2)
        self.done = s.sems(name + "unit_done", 2)
        self.out = s.sems(name + "bank_free", 2)
        self.pairs = {"sp": 0, "pe": 0, "act": 0}

    def load(self, sp, unit0, pairs):
        g0 = self.pairs["sp"]
        with sp.Fori(0, pairs) as i:
            for z in range(2):
                sp.wait_ge(self.done[z], i + (g0 + 1))
                sp.dma_start(self.ring[:, z], self.A.w_in_units[bass.ds(i * 2 + (unit0 + z), 1)]
                             .rearrange("u p k n -> p (u k) n")).then_inc(self.w_in[z], 16)
        self.pairs["sp"] += pairs

    def credit_pe(self, pe):
        for z in range(2):
            pe.sem_inc(self.done[z], 1)

    def credit_act(self, act):
        for z in range(2):
            act.sem_inc(self.out[z], 1)

    def multiply(self, pe, pairs, tok0, ntok):
        g0 = self.pairs["pe"]
        with pe.Fori(0, pairs) as i:
            for z in range(2):
                pe.wait_ge(self.w_in[z], i * 16 + 16 * (g0 + 1))
                pe.wait_ge(self.out[z], i + (g0 + 1))
                for j in range(2):
                    for k in range(KT):
                        m = pe.matmul(self.bank[:, z, j, 0:ntok], self.ring[:, z, k, j * P:(j + 1) * P],
                                      self.S.hT[:, k, tok0:tok0 + ntok], start=(k == 0), stop=(k == KT - 1))
                m.then_inc(self.done[z], 1)
        self.pairs["pe"] += pairs


SMALL_COLS = ((0, 8), (8, 8), (16, 8), (24, 8), (32, 16), (48, 16))


def delta_project_stage(nc, A, C, S):
    with Scope(nc, "delta_project_") as s:
        pj = Projector(s, A, S)
        ws = s.sb("ws", [P, KT, 64])
        cw = s.sb("cw", [P, 24, 9])
        raw = s.sb("raw", [P, 2, 2, 2 * L])
        raw_used = s.sems("raw_used", 2)
        ssm = s.ps("ssm", [P, 2, 512])
        bf, bb, af, ab = (s.sb(n, [HA, 2 * L]) for n in ("beta_f", "beta_b", "a_f", "a_b"))
        sm = s.sb("sm", [HA, 2, 2 * L])
        al, dtb = s.sb("al", [HA, 2]), s.sb("dtb", [HA, 2])
        x, nx, u, w, r, m = (s.sb("gate_" + n, [HA, 4, 2 * L]) for n in "xnuwrm")
        g = s.sb("g", [HA, 2, 2 * L])
        rows = s.sb("rows", [HA, 2, 2, 2 * L])
        quant = s.sb("quant", [P, 2, 2 * L])
        pt = s.ps("pt", [P, 2, 512])
        s_in, s_sm, s_pj, s_k, s_se, s_gi, s_v, s_a, s_o, s_t, s_cw = (s.sem(n) for n in (
            "in", "small_done", "unit_copied", "taps", "small_copied", "gate_in", "chain", "act", "rows_out", "turned",
            "conv_w_in"))

        with nc.Block() as block:
            @block.sync
            def _(sp):
                sp.dma_start(ws[:], A.w_small).then_inc(s_in, 16)
                pj.load(sp, 0, 1)
                sp.dma_start(cw[:], A.conv_w_col).then_inc(s_cw, 16)
                sp.dma_start(sm[:], A.scan_masks[0:HA, 0:2]).then_inc(s_gi, 16)
                sp.dma_start(al[:], A.a_log).then_inc(s_gi, 16)
                sp.dma_start(dtb[:], A.dt_bias).then_inc(s_gi, 16)
                pj.load(sp, 2, 1)
                pj.load(sp, 4, 4)
                sp.wait_ge(s_v, 23)
                for d in range(2):
                    for k in range(2):
                        sp.dma_start(A.row_scratch[d, :, k].rearrange("t h n -> h t n"),
                                     rows[:, d, k, :].rearrange("h (t n) -> h t n", n=P)).then_inc(s_o, 16)
                sp.wait_ge(s_o, 64)

            @block.tensor
            def _(pe):
                pj.credit_pe(pe)
                pe.wait_ge(s_in, 16)
                for n, (c0, cols) in enumerate(SMALL_COLS):
                    q, b = n % 3, n // 3
                    for k in range(KT):
                        i = pe.matmul(ssm[32 * q:32 * q + cols, b, :], ws[:, k, c0:c0 + cols], S.hT[:, k, :],
                                      start=(k == 0), stop=(k == KT - 1))
                i.then_inc(s_sm, 1)
                pj.multiply(pe, 2, L, L)
                pj.multiply(pe, 4, 0, 2 * L)
                pe.wait_ge(s_v, 32)
                pe.wait_ge(s_a, 5)
                for d in range(2):
                    for t in range(NTILE):
                        i = pe.transpose(pt[:, d, t * P:(t + 1) * P], quant[:, d, t * P:(t + 1) * P], C.ident)
                    i.then_inc(s_t, 1)

            @block.scalar
            def _(act):
                def take(pairs, dst, tile0, t0, ntok):
                    g0 = pj.pairs["act"]
                    with act.Fori(0, pairs) as i:
                        for u in range(2):
                            act.wait_ge(pj.done[u], i + (g0 + 2))
                            act.wait_ge(raw_used[u], i + (g0 + 1))
                            for j in range(2):
                                act.activation(raw[:, u, j, 0:ntok], pj.bank[:, u, j, 0:ntok], ACT.Copy)
                            for j in range(2):
                                t = i * 4 + (tile0 + 2 * u + j)
                                m = act.activation(dst[:, bass.ds(t, 1), :], pj.bank[:, u, j:j + 1, 0:ntok], ACT.Copy,
                                                   scale=cw[:, bass.ds(i * 4 + (tile0 + t0 + 2 * u + j), 1), 4:5]
                                                   .rearrange("p o n -> p (o n)"))
                            m.then_inc(pj.out[u], 1)
                            act.wait_ge(pj.out[u], i + (g0 + 2))
                            act.sem_inc(s_pj, 1)
                    pj.pairs["act"] += pairs

                pj.credit_act(act)
                act.wait_ge(s_sm, 1)
                for n, ((c0, cols), dst) in enumerate(zip(SMALL_COLS, (bf, bb, af, ab, S.lf, S.lb))):
                    q, b = n % 3, n // 3
                    i = act.activation(dst[:], ssm[32 * q:32 * q + cols, b, :], ACT.Copy)
                i.then_inc(s_se, 1)
                act.wait_ge(s_cw, 16)
                take(1, S.pq, 0, 0, L)
                act.wait_ge(s_v, 6)
                act.activation(u[:], nx[:], ACT.Exp).then_inc(s_a, 1)
                take(1, S.pq, 4, 0, L)
                act.wait_ge(s_v, 7)
                act.activation(r[:], w[:], ACT.Ln).then_inc(s_a, 1)
                act.wait_ge(s_gi, 48)
                act.activation(al[:], al[:], ACT.Exp).then_inc(s_a, 1)
                take(2, S.pkv, 0, 8, 2 * L)
                act.wait_ge(s_v, 28)
                for d in range(2):
                    i = act.activation(u[:, d, :], rows[:, d, 1, :], ACT.Exp)
                for d in range(2):
                    i = act.activation(quant[96:96 + HA, d, :], w[:, d, :], ACT.Exp)
                for d in range(2):
                    i = act.activation(x[:, 2 + d, :], x[:, 2 + d, :], ACT.Sigmoid)
                i.then_inc(s_a, 1)
                act.wait_ge(s_a, 4)
                for d in range(2):
                    i = act.activation(quant[32:32 + HA, d, :], x[:, 2 + d, :], ACT.Copy)
                i.then_inc(s_a, 1)
                take(2, S.pkv, 8, 8, 2 * L)
                act.wait_ge(s_se, 1)

            @block.vector
            def _(v):
                link = Chain(v, s_v)

                def convolve(buf, t0, first, units, image_only, base0):
                    per = 15 if image_only else 19
                    seen = 0 if t0 == 0 else 4
                    with v.Fori(0, units // 2) as i:
                        for u in range(2):
                            v.wait_ge(s_pj, i * 2 + (seen + first + u + 1))
                            base = i * (2 * per) + (base0 + u * per)
                            n, last = 0, {}
                            tap = [(dr, dc) for dr in (0, -1, 1) for dc in (-1, 0, 1) if (dr, dc) != (0, 0)]
                            for dr, dc in tap:
                                for z in range(2):
                                    t = i * 4 + (2 * (first + u) + z)
                                    out = buf[:, bass.ds(t, 1), :].rearrange("p o n -> p (o n)")
                                    for image in ((True,) if image_only or dr else (True, False)):
                                        cols = slice(L, 2 * L) if image else slice(0, L)
                                        dst = out if image_only else out[:, cols]
                                        xin = raw[:, u, z, 0:L] if image_only else raw[:, u, z, cols]
                                        wt = cw[:, bass.ds(i * 4 + (2 * (first + u) + z + t0), 1),
                                                3 * (dr + 1) + dc + 1:3 * (dr + 1) + dc + 2].rearrange("p o n -> p (o n)")
                                        width = GRID_W if image else L
                                        nr = L // width
                                        o = dst.rearrange("p (r c) -> p r c", c=width)
                                        xx = xin.rearrange("p (r c) -> p r c", c=width)
                                        r0, r1 = max(0, -dr), min(nr, nr - dr)
                                        c0, c1 = max(0, -dc), min(width, width - dc)
                                        oo = o[:, r0:r1, c0:c1]
                                        if (z, image) in last:
                                            v.wait_ge(s_k, base + last[z, image])
                                        m = v.scalar_tensor_tensor(oo, xx[:, r0 + dr:r1 + dr, c0 + dc:c1 + dc], wt, oo,
                                                                   ALU.mult, ALU.add)
                                        n += 1
                                        m.then_inc(s_k if n <= per else raw_used[u], 1)
                                        last[z, image] = n
                            assert n == per + 1

                v.wait_ge(s_gi, 48)
                v.wait_ge(s_se, 1)
                for d, a in enumerate((af, ab)):
                    link(v.tensor_scalar(x[:, d, :], a[:], dtb[:, d:d + 1], None, ALU.add))
                for d, b in enumerate((bf, bb)):
                    link(v.tensor_copy(x[:, 2 + d, :], b[:]))
                link(v.tensor_scalar(nx[:], x[:], -1.0, None, ALU.mult))
                link(v.tensor_tensor(nx[:], nx[:], x[:], ALU.min))
                v.wait_ge(s_cw, 16)
                convolve(S.pq, 0, 0, 4, True, 0)
                v.wait_ge(s_a, 1)
                link(v.tensor_scalar(w[:], u[:], 1.0, None, ALU.add))
                link(v.tensor_scalar(m[:], w[:], 1.0, None, ALU.is_equal))
                link(v.scalar_tensor_tensor(nx[:], w[:], -1.0, m[:], ALU.add, ALU.add))
                link(v.reciprocal(nx[:], nx[:]))
                link(v.tensor_tensor(nx[:], nx[:], u[:], ALU.mult))
                link(v.tensor_tensor(m[:], m[:], u[:], ALU.mult))
                convolve(S.pkv, 8, 0, 2, False, 4 * 15)
                v.wait_ge(s_a, 2)
                link(v.tensor_tensor(r[:], r[:], nx[:], ALU.mult))
                link(v.tensor_tensor(r[:], r[:], m[:], ALU.add))
                link(v.scalar_tensor_tensor(u[:, 0:2, :], x[:, 0:2, :], 0.0, r[:, 0:2, :], ALU.max, ALU.add))
                link(v.scalar_tensor_tensor(u[:, 2:4, :], x[:, 2:4, :], 0.0, r[:, 2:4, :], ALU.min, ALU.subtract))
                v.wait_ge(s_a, 3)
                for d in range(2):
                    link(v.tensor_scalar(g[:, d, :], u[:, d, :], al[:, d:d + 1], -1.0, ALU.mult, ALU.mult))
                link(v.tensor_scalar(g[:], g[:], G_ZERO, None, ALU.max))
                link(v.tensor_tensor_scan(rows[:, 0, 1, :], sm[:, 0, :], g[:, 0, :], 0.0, ALU.mult, ALU.add))
                link(v.tensor_tensor_scan(rows[:, 1, 1, ::-1], sm[:, 1, ::-1], g[:, 1, ::-1], 0.0, ALU.mult, ALU.add))
                for d in range(2):
                    link(v.tensor_tensor(rows[:, d, 0, :], rows[:, d, 1, :], u[:, 2 + d, :], ALU.add))
                link(v.memset(quant[:], 0.0))
                for d in range(2):
                    gc = rows[:, d, 1, :].rearrange("h (t n) -> h t n", n=P)
                    end = P - 1 if d == 0 else 0
                    link(v.tensor_scalar(quant[0:HA, d, :], rows[:, d, 1, :], -1.0, None, ALU.mult))
                    link(v.tensor_tensor(w[:, d, :].rearrange("h (t n) -> h t n", n=P),
                                         gc[:, :, end:end + 1].to_broadcast([HA, NTILE, P]), gc, ALU.subtract))
                convolve(S.pkv, 8, 2, 2, False, 4 * 15 + 2 * 19)
                v.wait_ge(s_a, 4)
                for d in range(2):
                    link(v.scalar_tensor_tensor(m[:, d, :], u[:, d, :], -1.0, x[:, 2 + d, :], ALU.mult, ALU.mult))
                for d in range(2):
                    link(v.tensor_copy(quant[64:64 + HA, d, :], m[:, d, :]))
                convolve(S.pkv, 8, 4, 4, False, 4 * 15 + 4 * 19)
                for d in range(2):
                    v.wait_ge(s_t, d + 1)
                    link(v.tensor_copy(S.tokq[:, d], pt[:, d, :].rearrange("p (t n) -> p t n", n=P)))

            @block.gpsimd
            def _(g):
                for z in range(2):
                    g.sem_inc(raw_used[z], 1)


def delta_scan_stage(nc, A, C, S):
    G = HA // HALF
    DK = float(P) ** -0.5
    with Scope(nc, "delta_scan_") as s:
        lvl = s.sb("lvl", [P, 2, LEVELS, P])
        strict = s.sb("strict", [P, 2, 2, P])
        ksl = s.sb("ksl", [P, HALF, 2 * L])
        qsl = s.sb("qsl", [P, HALF, L])
        tmp = s.sb("tmp", [P, HALF, 2 * L])
        ktok = s.sb("ktok", [P, NTILE, HALF, P])
        vtok = s.sb("vtok", [P, NTILE, HALF, P])
        tq = s.sb("tq", [P, 2, NTILE, 4, HALF])
        d2 = range(2)
        rw = [s.sb(f"rw{d}", [P, 2, HALF, P]) for d in d2]
        eg = [s.sb(f"eg{d}", [P, HALF, P]) for d in d2]
        egl = [s.sb(f"egl{d}", [P, 2, HALF]) for d in d2]
        mt = [s.sb(f"mt{d}", [P, HALF, P]) for d in d2]
        ms = [s.sb(f"ms{d}", [P, 2, HALF, P]) for d in d2]
        tt = [s.sb(f"tt{d}", [P, HALF, P]) for d in d2]
        t_ = [s.sb(f"t{d}", [P, HALF, P]) for d in d2]
        y = [s.sb(f"y{d}", [P, HALF, P]) for d in d2]
        at = [s.sb(f"at{d}", [P, HALF, P]) for d in d2]
        qg = [s.sb(f"qg{d}", [P, 2, HALF, P]) for d in d2]
        vb = [s.sb(f"vb{d}", [P, HALF, P]) for d in d2]
        kd = [s.sb(f"kd{d}", [P, HALF, P]) for d in d2]
        rr = [s.sb(f"rr{d}", [P, HALF, P]) for d in d2]
        vn = [s.sb(f"vn{d}", [P, HALF, P]) for d in d2]
        st = [s.sb(f"st{d}", [P, HALF, P]) for d in d2]
        bank = [[s.ps(f"bank{d}{b}", [P, HALF, P]) for b in range(3)] for d in d2]
        pa, pb, pc = ([bank[d][b] for d in d2] for b in range(3))
        allbank = [bank[d][b] for d in d2 for b in range(3)]
        fw, fo = s.sb("fill_w", [P, 2, KT, P]), s.sb("fill_out", [P, 2, 2 * L])
        fbank = [s.ps(f"fill_bank{b}", [P, 2 * L]) for b in range(2)]
        f_in, f_pe, f_ev, f_st = s.sems("fill_in", 2), s.sem("fill_done"), s.sem("fill_copied"), s.sems("fill_stored", 2)

        def whole(f):
            return f % 4 == 0

        s_in = s.sem("masks_in")
        s_si, s_sq, s_ss, s_rv, s_rt, s_nm = (s.sem(n) for n in ("silu_done", "squared", "sums_done", "logs_done", "roots_done", "normalised"))
        s_kt, s_ktc, s_vs, s_vt, s_vtc, s_tq = (s.sem(n) for n in ("k_turned", "k_copied", "v_silu", "v_turned", "v_copied", "columns_taken"))
        rowsem = s.sems("rows_in", 2)
        (s_eg, s_dm, s_vk, s_g, s_mt, s_ms, s_m1, s_t0, s_y, s_yc, s_dl, s_t, s_ks, s_r, s_vn, s_vnc, s_o,
         s_oc, s_kv, s_s, s_mk, s_qg) = (s.sems(n, 2) for n in (
             "eg_done", "decay_done", "vk_scaled", "gram_done", "mt_done", "masked", "m1_done", "t_start",
             "y_done", "y_copied", "delta_done", "t_updated", "ks_done", "r_done", "vnew_done", "vnew_copied",
             "o_done", "o_copied", "kv_done", "state_done", "mask_added", "qg_done"))

        def tile(d, n):
            return n if d == 0 else (n ^ 1)

        with nc.Block() as block:
            @block.sync
            def _(sp):
                sp.dma_start(lvl[:], A.level_masks).then_inc(s_in, 16)
                sp.dma_start(strict[:], A.tri_masks).then_inc(s_in, 16)

                def rows(i, n):
                    for d in d2:
                        sp.wait_ge(s_mt[d], i * NTILE + (n + 1))
                        sp.dma_start(rw[d][:], A.row_scratch[d, tile(d, n)]
                                     [:, bass.ds(i * HALF, HALF), :].rearrange("(o k) h n -> o k h n", o=1)
                                     .to_broadcast([P, 2, HALF, P])).then_inc(rowsem[d], 16)

                def store(i, f):
                    sp.wait_ge(f_ev, i * FILL + (f + 3))
                    if whole(f):
                        sp.dma_start(A.fill_whole[bass.ds(i * (FILL // 4) + f // 4, 1)].rearrange("c p n -> p (c n)"),
                                     fo[:, f % 2, :]).then_inc(f_st[f % 2], 16)
                    else:
                        sp.dma_start(A.fill_latent[bass.ds(i * (FILL * 3 // 4) + (f - f // 4 - 1), 1)]
                                     .rearrange("c p n -> p (c n)"), fo[:, f % 2, 0:L]).then_inc(f_st[f % 2], 16)

                with sp.Fori(0, G) as i:
                    rows(i, 0)
                    for f in range(FILL):
                        sp.wait_ge(f_pe, i * FILL + (f + 1))
                        sp.dma_start(fw[:, f % 2], A.w_fill[bass.ds(i * FILL + f, 1)]
                                     .rearrange("c p k n -> p (c k) n")).then_inc(f_in[f % 2], 16)
                        if f >= EARLY and f % 3 == 1 and (f - EARLY) // 3 + 1 < NTILE:
                            rows(i, (f - EARLY) // 3 + 1)
                        if f >= 3:
                            store(i, f - 3)
                    for f in range(FILL - 3, FILL):
                        store(i, f)
                for z in range(2):
                    sp.wait_ge(f_st[z], 16 + 16 * G * FILL // 2)

            @block.scalar
            def _(act):
                act.wait_ge(s_in, 32)

                def prep(n):
                    for d in d2:
                        lat = n >= 2
                        act.wait_ge(rowsem[d], i * (16 * NTILE) + 16 * (n + 1))
                        act.wait_ge(s_qg[d], i * NTILE + (n + 1))
                        act.activation(eg[d][:], rw[d][:, 1], ACT.Exp).then_inc(s_eg[d], 1)
                        act.wait_ge(s_mk[d], i * NTILE + (n + 1))
                        for k in range(2 if lat else 1):
                            for h in range(HALF):
                                m = act.activation(rw[d][:, k, h, :], rw[d][:, k, h, :], ACT.Exp,
                                                   bias=tq[:, d, tile(d, n), 0, h:h + 1])
                        m.then_inc(s_dm[d], 1)

                def copy_fill(f):
                    act.wait_ge(f_pe, i * FILL + (f + 3))
                    act.wait_ge(f_st[f % 2], i * (8 * FILL) + 16 * (f // 2 + 1))
                    n = 2 * L if whole(f) else L
                    act.activation(fo[:, f % 2, 0:n], fbank[f % 2][:, 0:n], ACT.Copy).then_inc(f_ev, 1)

                with act.Fori(0, G) as i:
                    act.wait_ge(s_vn[0], i * NTILE + 1)
                    act.wait_ge(s_vn[1], i * NTILE + 1)
                    act.wait_ge(s_qg[0], i * NTILE + 1)
                    act.wait_ge(s_qg[1], i * NTILE + 1)
                    act.activation(ksl[:], S.pkv[:, bass.ds(i * HALF, HALF), :], ACT.Silu)
                    act.activation(qsl[:], S.pq[:, bass.ds(i * HALF, HALF), :], ACT.Silu).then_inc(s_si, 1)
                    for f in range(4):
                        copy_fill(f)
                    for h in range(HALF):
                        act.wait_ge(s_ss, i * 8 + (h + 1))
                        m = act.activation(tmp[:, h, :], allbank[h][:].rearrange("p a n -> p (a n)"), ACT.Ln, bias=C.eps[:])
                    m.then_inc(s_rv, 1)
                    act.wait_ge(s_rv, i * 2 + 1)
                    act.activation(tmp[:], tmp[:], ACT.Exp, scale=-0.5).then_inc(s_rt, 1)
                    for f in range(4, 7):
                        copy_fill(f)
                    for b in range(2):
                        act.wait_ge(s_ss, i * 8 + (4 + 2 * b + 2))
                        m = act.activation(tmp[:, 2 * b:2 * b + 2, 0:L],
                                           allbank[4 + b][:].rearrange("p (h a) n -> p h (a n)", h=2), ACT.Ln, bias=C.eps[:])
                    m.then_inc(s_rv, 1)
                    act.wait_ge(s_rv, i * 2 + 2)
                    act.activation(tmp[:, :, 0:L], tmp[:, :, 0:L], ACT.Exp, scale=-0.5).then_inc(s_rt, 1)
                    for f in range(7, 9):
                        copy_fill(f)
                    act.wait_ge(s_nm, i * 2 + 2)
                    act.activation(tmp[:], S.pkv[:, bass.ds(i * HALF + HA, HALF), :], ACT.Silu).then_inc(s_vs, 1)
                    for b in range(4):
                        act.wait_ge(s_kt, i * 4 + (b + 1))
                        act.activation(ktok[:, b], allbank[b][:], ACT.Copy).then_inc(s_ktc, 1)
                    for f in range(9, EARLY - 1):
                        copy_fill(f)
                    for b in range(4):
                        act.wait_ge(s_vt, i * 4 + (b + 1))
                        act.activation(vtok[:, b], allbank[(4 + b) % 6][:], ACT.Copy).then_inc(s_vtc, 1)
                    act.wait_ge(s_tq, i + 1)
                    act.wait_ge(s_vtc, i * 4 + 4)
                    act.wait_ge(s_ktc, i * 4 + 4)
                    prep(0)
                    for n in range(NTILE):
                        for l in range(1, LEVELS):
                            for d in d2:
                                act.wait_ge(s_y[d], i * (6 * NTILE) + (6 * n + l))
                                act.activation(y[d][:], pa[d][:], ACT.Copy).then_inc(s_yc[d], 1)
                            if l % 2:
                                copy_fill(EARLY + 3 * n + l // 2 - 1)
                            if l == 2:
                                for d in d2:
                                    act.wait_ge(s_r[d], i * NTILE + (n + 1))
                                    if n > 0:
                                        act.wait_ge(s_kv[d], i * 3 + n)
                                    for h in range(HALF):
                                        act.activation(vb[d][:, h, :], vtok[:, tile(d, n), h, :], ACT.Copy,
                                                       scale=tq[:, d, tile(d, n), 1, h:h + 1])
                                    for h in range(HALF):
                                        m = act.activation(kd[d][:, h, :], ktok[:, tile(d, n), h, :], ACT.Copy,
                                                           scale=tq[:, d, tile(d, n), 3, h:h + 1])
                                    m.then_inc(s_vk[d], 1)
                            if l == 4 and n + 1 < NTILE:
                                prep(n + 1)
                        for d in d2:
                            act.wait_ge(s_vn[d], i * NTILE + (n + 2))
                            act.activation(vn[d][:], pc[d][:], ACT.Copy).then_inc(s_vnc[d], 1)
                    copy_fill(FILL - 1)

            @block.gpsimd
            def _(g):
                for d in d2:
                    for q in (s_mt, s_qg, s_r, s_vn, s_s, s_oc):
                        g.sem_inc(q[d], 1)
                g.sem_inc(f_pe, 2)
                g.sem_inc(f_ev, 2)
                for z in range(2):
                    g.sem_inc(f_st[z], 16)
                g.wait_ge(s_in, 32)

                def prep(n):
                    for d in d2:
                        end = P - 1 if d == 0 else 0
                        g.wait_ge(s_eg[d], i * NTILE + (n + 1))
                        for k in range(2 if n >= 2 else 1):
                            m = g.tensor_tensor(rw[d][:, k], rw[d][:, k], wide(strict[:, d, k, :], HALF), ALU.add)
                        m.then_inc(s_mk[d], 1)
                        if n >= 2:
                            t0 = (tile(d, n) - 2) * P
                            g.tensor_tensor(qg[d][:, n % 2], eg[d][:], qsl[:, :, t0:t0 + P], ALU.mult)
                        g.tensor_copy(egl[d][:, n % 2, :], eg[d][:, :, end]).then_inc(s_qg[d], 1)

                with g.Fori(0, G) as i:
                    g.wait_ge(s_si, i + 1)
                    g.tensor_tensor(tmp[:], ksl[:], ksl[:], ALU.mult).then_inc(s_sq, 1)
                    g.wait_ge(s_nm, i * 2 + 1)
                    g.tensor_tensor(tmp[:, :, 0:L], qsl[:], qsl[:], ALU.mult).then_inc(s_sq, 1)
                    g.wait_ge(s_nm, i * 2 + 2)
                    prep(0)
                    for n in range(NTILE):
                        for l in range(LEVELS):
                            for d in d2:
                                g.wait_ge(s_mt[d], i * NTILE + (n + 2))
                                if l >= 2:
                                    g.wait_ge(s_y[d] if l > 2 else s_t0[d],
                                              i * (6 * NTILE) + (6 * n + l - 2) if l > 2 else i * NTILE + (n + 1))
                                g.tensor_tensor(ms[d][:, l % 2], mt[d][:], wide(lvl[:, d, l, :], HALF),
                                                ALU.mult).then_inc(s_ms[d], 1)
                            if l == 5 and n + 1 < NTILE:
                                prep(n + 1)

            @block.vector
            def _(v):
                v.wait_ge(s_in, 32)
                with v.Fori(0, G) as i:
                    for d in d2:
                        for k in range(4):
                            m = v.tensor_copy(tq[:, d, :, k, :], S.tokq[:, d, :, bass.ds(i * HALF + 32 * k, HALF)])
                    m.then_inc(s_tq, 1)
                    v.wait_ge(s_rt, i * 2 + 1)
                    v.tensor_tensor(ksl[:], ksl[:], tmp[:], ALU.mult).then_inc(s_nm, 1)
                    v.wait_ge(s_rt, i * 2 + 2)
                    v.scalar_tensor_tensor(qsl[:], qsl[:], DK, tmp[:, :, 0:L], ALU.mult, ALU.mult).then_inc(s_nm, 1)
                    for n in range(NTILE):
                        lat = n >= 2
                        for d in d2:
                            v.wait_ge(s_dm[d], i * NTILE + (n + 1))
                            v.wait_ge(s_g[d], i * NTILE + (n + 1))
                            m = v.scalar_tensor_tensor(mt[d][:], pa[d][:], -1.0, rw[d][:, 0], ALU.mult, ALU.mult)
                            if lat:
                                m = v.tensor_tensor(at[d][:], pb[d][:], rw[d][:, 1], ALU.mult)
                            m.then_inc(s_mt[d], 1)
                        for d in d2:
                            v.wait_ge(s_m1[d], i * NTILE + (n + 1))
                            v.tensor_tensor(tt[d][:], ms[d][:, 0], wide(C.ident, HALF), ALU.add)
                            v.tensor_tensor(t_[d][:], pc[d][:], wide(C.ident, HALF), ALU.add).then_inc(s_t0[d], 1)
                        for l in range(1, LEVELS):
                            for d in d2:
                                v.wait_ge(s_dl[d], i * (6 * NTILE) + (6 * n + l))
                                m = v.tensor_tensor(tt[d][:], tt[d][:], pc[d][:], ALU.add)
                                if l < LEVELS - 1:
                                    m = v.tensor_tensor(t_[d][:], t_[d][:], pb[d][:], ALU.add)
                                m.then_inc(s_t[d], 1)
                        for d in d2:
                            v.wait_ge(s_vk[d], i * NTILE + (n + 1))
                            if n == 0:
                                v.tensor_copy(rr[d][:], vb[d][:]).then_inc(s_r[d], 1)
                            else:
                                v.wait_ge(s_ks[d], i * 3 + n)
                                for h in range(HALF):
                                    m = v.scalar_tensor_tensor(rr[d][:, h, :], pb[d][:, h, :],
                                                               tq[:, d, tile(d, n), 2, h:h + 1], vb[d][:, h, :],
                                                               ALU.mult, ALU.add)
                                m.then_inc(s_r[d], 1)
                        for d in d2:
                            if n < NTILE - 1:
                                v.wait_ge(s_kv[d], i * 3 + (n + 1))
                                if n == 0:
                                    m = v.tensor_copy(st[d][:], pa[d][:])
                                else:
                                    for h in range(HALF):
                                        m = v.scalar_tensor_tensor(st[d][:, h, :], st[d][:, h, :],
                                                                   egl[d][:, n % 2, h:h + 1], pa[d][:, h, :],
                                                                   ALU.mult, ALU.add)
                                m.then_inc(s_s[d], 1)
                        if lat:
                            for d in d2:
                                v.wait_ge(s_o[d], i * 2 + (n - 1))
                                t0 = (tile(d, n) - 2) * P
                                dst = S.oa[:, bass.ds(i * HALF, HALF), t0:t0 + P]
                                if n == 2:
                                    m = v.tensor_copy(dst, pb[d][:])
                                else:
                                    m = v.tensor_tensor(dst, dst, pb[d][:], ALU.add)
                                m.then_inc(s_oc[d], 1)

            @block.tensor
            def _(pe):
                def fill(f, half):
                    if half == 0:
                        pe.wait_ge(f_in[f % 2], i * (8 * FILL) + 16 * (f // 2 + 1))
                        pe.wait_ge(f_ev, i * FILL + (f + 1))
                    tok = slice(0, 2 * L) if whole(f) else slice(L, 2 * L)
                    for k in range(half * KT // 2, (half + 1) * KT // 2):
                        m = pe.matmul(fbank[f % 2][:, 0:tok.stop - tok.start], fw[:, f % 2, k, :], S.hT[:, k, tok],
                                      start=(k == 0), stop=(k == KT - 1))
                    if half:
                        m.then_inc(f_pe, 1)

                with pe.Fori(0, G) as i:
                    for d in d2:
                        pe.wait_ge(s_oc[d], i * 2 + 1)
                    for f in range(4):
                        fill(f, 0)
                        fill(f, 1)
                    for h in range(HALF):
                        if h == 0:
                            pe.wait_ge(s_sq, i * 2 + 1)
                        pe.matmul(allbank[h][:].rearrange("p a n -> p (a n)"), C.ones, tmp[:, h, :],
                                  start=True, stop=True).then_inc(s_ss, 1)
                    for f in range(4, 7):
                        fill(f, 0)
                        fill(f, 1)
                    for h in range(HALF):
                        if h == 0:
                            pe.wait_ge(s_sq, i * 2 + 2)
                        pe.matmul(allbank[4 + h // 2][:].rearrange("p a n -> p (a n)")[:, L * (h % 2):L * (h % 2 + 1)],
                                  C.ones, tmp[:, h, 0:L], start=True, stop=True).then_inc(s_ss, 1)
                    for f in range(7, 9):
                        fill(f, 0)
                        fill(f, 1)
                    pe.wait_ge(s_nm, i * 2 + 2)
                    for t in range(NTILE):
                        for h in range(HALF):
                            m = pe.transpose(allbank[t][:, h, :], ksl[:, h, t * P:(t + 1) * P], C.ident)
                        m.then_inc(s_kt, 1)
                    for f in range(9, EARLY):
                        fill(f, 0)
                        fill(f, 1)
                    pe.wait_ge(s_vs, i + 1)
                    for t in range(NTILE):
                        if t == 2:
                            pe.wait_ge(s_ktc, i * 4 + 2)
                        for h in range(HALF):
                            m = pe.transpose(allbank[(4 + t) % 6][:, h, :], tmp[:, h, t * P:(t + 1) * P], C.ident)
                        m.then_inc(s_vt, 1)
                    pe.wait_ge(s_ktc, i * 4 + 4)
                    pe.wait_ge(s_vtc, i * 4 + 4)
                    for n in range(NTILE):
                        lat = n >= 2
                        for d in d2:
                            t0 = tile(d, n) * P
                            if 0 < n:
                                pe.wait_ge(s_s[d], i * 3 + (n + 1))
                                pe.wait_ge(s_r[d], i * NTILE + (n + 1))
                            for h in range(HALF):
                                m = pe.matmul(pa[d][:, h, :], ksl[:, h, t0:t0 + P], ksl[:, h, t0:t0 + P],
                                              start=True, stop=True)
                            if lat:
                                if n == 3:
                                    pe.wait_ge(s_oc[d], i * 2 + 2)
                                for h in range(HALF):
                                    m = pe.matmul(pb[d][:, h, :], ksl[:, h, t0:t0 + P],
                                                  qsl[:, h, t0 - L:t0 - L + P], start=True, stop=True)
                            m.then_inc(s_g[d], 1)
                        for d in d2:
                            pe.wait_ge(s_ms[d], i * (LEVELS * NTILE) + (LEVELS * n + 1))
                            if n > 0:
                                pe.wait_ge(s_vnc[d], i * NTILE + n)
                            for h in range(HALF):
                                m = pe.transpose(pc[d][:, h, :], ms[d][:, 0, h, :], C.ident)
                            m.then_inc(s_m1[d], 1)
                        for l in range(1, LEVELS):
                            for d in d2:
                                pe.wait_ge(s_ms[d], i * (LEVELS * NTILE) + (LEVELS * n + l + 1))
                                if l == 1:
                                    pe.wait_ge(s_t0[d], i * NTILE + (n + 1))
                                else:
                                    pe.wait_ge(s_t[d], i * (6 * NTILE) + (6 * n + l - 1))
                                for h in range(HALF):
                                    m = pe.matmul(pa[d][:, h, :], ms[d][:, l % 2, h, :], t_[d][:, h, :],
                                                  start=True, stop=True)
                                m.then_inc(s_y[d], 1)
                            fill(EARLY + 3 * n + (l - 1) // 2, (l - 1) % 2)
                            for d in d2:
                                pe.wait_ge(s_yc[d], i * (6 * NTILE) + (6 * n + l))
                                for h in range(HALF):
                                    if l < LEVELS - 1:
                                        pe.matmul(pb[d][:, h, :], tt[d][:, h, :], y[d][:, h, :],
                                                  start=True, stop=True)
                                    m = pe.matmul(pc[d][:, h, :], y[d][:, h, :], tt[d][:, h, :],
                                                  start=True, stop=True)
                                m.then_inc(s_dl[d], 1)
                        if n > 0:
                            for d in d2:
                                t0 = tile(d, n) * P
                                pe.wait_ge(s_t[d], i * (6 * NTILE) + (6 * n + LEVELS - 2))
                                for h in range(HALF):
                                    m = pe.matmul(pb[d][:, h, :], ksl[:, h, t0:t0 + P], st[d][:, h, :],
                                                  start=True, stop=True)
                                m.then_inc(s_ks[d], 1)
                        for d in d2:
                            pe.wait_ge(s_t[d], i * (6 * NTILE) + (6 * n + LEVELS - 1))
                            pe.wait_ge(s_r[d], i * NTILE + (n + 2))
                            for h in range(HALF):
                                m = pe.matmul(pc[d][:, h, :], tt[d][:, h, :], rr[d][:, h, :], start=True, stop=True)
                            m.then_inc(s_vn[d], 1)
                        for d in d2:
                            pe.wait_ge(s_vnc[d], i * NTILE + (n + 1))
                            if lat:
                                for h in range(HALF):
                                    pe.matmul(pb[d][:, h, :], vn[d][:, h, :], at[d][:, h, :],
                                              start=True, stop=False)
                                    m = pe.matmul(pb[d][:, h, :], st[d][:, h, :], qg[d][:, n % 2, h, :],
                                                  start=False, stop=True)
                                m.then_inc(s_o[d], 1)
                            if n < NTILE - 1:
                                for h in range(HALF):
                                    m = pe.matmul(pa[d][:, h, :], kd[d][:, h, :], vn[d][:, h, :],
                                                  start=True, stop=True)
                                m.then_inc(s_kv[d], 1)


def linear_attention_stage(nc, A, C, S):
    d2 = range(2)
    DK = float(P) ** -0.5
    IG = 1.0 / GATE_NORM
    NH = HB
    DV2 = 2
    with Scope(nc, "linear_") as s:
        gq = s.sb("gq", [P, NH, L])
        gkv = s.sb("gkv", [P, NH + NH * DV2, 2 * L])
        gk, gv = gkv[:, 0:NH, :], gkv[:, NH:, :]
        wg = s.sb("wg", [GATE_RANK, 2, NH * P])
        bg = s.sb("bg", [P, 2, NH])
        sm = s.sb("sm", [P, 4, 2 * L])
        pick = s.sb("pick", [P, 2, 2, P], I32)
        spare = S.hT[:].rearrange("p (d h) n -> p d h n", d=2)
        z = s.sb("z", [P, NH, 2 * L])
        gc = s.sb("gc", [P, NH, 2 * L])
        gt = s.sb("gt", [P, NH, 2 * L])
        w = s.sb("w", [P, NH, 2 * L])
        zz, ww = (z[:], spare[:, 0]), (w[:], spare[:, 1])
        qa, ka, qc, kc = (s.sb(n, [P, NH, L]) for n in ("qa", "ka", "qc", "kc"))
        qt = [s.sb(f"qt{d}", [P, NH, L]) for d in d2]
        ktd = [s.sb(f"ktd{d}", [P, NTILE, NH, P]) for d in d2]
        at = [s.sb(f"at{d}", [P, 2, NH, P]) for d in d2]
        egl = s.sb("egl", [P, 2, NH, NTILE])
        vt = s.sb("vt", [P, NTILE, NH * DV2, P])
        st = [[s.sb(f"st{d}{n}", [P, NH, DV2 * P]) for n in range(3)] for d in d2]
        bank = [s.ps(f"bank{b}", [P, 4, P]) for b in range(8)]
        (s_in, s_zp, s_z, s_ab, s_ln, s_l, s_gc, s_d, s_ex, s_m, s_att, s_at, s_ktp, s_kt, s_vtp, s_vt, s_kv, s_st,
         s_o, s_oc, s_zero, s_gl, s_sum, s_x) = (s.sem(n) for n in (
             "in", "z_done", "z_biased", "exp_abs", "softplus", "log_gate", "cumsum", "exponent", "exped", "scaled",
             "att_done", "att_picked", "kd_turned", "kd_copied", "v_turned", "v_copied", "kv_done", "state_done",
             "o_done", "o_copied", "cleared", "end_decay", "att_summed", "projections_in"))

        def chunks(ap):
            return ap.rearrange("p h (c n) -> p (h c) n", n=GC)

        def tiles(ap):
            return ap.rearrange("p h (c n) -> p (h c) n", n=P)

        with nc.Block() as block:
            @block.sync
            def _(sp):
                sp.dma_start(wg[:], A.gate_w).then_inc(s_in, 16)
                sp.dma_start(bg[:], A.gate_b).then_inc(s_in, 16)
                sp.dma_start(sm[:], A.scan_masks).then_inc(s_in, 16)
                sp.dma_start(pick[:], A.pick_masks).then_inc(s_in, 16)
                sp.dma_start(gkv[:], A.fill_whole.rearrange("c p n -> p c n")).then_inc(s_x, 16)
                sp.dma_start(gq[:], A.fill_latent[0:NH].rearrange("c p n -> p c n")).then_inc(s_x, 16)

            @block.gpsimd
            def _(g):
                for d in d2:
                    m = g.memset(at[d][:], 0.0)
                m.then_inc(s_zero, 1)

            @block.tensor
            def _(pe):
                pe.wait_ge(s_in, 64)

                def gates(d):
                    lr = (S.lf, S.lb)[d]
                    if d:
                        pe.wait_ge(s_z, NH)
                    for h in range(NH):
                        m = pe.matmul(bank[h][:].rearrange("p a n -> p (a n)"), wg[:, d, h * P:(h + 1) * P], lr[:],
                                      start=True, stop=True)
                    m.then_inc(s_zp, 1)

                gates(0)
                gates(1)
                pe.wait_ge(s_x, 32)
                for t in range(NTILE):
                    for u in range(2):
                        b = 2 * t + u
                        if b >= 4:
                            pe.wait_ge(s_vt, b - 3)
                        for j in range(4):
                            m = pe.transpose(bank[4 + b % 4][:, j, :], gv[:, 4 * u + j, t * P:(t + 1) * P], C.ident)
                        m.then_inc(s_vtp, 1)
                pe.wait_ge(s_vt, 8)
                for d in d2:
                    pe.wait_ge(s_z, 2 * NH)
                    if d:
                        pe.wait_ge(s_at, 4)
                    pe.wait_ge(s_m, 6 * d + 4)
                    for t in range(2):
                        for c, (kk, qq) in enumerate(((ka, qa), (kc, qc))):
                            for h in range(NH):
                                m = pe.matmul(bank[2 * t + c][:, h, :], kk[:, h, t * P:(t + 1) * P],
                                              qq[:, h, t * P:(t + 1) * P], start=True, stop=True)
                            m.then_inc(s_att, 1)
                    pe.wait_ge(s_m, 6 * d + 6)
                    if d:
                        pe.wait_ge(s_kt, 4)
                    for t in range(NTILE):
                        for h in range(NH):
                            m = pe.transpose(bank[4 + t][:, h, :], ww[d][:, h, t * P:(t + 1) * P], C.ident)
                        m.then_inc(s_ktp, 1)
                for n in range(3):
                    for d in d2:
                        t = n ^ d
                        pe.wait_ge(s_kt, 4 * d + 4)
                        if n == 0:
                            pe.wait_ge(s_at, 8)
                        else:
                            pe.wait_ge(s_st, 2 * (n - 1) + d + 1)
                        for h in range(NH):
                            o = bank[2 * d + h // 2][:].rearrange("p a n -> p (a n)")[:, 256 * (h % 2):256 * (h % 2) + 256]
                            m = pe.matmul(o, ktd[d][:, t, h, :], vt[:, t, 2 * h:2 * h + 2, :].rearrange("p a n -> p (a n)"),
                                          start=True, stop=True)
                        m.then_inc(s_kv, 1)
                pe.wait_ge(s_sum, 1)
                pe.wait_ge(s_kt, 8)
                pe.wait_ge(s_st, 6)
                for t in range(2):
                    sf, sb = st[0][1 + t], st[1][2 - t]
                    for u in range(2):
                        for j in range(4):
                            c = 4 * u + j
                            h, e = c // 2, c % 2
                            o = bank[4 + 2 * t + u][:, j, :]
                            pe.matmul(o, vt[:, 2 + t, c, :], at[0][:, t, h, :], start=True, stop=False)
                            pe.matmul(o, sf[:, h, e * P:(e + 1) * P], qt[0][:, h, t * P:(t + 1) * P],
                                      start=False, stop=False)
                            m = pe.matmul(o, sb[:, h, e * P:(e + 1) * P], qt[1][:, h, t * P:(t + 1) * P],
                                          start=False, stop=True)
                        m.then_inc(s_o, 1)

            @block.scalar
            def _(act):
                for d in d2:
                    act.wait_ge(s_z, NH * (d + 1))
                    act.activation(ww[d], zz[d], ACT.Abs).then_inc(s_ab, 1)
                    act.wait_ge(s_ab, 2 * d + 1)
                    act.activation(ww[d], ww[d], ACT.Exp, scale=-1.0).then_inc(s_ab, 1)
                    act.wait_ge(s_ab, 2 * d + 2)
                    act.activation(ww[d], ww[d], ACT.Ln, bias=1.0).then_inc(s_ln, 1)
                for b in range(8):
                    t, u = b // 2, b % 2
                    act.wait_ge(s_vtp, b + 1)
                    act.activation(vt[:, t, 4 * u:4 * u + 4, :], bank[4 + b % 4][:], ACT.Copy).then_inc(s_vt, 1)
                for d in d2:
                    w = ww[d]
                    act.wait_ge(s_gc, d + 1)
                    end = P - 1 if d == 0 else 0
                    act.activation(egl[:, d], gt[:].rearrange("p h (t n) -> p h t n", n=P)[:, :, :, end],
                                   ACT.Exp, scale=IG).then_inc(s_gl, 1)
                    for e, (src, cols, sc) in enumerate((
                            (w, slice(L, 2 * L), IG), (w, slice(L, 2 * L), -IG), (gc, slice(L, 2 * L), IG),
                            (w, slice(L, 2 * L), IG), (gt, slice(L, 2 * L), IG), (w, slice(0, 2 * L), IG))):
                        act.wait_ge(s_d, 3 * d + (0, 1, 1, 2, 2, 3)[e] + (1 if e == 0 else 0))
                        if e:
                            act.wait_ge(s_m, 6 * d + e)
                        n = cols.stop - cols.start
                        act.activation(zz[d][:, :, 0:n], src[:, :, cols], ACT.Exp, scale=sc).then_inc(s_ex, 1)
                    for t in range(NTILE):
                        act.wait_ge(s_ktp, 4 * d + t + 1)
                        act.activation(ktd[d][:, t], bank[4 + t][:], ACT.Copy).then_inc(s_kt, 1)
                for b in range(4):
                    t, u = b // 2, b % 2
                    act.wait_ge(s_o, b + 1)
                    act.activation(S.ob[:, 4 * u:4 * u + 4, t * P:(t + 1) * P], bank[4 + b][:], ACT.Copy).then_inc(s_oc, 1)
                act.wait_ge(s_oc, 4)

            @block.vector
            def _(v):
                v.wait_ge(s_in, 64)
                for d in d2:
                    v.wait_ge(s_zp, d + 1)
                    for h in range(NH):
                        v.tensor_scalar(zz[d][:, h, :], bank[h][:].rearrange("p a n -> p (a n)"), bg[:, d, h:h + 1], None,
                                        ALU.add).then_inc(s_z, 1)
                for d in d2:
                    z, w = zz[d], ww[d]
                    v.wait_ge(s_ln, d + 1)
                    v.scalar_tensor_tensor(z, z, 0.0, w, ALU.min, ALU.subtract).then_inc(s_l, 1)
                    v.wait_ge(s_l, d + 1)
                    for mk, dst in ((2, gc), (0, gt)):
                        for h in range(NH):
                            o, l, k = dst[:, h, :], z[:, h, :], sm[:, mk + d, :]
                            if d:
                                o, l, k = dst[:, h, ::-1], z[:, h, ::-1], sm[:, mk + d, ::-1]
                            m = v.tensor_tensor_scan(o, k, l, 0.0, ALU.mult, ALU.add)
                    m.then_inc(s_gc, 1)
                    v.wait_ge(s_gc, d + 1)
                    lat = slice(L, 2 * L)
                    mid = GC // 2 if d == 0 else GC - 1 - GC // 2
                    cend, tend = (GC - 1, P - 1) if d == 0 else (0, 0)
                    gcl, wl = gc[:, :, lat], w[:, :, lat]

                    def less(dst, src, at_, n, flip):
                        c = src.rearrange("p h (c n) -> p h c n", n=n)
                        o = dst.rearrange("p h (c n) -> p h c n", n=n)
                        r = c[:, :, :, at_:at_ + 1].to_broadcast(list(c.shape))
                        for h in range(NH):
                            a, b = (r[:, h], c[:, h]) if flip else (c[:, h], r[:, h])
                            m = v.tensor_tensor(o[:, h], a, b, ALU.subtract)
                        m.then_inc(s_d, 1)

                    less(wl, gcl, mid, GC, False)
                    def times(dst, x, n, sc, e):
                        v.wait_ge(s_ex, 6 * d + e + 1)
                        v.scalar_tensor_tensor(dst, z[:, :, 0:n], sc, x, ALU.mult, ALU.mult).then_inc(s_m, 1)
                    if d:
                        v.wait_ge(s_att, 4)
                    else:
                        v.wait_ge(s_x, 32)
                    times(qa[:], gq[:], L, DK, 0)
                    times(ka[:], gk[:, :, lat], L, 1.0, 1)
                    less(wl, gcl, cend, GC, True)
                    times(qc[:], gq[:], L, DK, 2)
                    times(kc[:], gk[:, :, lat], L, 1.0, 3)
                    less(w, gt[:], tend, P, True)
                    times(qt[d][:], gq[:], L, DK, 4)
                    times(w, gk, 2 * L, 1.0, 5)
                    if d == 0:
                        v.wait_ge(s_zero, 1)
                    for t in range(2):
                        for c in range(2):
                            v.wait_ge(s_att, 4 * d + 2 * t + c + 1)
                            v.copy_predicated(at[d][:, t], wide(pick[:, d, c, :], NH), bank[2 * t + c][:]).then_inc(s_at, 1)
                            v.wait_ge(s_at, 4 * d + 2 * t + c + 1)
                v.wait_ge(s_at, 8)
                v.tensor_tensor(at[0][:], at[0][:], at[1][:], ALU.add).then_inc(s_sum, 1)
                v.wait_ge(s_gl, 2)
                for n in range(3):
                    for d in d2:
                        t = n ^ d
                        v.wait_ge(s_kv, 2 * n + d + 1)
                        for h in range(NH):
                            o = bank[2 * d + h // 2][:].rearrange("p a n -> p (a n)")[:, 256 * (h % 2):256 * (h % 2) + 256]
                            if n == 0:
                                m = v.tensor_copy(st[d][n][:, h, :], o)
                            else:
                                m = v.scalar_tensor_tensor(st[d][n][:, h, :], st[d][n - 1][:, h, :],
                                                           egl[:, d, h, t:t + 1], o, ALU.mult, ALU.add)
                        m.then_inc(s_st, 1)
                        v.wait_ge(s_st, 2 * n + d + 1)


def merge_stage(nc, A, C, S):
    with Scope(nc, "merge_") as s:
        pz = s.sb("pz", [P, 4 * HA, L])

        w, s_w = [s.sb(f"w{n}", [P, KT, D]) for n in range(2)], s.sems("branch_weights_in", 2)
        sq, sqb = s.sb("sq", [P, HA, L]), s.sb("sqb", [P, HA, L])
        ra, rb = s.sb("ra", [P, HA, L]), s.sb("rb", [P, HB, L])
        gain = s.sb("gain", [P, 3])
        y = s.sb("y", [P, HA, L])
        junk = s.sb("junk", [P, D])
        ss, rstd = s.sb("ss", [P, 2]), s.sb("rstd", [P, 2])
        bank = [s.ps(f"bank{b}", [P, 2, L]) for b in range(8)]
        (s_in, s_wo, s_x, s_sq, s_ss, s_v, s_rt, s_sil, s_ya, s_pa, s_t, s_y, s_z, s_xs, s_n, s_tr, s_h, s_pz, s_ln, s_sqb) = (
            s.sem(n) for n in ("in", "wo_in", "x_in", "squared", "sums", "chain", "rooted", "silu", "gated",
                               "branch", "mixed", "y_done", "out_done", "x_squares", "norm", "turned", "h_done",
                               "projections_in", "logs_done",
                               "linear_squared"))
        with nc.Block() as block:
            @block.sync
            def _(sp):
                sp.dma_start(gain[:], A.head_gains).then_inc(s_in, 16)
                sp.dma_start(pz[:, 0:2 * HA], A.fill_latent[HB:HB + 2 * HA].rearrange("c p n -> p c n")).then_inc(s_in, 16)
                sp.dma_start(w[0][:], A.w_out_a.rearrange("(k p) n -> p k n", p=P)).then_inc(s_w[0], 16)
                sp.dma_start(w[1][:], A.w_out_b.rearrange("(k p) n -> p k n", p=P)).then_inc(s_w[1], 16)
                sp.dma_start(pz[:, 2 * HA:], A.fill_latent[HB + 2 * HA:].rearrange("c p n -> p c n")).then_inc(s_pz, 16)
                sp.dma_start(S.x[:], A.xall[2:4].rearrange("t p d -> p t d")).then_inc(s_x, 16)
                sp.wait_ge(s_pa, 1)
                sp.dma_start(w[0][:], A.w_out.rearrange("(k p) n -> p k n", p=P)).then_inc(s_wo, 16)

            @block.gpsimd
            def _(g):
                g.tensor_tensor(sq[:], S.oa[:], S.oa[:], ALU.mult).then_inc(s_sq, 1)

            @block.scalar
            def _(act):
                for n, (r, first, width) in enumerate(((ra, 0, P), (rb, 4, 2 * P))):
                    act.wait_ge(s_ss, n + 1)
                    for b in range(4 if n == 0 else 2):
                        m = act.activation(r[:, 2 * b:2 * b + 2, :], bank[first + b][:], ACT.Ln, bias=C.eps[:],
                                           scale=1.0 / width)
                    m.then_inc(s_ln, 1)
                    act.wait_ge(s_ln, n + 1)
                    act.activation(r[:], r[:], ACT.Exp, scale=-0.5).then_inc(s_rt, 1)
                act.wait_ge(s_in, 32)
                act.activation(pz[:, 0:16, :], pz[:, 0:16, :], ACT.Silu).then_inc(s_sil, 1)
                act.wait_ge(s_pz, 16)
                act.activation(pz[:, 16:32, :], pz[:, 16:32, :], ACT.Sigmoid).then_inc(s_sil, 1)
                for t in range(2):
                    act.wait_ge(s_z, t + 1)
                    act.activation(junk[:], S.x[:, t, :], ACT.Square, accum_out=ss[:, t:t + 1]).then_inc(s_xs, 1)
                    act.wait_ge(s_xs, t + 1)
                act.wait_ge(s_n, 2)
                act.activation(rstd[:], ss[:], ACT.Sqrt).then_inc(s_n, 1)

            @block.tensor
            def _(pe):
                flat = lambda b: bank[b][:].rearrange("p a n -> p (a n)")
                pe.wait_ge(s_sq, 1)
                for b in range(4):
                    m = pe.matmul(flat(b), C.ones, sq[:, 2 * b:2 * b + 2, :].rearrange("p a n -> p (a n)"),
                                  start=True, stop=True)
                m.then_inc(s_ss, 1)
                pe.wait_ge(s_sqb, 1)
                for h in range(HB):
                    for e in range(2):
                        m = pe.matmul(bank[4 + h // 2][:, h % 2, :], C.ones, sqb[:, 2 * h + e, :],
                                      start=(e == 0), stop=(e == 1))
                m.then_inc(s_ss, 1)
                for n, src in enumerate((S.oa, S.ob)):
                    pe.wait_ge(s_w[n], 16)
                    pe.wait_ge(s_ya, n + 1)
                    if n == 1:
                        pe.wait_ge(s_rt, 2)
                    for o in range(KT):
                        for k in range(KT):
                            m = pe.matmul(bank[4 * n + o // 2][:, o % 2, :], w[n][:, k, o * P:(o + 1) * P],
                                          src[:, k, :], start=(k == 0), stop=(k == KT - 1))
                    m.then_inc(s_pa, 1)
                pe.wait_ge(s_wo, 16)
                pe.wait_ge(s_y, 1)
                for t in range(2):
                    for h in range(2):
                        for k in range(KT):
                            m = pe.matmul(flat(2 * t + h), y[:, k, t * P:(t + 1) * P],
                                          w[0][:, k, 512 * h:512 * h + 512], start=(k == 0), stop=(k == KT - 1))
                        m.then_inc(s_t, 1)
                for t in range(2):
                    pe.wait_ge(s_h, 1 + t)
                    for k in range(KT):
                        b = 4 + 2 * t + k // 4
                        m = pe.transpose(flat(b)[:, (k % 4) * P:(k % 4 + 1) * P], S.xn[:, t, k * P:(k + 1) * P], C.ident)
                    m.then_inc(s_tr, 1)

            @block.vector
            def _(v):
                link = Chain(v, s_v)
                v.tensor_tensor(sqb[:], S.ob[:], S.ob[:], ALU.mult).then_inc(s_sqb, 1)
                v.wait_ge(s_in, 32)
                v.wait_ge(s_rt, 1)
                v.wait_ge(s_sil, 1)
                link(v.scalar_tensor_tensor(S.oa[:], S.oa[:], gain[:, 0:1], ra[:], ALU.mult, ALU.mult))
                v.tensor_tensor(S.oa[:], S.oa[:], pz[:, 0:HA, :], ALU.mult).then_inc(s_ya, 1)
                v.wait_ge(s_rt, 2)
                for c in range(HA):
                    m = v.scalar_tensor_tensor(S.ob[:, c, :], S.ob[:, c, :], gain[:, 1 + c % 2:2 + c % 2],
                                               rb[:, c // 2, :], ALU.mult, ALU.mult)
                link(m)
                v.tensor_tensor(S.ob[:], S.ob[:], pz[:, HA:2 * HA, :], ALU.mult).then_inc(s_ya, 1)
                v.wait_ge(s_pa, 1)
                v.wait_ge(s_sil, 2)
                for b in range(4):
                    m = v.tensor_tensor(y[:, 2 * b:2 * b + 2, :], bank[b][:], pz[:, 16 + 2 * b:18 + 2 * b, :], ALU.mult)
                link(m)
                v.wait_ge(s_pa, 2)
                for b in range(4):
                    m = v.tensor_tensor(sq[:, 2 * b:2 * b + 2, :], bank[4 + b][:], pz[:, 24 + 2 * b:26 + 2 * b, :], ALU.mult)
                link(m)
                v.tensor_tensor(y[:], y[:], sq[:], ALU.add).then_inc(s_y, 1)
                v.wait_ge(s_x, 16)
                for t in range(2):
                    for h in range(2):
                        c = slice(512 * h, 512 * h + 512)
                        v.wait_ge(s_t, 2 * t + h + 1)
                        link(v.tensor_tensor(S.xn[:, t, c], bank[2 * t + h][:].rearrange("p a n -> p (a n)"),
                                             S.g1[:, c], ALU.mult))
                        m = v.tensor_tensor(S.x[:, t, c], S.x[:, t, c], S.xn[:, t, c], ALU.add)
                    m.then_inc(s_z, 1)
                v.wait_ge(s_xs, 2)
                v.tensor_scalar(ss[:], ss[:], 1.0 / D, EPS, ALU.mult, ALU.add).then_inc(s_n, 1)
                v.wait_ge(s_n, 1)
                v.reciprocal(ss[:], ss[:]).then_inc(s_n, 1)
                v.wait_ge(s_n, 3)
                for t in range(2):
                    v.tensor_scalar(S.xn[:, t, :], S.x[:, t, :], rstd[:, t:t + 1], None, ALU.mult).then_inc(s_h, 1)
                for t in range(2):
                    v.wait_ge(s_tr, t + 1)
                    for k in range(KT):
                        v.tensor_scalar(S.h2T[:, k, t * P:(t + 1) * P],
                                        bank[4 + 2 * t + k // 4][:].rearrange("p a n -> p (a n)")
                                        [:, (k % 4) * P:(k % 4 + 1) * P],
                                        S.a2[:, k:k + 1], S.b2[:, k:k + 1], ALU.mult, ALU.add)


def router_stage(nc, A, C, S):
    with Scope(nc, "router_") as s:
        wr = s.sb("wr", [P, KT, NE])
        br = s.sb("br", [P, NE])
        tri, iota = s.sb("tri", [P, P]), s.sb("iota", [P, NE])
        lg = s.sb("lg", [P, 2, NE])
        top = s.sb("top", [P, 2, 8])
        idx = s.sb("idx", [P, 2, 8], U32)
        idf = s.sb("idf", [P, 2, 8])
        ex, tot, nmax = s.sb("ex", [P, 2, TOPK]), s.sb("tot", [P, 2]), s.sb("nmax", [P, 2])
        one = s.sb("one", [P, 2, NE])
        most = s.sb("most", [P, 1])
        pl = s.ps("pl", [P, 2, NE])
        pp = s.ps("pp", [P, 3, NE])
        bias, back = s.sb("bias", [NE, 3 * D]), s.sb("back", [NE, 3 * D])
        s_in, s_l, s_v, s_e, s_p, s_bd, s_bg, s_small, s_db, s_gb = (s.sem(n) for n in (
            "in", "logits", "chain", "exped", "placed", "later_bias_in", "first_bias_in", "small_in", "later_parts", "first_parts"))

        def split_bias(eng, sem, cols):
            link = Chain(eng, sem)
            for n in range(3):
                part = S.bparts[n * NE:(n + 1) * NE, cols]
                link(eng.tensor_copy(part, bias[:, cols]))
                if n < 2:
                    link(eng.tensor_copy(back[:, cols], part))
                    link(eng.tensor_tensor(bias[:, cols], bias[:, cols], back[:, cols], ALU.subtract))

        with nc.Block() as block:
            @block.sync
            def _(sp):
                sp.dma_start(wr[:], A.w_router.rearrange("(k p) n -> p k n", p=P)).then_inc(s_in, 16)
                sp.dma_start(br[:], A.b_router.to_broadcast([P, NE])).then_inc(s_in, 16)
                sp.dma_start(tri[:], A.before_mask).then_inc(s_in, 16)
                sp.dma_start(iota[:], A.iota[:, 0:NE]).then_inc(s_in, 16)
                sp.dma_start(bias[:, 2 * D:3 * D], A.b_down).then_inc(s_bd, 16)
                sp.dma_start(bias[:, D:2 * D], A.b_gu[:, D:2 * D]).then_inc(s_bd, 16)
                sp.dma_start(bias[:, 0:D], A.b_gu[:, 0:D]).then_inc(s_bg, 16)
                sp.dma_start(S.pick[:], A.bias_pick).then_inc(s_small, 16)
                sp.dma_start(S.slot[:], A.iota[:, 0:SLOTS]).then_inc(s_small, 16)
                sp.dma_start(S.shift[:], A.pass_start).then_inc(s_small, 16)
                for n in range(EXPERT_RING):
                    load_expert_unit(sp, A, S, 0, n)
                sp.wait_ge(s_small, 48)

            @block.gpsimd
            def _(g):
                g.wait_ge(s_bg, 16)
                split_bias(g, s_gb, slice(0, D))
                g.memset(S.put[:], 0.0)
                g.memset(S.acc, 0.0)

            @block.tensor
            def _(pe):
                pe.wait_ge(s_in, 64)
                for t in range(2):
                    for k in range(KT):
                        m = pe.matmul(pl[:, t, :], S.h2T[:, k, t * P:(t + 1) * P], wr[:, k, :],
                                      start=(k == 0), stop=(k == KT - 1))
                m.then_inc(s_l, 1)
                pe.wait_ge(s_v, PLACE_AT)
                pe.matmul(pp[:, 0, :], tri[:], S.mask[:, 0, 0:NE], start=True, stop=True)
                pe.matmul(pp[:, 1, :], C.ones, S.mask[:, 0, 0:NE], start=True, stop=False)
                pe.matmul(pp[:, 1, :], tri[:], S.mask[:, 1, 0:NE], start=False, stop=True)
                pe.matmul(pp[:, 2, :], C.ones, S.mask[:, 0, 0:NE], start=True, stop=False)
                pe.matmul(pp[:, 2, :], C.ones, S.mask[:, 1, 0:NE], start=False, stop=True).then_inc(s_p, 1)

            @block.scalar
            def _(act):
                act.wait_ge(s_v, 12)
                for t in range(2):
                    m = act.activation(ex[:, t, :], top[:, t, 0:TOPK], ACT.Exp, bias=nmax[:, t:t + 1],
                                       accum_out=tot[:, t:t + 1])
                m.then_inc(s_e, 1)

            @block.vector
            def _(v):
                link = Chain(v, s_v)
                v.wait_ge(s_bd, 32)
                split_bias(v, s_db, slice(D, 3 * D))
                v.wait_ge(s_in, 64)
                v.wait_ge(s_l, 1)
                link(v.tensor_tensor(lg[:], pl[:], wide(br[:], 2), ALU.add))
                for t in range(2):
                    link(v.max(top[:, t, :], lg[:, t, :]))
                    link(v.max_index(idx[:, t, :], top[:, t, :], lg[:, t, :]))
                link(v.tensor_copy(idf[:], idx[:]))
                link(v.tensor_scalar(nmax[:], top[:, :, 0], -1.0, None, ALU.mult))
                for b in (S.wgt, S.mask, S.pos):
                    link(v.memset(b[:], 0.0))
                link(v.memset(one[:], 0.0))
                link(v.tensor_copy(S.posp[:], S.pos[:]))
                v.wait_ge(s_e, 1)
                link(v.reciprocal(tot[:], tot[:]))
                for t in range(2):
                    link(v.tensor_scalar(ex[:, t, :], ex[:, t, :], tot[:, t:t + 1], None, ALU.mult))
                for r in range(TOPK):
                    for t in range(2):
                        for dst, val in ((S.wgt, ex[:, t, r:r + 1]), (S.mask, 1.0)):
                            link(v.tensor_scalar(one[:, t, :], iota[:], idf[:, t, r:r + 1], val,
                                                 ALU.is_equal, ALU.mult))
                            link(v.tensor_tensor(dst[:, t, 0:NE], dst[:, t, 0:NE], one[:, t, :], ALU.add))
                assert link.n == PLACE_AT
                v.wait_ge(s_p, 1)
                link(v.tensor_copy(S.pos[:, :, 0:NE], pp[:, 0:2, :]))
                link(v.tensor_copy(S.posp[:], S.pos[:]))
                link(v.tensor_reduce(most[:], pp[:, 2, :], AX, ALU.max))
                link(v.tensor_copy(S.count[:], most[:]))


PLACE_AT = 12 + 1 + 2 + TOPK * 2 * 2 * 2


def load_expert_unit(sp, A, S, e, n):
    dst = S.ring[:, n, :]
    if n < KT:
        src = A.w_gu[bass.ds(e, 1), n * P:(n + 1) * P, :].rearrange("e p n -> (e p) n")
    else:
        m = n - KT
        src = A.w_down[bass.ds(e, 1), 2 * m * P:2 * (m + 1) * P, :].rearrange("e (a p) n -> p (e a) n", p=P)
        dst = dst.rearrange("p (a n) -> p a n", a=2)
    sp.dma_start(dst, src).then_inc(S.landed[n], 16)


def expert_stage(nc, A, C, S):
    RING = EXPERT_RING
    GU, DN = KT, 4
    PER = 2 * (GU + DN)
    PAIRS = NE // 2
    F = D
    with Scope(nc, "expert_") as s:
        bsel = s.sb("bsel", [3 * NE, 2 * SLOTS], BF16)
        iota, shift, pick, bparts = S.slot, S.shift, S.pick, S.bparts
        sel = s.sb("sel", [P, 2, 2, SLOTS])
        selw = s.sb("selw", [P, 2, 3, SLOTS])
        put = S.put[:].rearrange("p (e h x) n -> p e h (x n)", e=2, h=2)[:, :, :, 0:L]
        xT = S.work[:, 0:KT * P].rearrange("p (k n) -> p k n", k=KT)
        glu, lin, sig, hid, hidT, ysb = (S.work[:, KT * P + 512 * n:KT * P + 512 * (n + 1)] for n in range(6))
        hidT = hidT.rearrange("p (c n) -> p c n", c=4)
        gb, lb = s.ps("gb", [P, 512]), s.ps("lb", [P, 512])
        tb, yb = s.ps("tb", [P, 4, P]), s.ps("yb", [P, 512])
        xb = [s.ps(f"xb{n}", [P, 4, P]) for n in range(2)]
        ob = [s.ps(f"ob{n}", [P, 512]) for n in range(2)]
        landed, ring = S.landed, S.ring
        (s_used, s_sel, s_gx, s_xT, s_selw, s_pt, s_put, s_glu, s_lin, s_sig, s_hid, s_tr, s_trc,
         s_yc, s_sc, s_ac, s_bs, s_shift) = (s.sem(n) for n in (
             "unit_used", "picks", "gathered", "x_ready", "weights", "put_turned", "put_ready",
             "glu_done", "lin_done", "sig_done", "hid_done", "hid_turned", "hid_copied", "y_copied",
             "spread", "added", "bias_pick", "shifted"))

        def up_done(it, j):
            return it * PER + (RING + j * (GU + DN) + GU)

        def down_done(it, j):
            return it * PER + (RING + (j + 1) * (GU + DN))

        def passes(eng, body):
            count = eng.value_load(S.count[0:1, 0:1], min_val=0, max_val=L)
            with eng.Fori(0, L // SLOTS) as p:
                with eng.If(count > p * SLOTS):
                    body(p)

        with nc.Block() as block:
            @block.sync
            def _(sp):
                def load(e, it, j):
                    for n in range(GU + DN):
                        sp.wait_ge(s_used, it * PER + (j * RING + n + 1))
                        load_expert_unit(sp, A, S, e, n)

                def body(p):
                    with sp.Fori(0, PAIRS - 1) as i:
                        load(i * 2 + 1, p * PAIRS + i, 1)
                        load(i * 2 + 2, p * PAIRS + i, 2)
                    load(NE - 1, p * PAIRS, 2 * PAIRS - 1)
                    with sp.If(count > p * SLOTS + SLOTS):
                        load(0, p * PAIRS, 2 * PAIRS)

                count = sp.value_load(S.count[0:1, 0:1], min_val=0, max_val=L)
                with sp.Fori(0, L // SLOTS) as p:
                    with sp.If(count > p * SLOTS):
                        body(p)

            @block.gpsimd
            def _(g):
                g.sem_inc(s_used, RING)
                g.sem_inc(s_ac, 2)

                def body(p):
                    with g.Fori(0, PAIRS) as i:
                        it = p * PAIRS + i
                        for j in range(2):
                            g.wait_ge(s_used, it * PER + (1 if j == 0 else RING))
                            g.tensor_copy(bsel[:, j * SLOTS:(j + 1) * SLOTS],
                                          pick[:, bass.ds(i * (2 * SLOTS) + j * SLOTS, SLOTS)]).then_inc(s_bs, 1)
                passes(g, body)

            @block.vector
            def _(v):
                def picks(e):
                    for t in range(2):
                        for j in range(2):
                            m = v.tensor_scalar(sel[:, t, j, :], iota[:], S.posp[:, t, bass.ds(e + j, 1)],
                                                S.mask[:, t, bass.ds(e + j, 1)], ALU.is_equal, ALU.mult)
                    m.then_inc(s_sel, 1)

                def body(p):
                    v.tensor_scalar(S.posp[:], S.pos[:], shift[:, bass.ds(p, 1)], None, ALU.subtract).then_inc(s_shift, 1)
                    v.wait_ge(s_shift, p + 1)
                    picks(0)
                    with v.Fori(0, PAIRS) as i:
                        it = p * PAIRS + i
                        gth = it + p
                        for t in range(2):
                            for c in range(3):
                                e = i * 2 + (c % 2)
                                m = v.tensor_scalar(selw[:, t, c, :], iota[:], S.posp[:, t, bass.ds(e, 1)],
                                                    S.wgt[:, t, bass.ds(e, 1)], ALU.is_equal, ALU.mult)
                        m.then_inc(s_selw, 1)
                        v.wait_ge(s_gx, gth + 1)
                        picks(i * 2 + 2)
                        for j in range(2):
                            v.wait_ge(s_used, up_done(it, j))
                            v.tensor_scalar(glu, gb[:], LIMIT, None, ALU.min).then_inc(s_glu, 1)
                            v.tensor_scalar(lin, lb[:], LIMIT, -LIMIT, ALU.min, ALU.max).then_inc(s_lin, 1)
                            v.wait_ge(s_glu, it * 2 + (j + 1))
                            v.wait_ge(s_lin, it * 4 + (2 * j + 1))
                            v.scalar_tensor_tensor(lin, lin, 1.0, glu, ALU.add, ALU.mult).then_inc(s_lin, 1)
                            v.wait_ge(s_lin, it * 4 + (2 * j + 2))
                            v.wait_ge(s_sig, it * 2 + (j + 1))
                            v.tensor_tensor(hid, lin, sig, ALU.mult).then_inc(s_hid, 1)
                        for j in range(2):
                            v.wait_ge(s_ac, it * 8 + (4 * j + 2))
                            for q in range(4):
                                v.wait_ge(s_sc, it * 8 + (4 * j + q + 1))
                                a = S.acc[:, q // 2, 512 * (q % 2):512 * (q % 2) + 512]
                                v.tensor_tensor(a, a, ob[q % 2][:], ALU.add).then_inc(s_ac, 1)
                passes(v, body)

            @block.scalar
            def _(act):
                def take():
                    for k in range(KT):
                        m = act.activation(xT[:, k, :], xb[k // 4][:, k % 4, :], ACT.Identity,
                                           scale=S.a2[:, k:k + 1], bias=S.b2[:, k:k + 1])
                    m.then_inc(s_xT, 1)

                def body(p):
                    act.wait_ge(s_gx, p * (PAIRS + 1) + 1)
                    take()
                    with act.Fori(0, PAIRS) as i:
                        it = p * PAIRS + i
                        gth = it + p
                        act.wait_ge(s_pt, it + 1)
                        for w in range(2):
                            lo, hi = w, 1 - w
                            act.activation(put[0:SLOTS, lo, 0, :].rearrange("p (t n) -> p t n", n=P),
                                           tb[0:SLOTS, 2 * w:2 * w + 2, :], ACT.Copy)
                            m = act.activation(put[SLOTS:P, hi, 1, :].rearrange("p (t n) -> p t n", n=P),
                                               tb[SLOTS:P, 2 * w:2 * w + 2, :], ACT.Copy)
                        m.then_inc(s_put, 1)
                        for j in range(2):
                            act.wait_ge(s_glu, it * 2 + (j + 1))
                            act.activation(sig, glu, ACT.Sigmoid, scale=ALPHA).then_inc(s_sig, 1)
                            if j == 1:
                                act.wait_ge(s_gx, gth + 2)
                                take()
                            act.wait_ge(s_tr, it * 2 + (j + 1))
                            act.activation(hidT, tb[:], ACT.Copy).then_inc(s_trc, 1)
                            act.wait_ge(s_used, down_done(it, j))
                            act.activation(ysb, yb[:], ACT.Copy).then_inc(s_yc, 1)
                passes(act, body)

            @block.tensor
            def _(pe):
                halves = (slice(0, SLOTS), slice(SLOTS, P))

                def spread(it, j):
                    pe.wait_ge(s_yc, it * 2 + (j + 1))
                    for q in range(4):
                        pe.wait_ge(s_ac, it * 8 + (4 * j + q + 1))
                        t, h = q // 2, q % 2
                        pe.matmul(ob[h][:], put[:, j, h, t * P:(t + 1) * P], ysb,
                                  start=True, stop=True).then_inc(s_sc, 1)

                def gather():
                    for k in range(KT):
                        for t in range(2):
                            m = pe.matmul(xb[k // 4][:, k % 4, :], S.xn[:, t, k * P:(k + 1) * P],
                                          sel[:, t].rearrange("p j n -> p (j n)"), start=(t == 0), stop=(t == 1))
                    m.then_inc(s_gx, 1)

                def body(p):
                    pe.wait_ge(s_sel, p * (PAIRS + 1) + 1)
                    gather()
                    with pe.Fori(0, PAIRS) as i:
                        it = p * PAIRS + i
                        gth = it + p
                        pe.wait_ge(s_xT, gth + 1)
                        u = 0
                        for j in range(2):
                            x = slice(j * SLOTS, (j + 1) * SLOTS)
                            pe.wait_ge(s_bs, it * 2 + (j + 1))
                            for b, c0 in ((gb, 0), (lb, F)):
                                for h in range(2):
                                    pe.matmul(b[halves[h], :], bsel[:, x], bparts[:, c0 + 512 * h:c0 + 512 * h + 512],
                                              start=True, stop=False)
                            for k in range(GU):
                                z = u % RING
                                pe.wait_ge(landed[z], it * 32 + 16 * (u // RING + 1))
                                for b, c0 in ((gb, 0), (lb, F)):
                                    for h in range(2):
                                        m = pe.matmul(b[halves[h], :], xT[:, k, x],
                                                      ring[:, z, c0 + 512 * h:c0 + 512 * h + 512],
                                                      start=False, stop=(k == GU - 1))
                                m.then_inc(s_used, 1)
                                u += 1
                            if j == 0:
                                pe.wait_ge(s_selw, it + 1)
                                for w in range(2):
                                    for t in range(2):
                                        m = pe.transpose(tb[:, 2 * w + t, :],
                                                         selw[:, t, w:w + 2, :].rearrange("p j n -> p (j n)"), C.ident)
                                m.then_inc(s_pt, 1)
                                pe.wait_ge(s_sel, gth + 2)
                                gather()
                                pe.wait_ge(s_put, it + 1)
                            else:
                                spread(it, 0)
                            pe.wait_ge(s_hid, it * 2 + (j + 1))
                            for c in range(4):
                                m = pe.transpose(tb[:, c, :], hid[:, c * P:(c + 1) * P], C.ident)
                            m.then_inc(s_tr, 1)
                            for h in range(2):
                                pe.matmul(yb[halves[h], :], bsel[:, x],
                                          bparts[:, 2 * F + 512 * h:2 * F + 512 * h + 512], start=True, stop=False)
                            pe.wait_ge(s_trc, it * 2 + (j + 1))
                            for n in range(DN):
                                z = u % RING
                                pe.wait_ge(landed[z], it * 32 + 16 * (u // RING + 1))
                                for a in range(2):
                                    f = 2 * n + a
                                    c, hh = f % 4, f // 4
                                    for h in range(2):
                                        m = pe.matmul(yb[halves[h], :], hidT[:, c, hh * SLOTS:(hh + 1) * SLOTS],
                                                      ring[:, z, a * F + 512 * h:a * F + 512 * h + 512],
                                                      start=False, stop=(f == 7))
                                m.then_inc(s_used, 1)
                                u += 1
                        spread(it, 1)
                passes(pe, body)


def close_first_stage(nc, A, C, S):
    with Scope(nc, "close_") as s:
        gf = s.sb("gf", [P, D])
        junk = s.sb("junk", [P, D])
        ss, rstd = s.sb("ss", [P, 2]), s.sb("rstd", [P, 2])
        s_in, s_v, s_a = s.sem("in"), s.sem("chain"), s.sem("act")
        with nc.Block() as block:
            @block.sync
            def _(sp):
                sp.dma_start(gf[:], A.final_norm_g.to_broadcast([P, D])).then_inc(s_in, 16)

            @block.scalar
            def _(act):
                for t in range(2):
                    act.wait_ge(s_v, 3 + t)
                    act.activation(junk[:], S.x[:, t, :], ACT.Square, accum_out=ss[:, t:t + 1]).then_inc(s_a, 1)
                    act.wait_ge(s_a, t + 1)
                act.wait_ge(s_v, 6)
                act.activation(rstd[:], ss[:], ACT.Sqrt).then_inc(s_a, 1)

            @block.vector
            def _(v):
                link = Chain(v, s_v)
                for t in range(2):
                    link(v.tensor_tensor(S.acc[:, t, :], S.acc[:, t, :], S.g2, ALU.mult))
                for t in range(2):
                    link(v.tensor_tensor(S.x[:, t, :], S.x[:, t, :], S.acc[:, t, :], ALU.add))
                v.wait_ge(s_a, 2)
                link(v.tensor_scalar(ss[:], ss[:], 1.0 / D, EPS, ALU.mult, ALU.add))
                link(v.reciprocal(ss[:], ss[:]))
                v.wait_ge(s_a, 3)
                v.wait_ge(s_in, 16)
                for t in range(2):
                    v.scalar_tensor_tensor(S.g[:, t, :], S.x[:, t, :], rstd[:, t:t + 1], gf[:], ALU.mult, ALU.mult)


H2 = 8
HD = 64
NOPE, ROPE = 64, 32
QL, KVL = 384, 256
WA = H2 * HD
FF = 2816
FT = FF // P
IN2 = 3 * WA + QL + KVL + ROPE


def attend_stage(nc, A, C, S):
    HQ = NOPE + ROPE
    with Scope(nc, "attend_") as s:
        proj = s.sb("proj", [P, 2, IN2])
        gcol = s.sb("gcol", [P, KT + 3 + 2 + KT])
        s_in, s_w = s.sem("in"), s.sems("w_in", 3)
        stat, rstd, junk = s.sb("stat", [P, 12]), s.sb("rstd", [P, 12]), s.sb("junk", [P, D])
        COLS = [(c, min(512, IN2 - c)) for c in range(0, IN2, 512)]
        with Scope(nc, "attend_in_") as q:
            wi = q.sb("wi", [P, 3, KT, 512])
            xn, hT = q.sb("xn", [P, 2, D]), q.sb("hT", [P, KT, L])
            pt = [q.ps(f"pt{n}", [P, 4, P]) for n in range(4)]
            pj = [q.ps(f"pj{n}", [P, 512]) for n in range(4)]
            s_a, s_v, s_t, s_h, s_p, s_c = (q.sem(n) for n in ("act", "chain", "turned", "hT_done", "projected", "copied"))
            with nc.Block() as block:
                @block.sync
                def _(sp):
                    sp.dma_start(gcol[:], A.gains2_col).then_inc(s_in, 16)
                    for u, (c, n) in enumerate(COLS):
                        if u >= 3:
                            sp.wait_ge(s_p, 2 * (u - 2))
                        sp.dma_start(wi[:, u % 3, :, 0:n], A.w_in_2[:, c:c + n]
                                     .rearrange("(k p) n -> p k n", p=P)).then_inc(s_w[u % 3], 16)

                @block.scalar
                def _(act):
                    for t in range(2):
                        act.activation(junk[:], S.x[:, t, :], ACT.Square, accum_out=stat[:, t:t + 1]).then_inc(s_a, 1)
                        act.wait_ge(s_a, t + 1)
                    act.wait_ge(s_v, 2)
                    act.activation(rstd[:, 0:2], stat[:, 0:2], ACT.Sqrt).then_inc(s_a, 1)
                    for u, (c, n) in enumerate(COLS):
                        for t in range(2):
                            b = 2 * u + t
                            act.wait_ge(s_p, b + 1)
                            act.activation(proj[:, t, c:c + n], pj[b % 4][:, 0:n], ACT.Copy).then_inc(s_c, 1)

                @block.vector
                def _(v):
                    link = Chain(v, s_v)
                    v.wait_ge(s_a, 2)
                    link(v.tensor_scalar(stat[:, 0:2], stat[:, 0:2], 1.0 / D, EPS, ALU.mult, ALU.add))
                    link(v.reciprocal(stat[:, 0:2], stat[:, 0:2]))
                    v.wait_ge(s_a, 3)
                    for t in range(2):
                        link(v.tensor_scalar(xn[:, t, :], S.x[:, t, :], rstd[:, t:t + 1], None, ALU.mult))
                    v.wait_ge(s_in, 16)
                    for b in range(4):
                        t, h = b // 2, b % 2
                        v.wait_ge(s_t, b + 1)
                        for k in range(4):
                            kk = 4 * h + k
                            m = v.tensor_scalar(hT[:, kk, t * P:(t + 1) * P], pt[b][:, k, :], gcol[:, kk:kk + 1], None,
                                                ALU.mult)
                        m.then_inc(s_h, 1)

                @block.tensor
                def _(pe):
                    for b in range(4):
                        t, h = b // 2, b % 2
                        pe.wait_ge(s_v, 3 + t)
                        for k in range(4):
                            m = pe.transpose(pt[b][:, k, :], xn[:, t, (4 * h + k) * P:(4 * h + k + 1) * P], C.ident)
                        m.then_inc(s_t, 1)
                    pe.wait_ge(s_h, 4)
                    for u, (c, n) in enumerate(COLS):
                        pe.wait_ge(s_w[u % 3], 16 * (u // 3 + 1))
                        for t in range(2):
                            b = 2 * u + t
                            if b >= 4:
                                pe.wait_ge(s_c, b - 3)
                            for k in range(KT):
                                m = pe.matmul(pj[b % 4][:, 0:n], hT[:, k, t * P:(t + 1) * P], wi[:, u % 3, k, 0:n],
                                              start=(k == 0), stop=(k == KT - 1))
                            m.then_inc(s_p, 1)

        qz = s.sb("qz", [P, H2, L])
        ka = s.sb("ka", [P, H2 // 2, L])
        qb, kb = s.sb("qb", [HQ, H2, L]), s.sb("kb", [HQ, H2, L])
        vb = s.sb("vb", [P, 2, H2, HD])
        bias = s.sb("bias", [P, H2, 2, L])
        wo = s.sb("wo", [P, KT, D])
        gpost = s.sb("gpost", [P, D])
        s_wo = s.sem("wo_in")
        with Scope(nc, "attend_latent_") as q:
            cn = q.sb("cn", [P, 2, QL + KVL])
            cT = q.sb("cT", [P, 5, L])
            wuq, wukv = q.sb("wuq", [P, 3, H2 * HQ]), q.sb("wukv", [P, 2, 2 * WA])
            rope = q.sb("rope", [P, 2, 2, ROPE // 2])
            qc, kc = q.sb("qc", [P, 2, H2, HQ]), q.sb("kc", [P, 2, H2, HQ])
            t1, t2 = q.sb("t1", [P, H2, ROPE // 2]), q.sb("t2", [P, H2, ROPE // 2])
            r1 = q.sb("r1", [P, 4, ROPE // 2])
            bank = [q.ps(f"bank{n}", [P, 4, P]) for n in range(8)]
            s_in, s_a, s_v, s_t, s_u, s_e, s_d, s_z, s_q, s_te = (q.sem(n) for n in (
                "in", "act", "chain", "turned", "up_done", "copied", "dve", "zeroed", "q_turned", "q_copied"))
            flat = lambda b: bank[b][:].rearrange("p a n -> p (a n)")
            with nc.Block() as block:
                @block.sync
                def _(sp):
                    sp.dma_start(wuq[:], A.w_uq.rearrange("(k p) n -> p k n", p=P)).then_inc(s_in, 16)
                    sp.dma_start(wukv[:], A.w_ukv.rearrange("(k p) n -> p k n", p=P)).then_inc(s_in, 16)
                    sp.dma_start(rope[:], A.rope).then_inc(s_in, 16)
                    sp.dma_start(bias[:], A.key_bias).then_inc(s_wo, 16)
                    sp.dma_start(wo[:], A.w_o.rearrange("(k p) n -> p k n", p=P)).then_inc(s_wo, 16)
                    sp.dma_start(gpost[:], A.norm_mix_post.to_broadcast([P, D])).then_inc(s_wo, 16)

                @block.gpsimd
                def _(g):
                    g.memset(qz[:], 0.0).then_inc(s_z, 1)

                @block.scalar
                def _(act):
                    for t in range(2):
                        act.activation(junk[:, 0:QL], proj[:, t, 3 * WA:3 * WA + QL], ACT.Square,
                                       accum_out=stat[:, 2 + t:3 + t]).then_inc(s_a, 1)
                        act.wait_ge(s_a, 2 * t + 1)
                        act.activation(junk[:, 0:KVL], proj[:, t, 3 * WA + QL:3 * WA + QL + KVL], ACT.Square,
                                       accum_out=stat[:, 4 + t:5 + t]).then_inc(s_a, 1)
                        act.wait_ge(s_a, 2 * t + 2)
                    act.wait_ge(s_v, 3)
                    act.activation(rstd[:, 2:6], stat[:, 2:6], ACT.Sqrt).then_inc(s_a, 1)
                    act.wait_ge(s_z, 1)
                    for t in range(2):
                        act.wait_ge(s_q, 2 * t + 1)
                        for c in range(4):
                            for r in range(2):
                                m = act.activation(qz[r * HD:(r + 1) * HD, 2 * c + r, t * P:(t + 1) * P],
                                                   bank[2 * t][r * HD:(r + 1) * HD, c, :], ACT.Copy)
                        m.then_inc(s_te, 1)
                        act.wait_ge(s_q, 2 * t + 2)
                        act.activation(ka[:, :, t * P:(t + 1) * P], bank[2 * t + 1][:], ACT.Copy).then_inc(s_te, 1)
                    for n in range(8):
                        x, t, g = n // 4, (n // 2) % 2, n % 2
                        act.wait_ge(s_q, 4 + n + 1)
                        act.activation((qb, kb)[x][:, 4 * g:4 * g + 4, t * P:(t + 1) * P], bank[n][0:HQ, :, :],
                                       ACT.Copy).then_inc(s_te, 1)

                @block.vector
                def _(v):
                    link = Chain(v, s_v)
                    v.wait_ge(s_a, 4)
                    link(v.tensor_scalar(stat[:, 2:4], stat[:, 2:4], 1.0 / QL, EPS, ALU.mult, ALU.add))
                    link(v.tensor_scalar(stat[:, 4:6], stat[:, 4:6], 1.0 / KVL, EPS, ALU.mult, ALU.add))
                    link(v.reciprocal(stat[:, 2:6], stat[:, 2:6]))
                    v.wait_ge(s_a, 5)
                    for t in range(2):
                        v.tensor_scalar(cn[:, t, 0:QL], proj[:, t, 3 * WA:3 * WA + QL], rstd[:, 2 + t:3 + t], None, ALU.mult)
                        link(v.tensor_scalar(cn[:, t, QL:], proj[:, t, 3 * WA + QL:3 * WA + QL + KVL],
                                             rstd[:, 4 + t:5 + t], None, ALU.mult))
                    for k in range(5):
                        v.wait_ge(s_t, k + 1)
                        m = v.tensor_scalar(cT[:, k, :], flat(4 + k % 4)[:, 0:L], gcol[:, KT + k:KT + k + 1], None, ALU.mult)
                        link(m)
                    v.wait_ge(s_in, 48)
                    for t in range(2):
                        cos, sin = rope[:, 0, t, :], rope[:, 1, t, :]
                        v.wait_ge(s_u, 2 * t + 1)
                        for g in range(2):
                            src = flat(4 * t + g)[:, 0:4 * HQ].rearrange("p (h n) -> p h n", n=HQ)
                            m = v.tensor_copy(qc[:, t, 4 * g:4 * g + 4, :], src)
                        link(m)
                        v.wait_ge(s_u, 2 * t + 2)
                        for g in range(2):
                            src = flat(4 * t + 2 + g).rearrange("p (h n) -> p h n", n=NOPE + HD)
                            v.tensor_copy(kc[:, t, 4 * g:4 * g + 4, 0:NOPE], src[:, :, 0:NOPE])
                            m = v.tensor_copy(vb[:, t, 4 * g:4 * g + 4, :], src[:, :, NOPE:])
                        link(m)

                        def turn(dst, x1, x2, c, s_, a, b):
                            h = ROPE // 2
                            v.tensor_tensor(a, x2, s_, ALU.mult)
                            link(v.tensor_tensor(b, x1, s_, ALU.mult))
                            v.tensor_tensor(dst[..., 0:h], x1, c, ALU.mult)
                            link(v.tensor_tensor(dst[..., h:], x2, c, ALU.mult))
                            v.tensor_tensor(dst[..., 0:h], dst[..., 0:h], a, ALU.subtract)
                            link(v.tensor_tensor(dst[..., h:], dst[..., h:], b, ALU.add))

                        h = ROPE // 2
                        kr = proj[:, t, IN2 - ROPE:]
                        kd = r1[:, 2:4, :].rearrange("p a n -> p (a n)")
                        turn(kd, kr[:, 0:h], kr[:, h:], cos, sin, r1[:, 0, :], r1[:, 1, :])
                        link(v.tensor_copy(kc[:, t, :, NOPE:], wide(kd, H2)))
                        x1, x2 = qc[:, t, :, NOPE:NOPE + h], qc[:, t, :, NOPE + h:]
                        cw, sw = wide(cos, H2), wide(sin, H2)
                        v.tensor_tensor(t1[:], x2, sw, ALU.mult)
                        link(v.tensor_tensor(t2[:], x1, sw, ALU.mult))
                        v.tensor_tensor(x1, x1, cw, ALU.mult)
                        link(v.tensor_tensor(x2, x2, cw, ALU.mult))
                        v.tensor_tensor(x1, x1, t1[:], ALU.subtract)
                        link(v.tensor_tensor(x2, x2, t2[:], ALU.add))
                        v.sem_inc(s_d, 1)
                    assert link.n == 10 + 2 * 9

                @block.tensor
                def _(pe):
                    for t in range(2):
                        for x in range(2):
                            for c in range(4):
                                m = pe.transpose(bank[2 * t + x][:, c, :],
                                                 proj[:, t, x * WA + c * P:x * WA + (c + 1) * P], C.ident)
                            m.then_inc(s_q, 1)
                    pe.wait_ge(s_v, 5)
                    for k in range(5):
                        if k == 4:
                            pe.wait_ge(s_v, 6)
                        for t in range(2):
                            m = pe.transpose(bank[4 + k % 4][:, t, :], cn[:, t, k * P:(k + 1) * P], C.ident)
                        m.then_inc(s_t, 1)
                    pe.wait_ge(s_v, 10)
                    pe.wait_ge(s_te, 4)
                    pe.wait_ge(s_in, 48)
                    for t in range(2):
                        for g in range(2):
                            for k in range(3):
                                m = pe.matmul(flat(4 * t + g)[:, 0:4 * HQ], cT[:, k, t * P:(t + 1) * P],
                                              wuq[:, k, 4 * HQ * g:4 * HQ * (g + 1)], start=(k == 0), stop=(k == 2))
                        m.then_inc(s_u, 1)
                        for g in range(2):
                            for k in range(2):
                                m = pe.matmul(flat(4 * t + 2 + g), cT[:, 3 + k, t * P:(t + 1) * P],
                                              wukv[:, k, 512 * g:512 * (g + 1)], start=(k == 0), stop=(k == 1))
                        m.then_inc(s_u, 1)
                    pe.wait_ge(s_v, 28)
                    for n in range(8):
                        x, t, g = n // 4, (n // 2) % 2, n % 2
                        for h in range(4):
                            m = pe.transpose(bank[n][0:HQ, h, :], (qc, kc)[x][:, t, 4 * g + h, :], C.ident)
                        m.then_inc(s_q, 1)

        sc = s.sb("sc", [P, 2, 2, L])
        mx = s.sb("mx", [P, 2, 2])
        pr = s.sb("pr", [P, 2, 2, L])
        prT = s.sb("prT", [P, 2, 4, P])
        rs = s.sb("rs", [P, 2, 2, H2])
        y = s.sb("y", [P, 2, 2, WA])
        yT = s.sb("yT", [P, KT, L])
        with Scope(nc, "attend_soft_") as q:
            pS = [q.ps(f"pS{n}", [P, 2, L]) for n in range(2)]
            pT = [q.ps(f"pT{n}", [P, 4, P]) for n in range(2)]
            pO = [q.ps(f"pO{n}", [P, H2, HD]) for n in range(2)]
            pY = [q.ps(f"pY{n}", [P, 512]) for n in range(2)]
            (s_s, s_b, s_m, s_e, s_pt, s_pc, s_o, s_r, s_y, s_a, s_v, s_t, s_tc, s_f, s_x) = (q.sem(n) for n in (
                "scores", "biased", "negmax", "exped", "turned", "turned_copied", "o_done", "recip", "y_done",
                "act", "chain", "y_turned", "y_copied", "out_done", "x_done"))
            STEPS = [(a, t, c) for a in range(2) for t in range(2) for c in range(H2 // 2)]
            with nc.Block() as block:
                @block.tensor
                def _(pe):
                    def scores(n):
                        a, t, c = STEPS[n]
                        if n >= 2:
                            pe.wait_ge(s_e, n - 1)
                        for r in range(2):
                            h = 2 * c + r
                            if a == 0:
                                m = pe.matmul(pS[n % 2][:, r, :], qz[:, h, t * P:(t + 1) * P], ka[:, c, :],
                                              start=True, stop=True)
                            else:
                                m = pe.matmul(pS[n % 2][:, r, :], qb[:, h, t * P:(t + 1) * P], kb[:, h, :],
                                              start=True, stop=True)
                        m.then_inc(s_s, 1)

                    def turn(n):
                        pe.wait_ge(s_e, n + 1)
                        if n >= 2:
                            pe.wait_ge(s_pc, n - 1)
                        for r in range(2):
                            for k in range(2):
                                m = pe.transpose(pT[n % 2][:, 2 * r + k, :], pr[:, n % 2, r, k * P:(k + 1) * P], C.ident)
                        m.then_inc(s_pt, 1)

                    def values(n):
                        a, t, c = STEPS[n]
                        pe.wait_ge(s_pc, n + 1)
                        if c == 0 and n >= 8:
                            pe.wait_ge(s_y, n // 4 - 1)
                        for r in range(2):
                            h = 2 * c + r
                            for k in range(2):
                                val = proj[:, k, 2 * WA + h * HD:2 * WA + (h + 1) * HD] if a == 0 else vb[:, k, h, :]
                                m = pe.matmul(pO[(n // 4) % 2][:, h, :], prT[:, n % 2, 2 * r + k, :], val,
                                              start=(k == 0), stop=(k == 1))
                        m.then_inc(s_o, 1)

                    pe.wait_ge(s_wo, 48)
                    for n in range(len(STEPS) + 2):
                        if n < len(STEPS):
                            scores(n)
                        if 1 <= n <= len(STEPS):
                            turn(n - 1)
                        if n >= 2:
                            values(n - 2)
                    for b in range(4):
                        t, a = b // 2, b % 2
                        bk = pT[b % 2]
                        pe.wait_ge(s_v, 3 + t)
                        if b >= 2:
                            pe.wait_ge(s_tc, b - 1)
                        for k in range(4):
                            m = pe.transpose(bk[:, k, :], y[:, t, a, k * P:(k + 1) * P], C.ident)
                        m.then_inc(s_t, 1)
                    pe.wait_ge(s_tc, 4)
                    for b in range(4):
                        t, h = b // 2, b % 2
                        if b >= 2:
                            pe.wait_ge(s_f, b - 1)
                        for k in range(KT):
                            m = pe.matmul(pY[h][:], yT[:, k, t * P:(t + 1) * P], wo[:, k, 512 * h:512 * h + 512],
                                          start=(k == 0), stop=(k == KT - 1))
                        m.then_inc(s_x, 1)

                def copy_turned(act, n):
                    act.wait_ge(s_pt, n + 1)
                    if n >= 2:
                        act.wait_ge(s_o, n - 1)
                    act.activation(prT[:, n % 2], pT[n % 2][:], ACT.Copy).then_inc(s_pc, 1)

                @block.scalar
                def _(act):
                    for n, (a, t, c) in enumerate(STEPS):
                        act.wait_ge(s_m, n + 1)
                        if n >= 2:
                            act.wait_ge(s_pt, n - 1)
                        scale = 1.0 if a == 0 else HQ ** -0.5
                        src = sc[:, n % 2] if a == 0 else pS[n % 2][:]
                        for r in range(2):
                            m = act.activation(pr[:, n % 2, r, :], src[:, r, :], ACT.Exp, bias=mx[:, n % 2, r:r + 1],
                                               scale=scale, accum_out=rs[:, a, t, 2 * c + r:2 * c + r + 1])
                        m.then_inc(s_e, 1)
                        if n >= 1:
                            copy_turned(act, n - 1)
                    copy_turned(act, len(STEPS) - 1)
                    for t in range(2):
                        for a in range(2):
                            act.wait_ge(s_y, 4)
                            act.activation(junk[:, 0:WA], y[:, t, a, :], ACT.Square,
                                           accum_out=stat[:, 6 + 2 * t + a:7 + 2 * t + a]).then_inc(s_a, 1)
                            act.wait_ge(s_a, 2 * t + a + 1)
                    act.wait_ge(s_v, 2)
                    act.activation(rstd[:, 6:10], stat[:, 6:10], ACT.Sqrt).then_inc(s_a, 1)
                    for t in range(2):
                        for h in range(2):
                            b = 2 * t + h
                            act.wait_ge(s_x, b + 1)
                            act.activation(y[:, t, h, :], pY[h][:], ACT.Copy).then_inc(s_f, 1)
                            act.wait_ge(s_f, b + 1)
                        act.activation(junk[:], y[:, t].rearrange("p a n -> p (a n)"), ACT.Square,
                                       accum_out=stat[:, 10 + t:11 + t]).then_inc(s_a, 1)
                        act.wait_ge(s_a, 6 + t)
                    act.wait_ge(s_v, 6)
                    act.activation(rstd[:, 10:12], stat[:, 10:12], ACT.Sqrt).then_inc(s_a, 1)

                @block.vector
                def _(v):
                    link = Chain(v, s_v)
                    v.wait_ge(s_wo, 48)

                    def take(g):
                        a, t = g // 2, g % 2
                        v.wait_ge(s_o, 4 * g + 4)
                        v.reciprocal(rs[:, a, t, :], rs[:, a, t, :]).then_inc(s_r, 1)
                        v.wait_ge(s_r, g + 1)
                        v.tensor_tensor(y[:, t, a, :].rearrange("p (h n) -> p h n", n=HD), pO[g % 2][:],
                                        deep(rs[:, a, t, :], HD), ALU.mult).then_inc(s_y, 1)

                    nb = 0
                    for n, (a, t, c) in enumerate(STEPS):
                        v.wait_ge(s_s, n + 1)
                        if n >= 2:
                            v.wait_ge(s_e, n - 1)
                        if a == 0:
                            v.scalar_tensor_tensor(sc[:, n % 2], pS[n % 2][:], HD ** -0.5, bias[:, 2 * c:2 * c + 2, t, :],
                                                   ALU.mult, ALU.add).then_inc(s_b, 1)
                            nb += 1
                            v.wait_ge(s_b, nb)
                            src, neg = sc[:, n % 2], -1.0
                        else:
                            src, neg = pS[n % 2][:], -HQ ** -0.5
                        v.tensor_reduce(mx[:, n % 2, :], src, AX, ALU.max).then_inc(s_b, 1)
                        nb += 1
                        v.wait_ge(s_b, nb)
                        v.tensor_scalar(mx[:, n % 2, :], mx[:, n % 2, :], neg, None, ALU.mult).then_inc(s_m, 1)
                        if n % 4 == 3 and n >= 7:
                            take(n // 4 - 1)
                    take(3)
                    v.wait_ge(s_a, 4)
                    link(v.tensor_scalar(stat[:, 6:10], stat[:, 6:10], 1.0 / WA, EPS, ALU.mult, ALU.add))
                    link(v.reciprocal(stat[:, 6:10], stat[:, 6:10]))
                    v.wait_ge(s_a, 5)
                    for t in range(2):
                        for a in range(2):
                            m = v.tensor_scalar(y[:, t, a, :], y[:, t, a, :], rstd[:, 6 + 2 * t + a:7 + 2 * t + a], None,
                                                ALU.mult)
                        link(m)
                    for b in range(4):
                        t, a = b // 2, b % 2
                        v.wait_ge(s_t, b + 1)
                        for k in range(4):
                            kk = 4 * a + k
                            m = v.tensor_scalar(yT[:, kk, t * P:(t + 1) * P], pT[b % 2][:, k, :],
                                                gcol[:, KT + 5 + kk:KT + 6 + kk], None, ALU.mult)
                        m.then_inc(s_tc, 1)
                    v.wait_ge(s_a, 7)
                    link(v.tensor_scalar(stat[:, 10:12], stat[:, 10:12], 1.0 / D, EPS, ALU.mult, ALU.add))
                    link(v.reciprocal(stat[:, 10:12], stat[:, 10:12]))
                    v.wait_ge(s_a, 8)
                    for t in range(2):
                        row = y[:, t].rearrange("p a n -> p (a n)")
                        link(v.scalar_tensor_tensor(row, row, rstd[:, 10 + t:11 + t], gpost[:], ALU.mult, ALU.mult))
                        v.tensor_tensor(S.x[:, t, :], S.x[:, t, :], row, ALU.add)


def feed_forward_stage(nc, A, C, S, out):
    with Scope(nc, "ffn_") as s:
        xn, hT = s.sb("xn", [P, 2, D]), s.sb("hT", [P, KT, L])
        gcol, gpost = s.sb("gcol", [P, KT]), s.sb("gpost", [P, D])
        stat, rstd, junk = s.sb("stat", [P, 4]), s.sb("rstd", [P, 4]), s.sb("junk", [P, D])
        wu = s.sb("wu", [P, 2, KT, 2 * P])
        wd = s.sb("wd", [P, 2, D])
        cw = s.sb("cw", [P, FT, 8])
        cv = s.sb("cv", [P, 2, 2, L])
        ge = s.sb("ge", [P, 2, L])
        ac = s.sb("ac", [P, 2, L])
        y = s.sb("y", [P, 2, D])
        pu = [s.ps(f"pu{n}", [P, 2, L]) for n in range(2)]
        py = [s.ps(f"py{n}", [P, 512]) for n in range(4)]
        pt = [s.ps(f"pt{n}", [P, 4, P]) for n in range(2)]
        zero = s.sb("zero", [P, 512], BF16)
        u_in, d_in = s.sems("up_in", 2), s.sems("down_in", 2)
        d_free = s.sems("down_used", 2)
        up, conv, gel, hid = s.sems("up_done", 2), s.sems("conv_done", 2), s.sems("gelu_done", 2), s.sems("hid_done", 2)
        (s_in, s_a, s_v, s_t, s_h, s_k, s_z, s_y, s_c, s_out) = (s.sem(n) for n in (
            "in", "act", "chain", "turned", "hT_done", "taps", "zeroed", "down_done", "y_copied", "out"))
        with nc.Block() as block:
            @block.sync
            def _(sp):
                sp.dma_start(gcol[:], A.norm_ffn_pre_col).then_inc(s_in, 16)
                sp.dma_start(cw[:], A.conv_2_col).then_inc(s_in, 16)
                sp.dma_start(gpost[:], A.norm_ffn_post.to_broadcast([P, D])).then_inc(s_in, 16)
                with sp.Fori(0, FT // 2) as i:
                    for z in range(2):
                        sp.wait_ge(up[z], i + 1)
                        sp.dma_start(wu[:, z], A.w_up_units[bass.ds(i * 2 + z, 1)]
                                     .rearrange("u p k n -> p (u k) n")).then_inc(u_in[z], 16)
                        sp.wait_ge(d_free[z], i + 1)
                        sp.dma_start(wd[:, z, :], A.w_down_2[bass.ds(i * (2 * P) + z * P, P), :]).then_inc(d_in[z], 16)
                for t in range(2):
                    sp.wait_ge(s_v, 8 + 2 * t)
                    sp.dma_start(out[0, t * P:(t + 1) * P, :], y[:, t, :]).then_inc(s_out, 16)
                sp.wait_ge(s_out, 32)

            @block.gpsimd
            def _(g):
                for z in range(2):
                    g.sem_inc(up[z], 1)
                    g.sem_inc(d_free[z], 1)
                g.memset(zero[:], 0.0).then_inc(s_z, 1)

            @block.scalar
            def _(act):
                for t in range(2):
                    act.activation(junk[:], S.x[:, t, :], ACT.Square, accum_out=stat[:, t:t + 1]).then_inc(s_a, 1)
                    act.wait_ge(s_a, t + 1)
                act.wait_ge(s_v, 2)
                act.activation(rstd[:, 0:2], stat[:, 0:2], ACT.Sqrt).then_inc(s_a, 1)
                with act.Fori(0, FT // 2) as i:
                    for z in range(2):
                        act.wait_ge(conv[z], i + 1)
                        act.activation(ge[:, z, :], cv[:, z, 0, :], ACT.Gelu_apprx_tanh).then_inc(gel[z], 1)
                for b in range(4):
                    act.wait_ge(s_y, 1)
                    act.activation(y[:, b // 2, 512 * (b % 2):512 * (b % 2) + 512], py[b][:], ACT.Copy).then_inc(s_c, 1)
                    act.wait_ge(s_c, b + 1)
                    if b % 2:
                        t = b // 2
                        act.activation(junk[:], y[:, t, :], ACT.Square, accum_out=stat[:, 2 + t:3 + t]).then_inc(s_a, 1)
                        act.wait_ge(s_a, 4 + t)
                act.wait_ge(s_v, 6)
                act.activation(rstd[:, 2:4], stat[:, 2:4], ACT.Sqrt).then_inc(s_a, 1)

            @block.tensor
            def _(pe):
                for b in range(4):
                    t, h = b // 2, b % 2
                    pe.wait_ge(s_v, 3 + t)
                    if b >= 2:
                        pe.wait_ge(s_h, b - 1)
                    for k in range(4):
                        m = pe.transpose(pt[b % 2][:, k, :], xn[:, t, (4 * h + k) * P:(4 * h + k + 1) * P], C.ident)
                    m.then_inc(s_t, 1)
                pe.wait_ge(s_z, 1)
                for b in range(4):
                    pe.matmul(py[b][:], zero[:, 0:P], zero[:], start=True, stop=False)
                pe.wait_ge(s_h, 4)

                def ups(z, landed):
                    pe.wait_ge(u_in[z], landed)
                    for g in range(2):
                        for k in range(KT):
                            m = pe.matmul(pu[z][:, g, :], wu[:, z, k, g * P:(g + 1) * P], hT[:, k, :],
                                          start=(k == 0), stop=(k == KT - 1))
                    m.then_inc(up[z], 1)

                def downs(z, n):
                    pe.wait_ge(d_in[z], n * 16)
                    pe.wait_ge(hid[z], n)
                    for b in range(4):
                        t, h = b // 2, b % 2
                        m = pe.matmul(py[b][:], ac[:, z, t * P:(t + 1) * P], wd[:, z, 512 * h:512 * h + 512],
                                      start=False, stop=False, skip_group_check=True)
                    m.then_inc(d_free[z], 1)

                ups(0, 16)
                with pe.Fori(0, FT // 2 - 1) as i:
                    ups(1, i * 16 + 16)
                    downs(0, i + 1)
                    ups(0, i * 16 + 32)
                    downs(1, i + 1)
                ups(1, FT // 2 * 16)
                downs(0, FT // 2)
                downs(1, FT // 2)
                for b in range(4):
                    m = pe.matmul(py[b][:], zero[:, 0:P], zero[:], start=False, stop=True)
                m.then_inc(s_y, 1)

            @block.vector
            def _(v):
                link = Chain(v, s_v)
                v.wait_ge(s_a, 2)
                link(v.tensor_scalar(stat[:, 0:2], stat[:, 0:2], 1.0 / D, EPS, ALU.mult, ALU.add))
                link(v.reciprocal(stat[:, 0:2], stat[:, 0:2]))
                v.wait_ge(s_a, 3)
                for t in range(2):
                    link(v.tensor_scalar(xn[:, t, :], S.x[:, t, :], rstd[:, t:t + 1], None, ALU.mult))
                v.wait_ge(s_in, 48)
                for b in range(4):
                    t, h = b // 2, b % 2
                    v.wait_ge(s_t, b + 1)
                    for k in range(4):
                        kk = 4 * h + k
                        m = v.tensor_scalar(hT[:, kk, t * P:(t + 1) * P], pt[b % 2][:, k, :], gcol[:, kk:kk + 1], None,
                                            ALU.mult)
                    m.then_inc(s_h, 1)
                with v.Fori(0, FT // 2) as i:
                    for z in range(2):
                        v.wait_ge(up[z], i + 2)
                        w = lambda j: cw[:, bass.ds(i * 2 + z, 1), j:j + 1].rearrange("p o n -> p (o n)")
                        base = i * 12 + 6 * z
                        for g in range(2):
                            v.tensor_scalar(cv[:, z, g, :], pu[z][:, g, :], w(4 * g + 1), w(4 * g + 3),
                                            ALU.mult, ALU.add).then_inc(s_k, 1)
                        for g in range(2):
                            v.wait_ge(s_k, base + (1 + g))
                            v.scalar_tensor_tensor(cv[:, z, g, 1:], pu[z][:, g, :L - 1], w(4 * g), cv[:, z, g, 1:],
                                                   ALU.mult, ALU.add).then_inc(s_k, 1)
                        for g in range(2):
                            v.wait_ge(s_k, base + (3 + g))
                            m = v.scalar_tensor_tensor(cv[:, z, g, :L - 1], pu[z][:, g, 1:], w(4 * g + 2),
                                                       cv[:, z, g, :L - 1], ALU.mult, ALU.add).then_inc(s_k, 1)
                        v.wait_ge(s_k, base + 6)
                        v.sem_inc(conv[z], 1)
                        v.wait_ge(gel[z], i + 1)
                        v.tensor_tensor(ac[:, z, :], ge[:, z, :], cv[:, z, 1, :], ALU.mult).then_inc(hid[z], 1)
                v.wait_ge(s_a, 5)
                link(v.tensor_scalar(stat[:, 2:4], stat[:, 2:4], 1.0 / D, EPS, ALU.mult, ALU.add))
                link(v.reciprocal(stat[:, 2:4], stat[:, 2:4]))
                v.wait_ge(s_a, 6)
                for t in range(2):
                    link(v.scalar_tensor_tensor(y[:, t, :], y[:, t, :], rstd[:, 2 + t:3 + t], gpost[:], ALU.mult, ALU.mult))
                    link(v.tensor_tensor(y[:, t, :], S.x[:, t, :], y[:, t, :], ALU.add))


class Bag:
    pass


def build(nc, A, out):
    with Scope(nc) as s:
        C, S = Bag(), Bag()
        C.const = s.sb("const", [P, 2, P])
        C.ident, C.ones = C.const[:, 0, :], C.const[:, 1, :]
        C.eps = s.sb("eps", [P, 1])
        S.a2, S.b2 = s.sb("a2", [P, KT]), s.sb("b2", [P, KT])
        S.g = s.sb("gates", [P, 2, D])
        S.g1, S.g2 = S.g[:, 0, :], S.g[:, 1, :]
        with Scope(nc) as mix:
            S.hT = mix.sb("hT", [P, KT, 2 * L])
            modulate_stage(nc, A, C, S)
            S.lf, S.lb = mix.sb("lf", [GATE_RANK, 2 * L]), mix.sb("lb", [GATE_RANK, 2 * L])
            S.oa = mix.sb("oa", [P, HA, L])
            with Scope(nc) as da:
                S.tokq = da.sb("tokq", [P, 2, NTILE, P])
                S.pq, S.pkv = da.sb("pq", [P, HA, L]), da.sb("pkv", [P, 2 * HA, 2 * L])
                delta_project_stage(nc, A, C, S)
                delta_scan_stage(nc, A, C, S)
            S.ob = mix.sb("ob", [P, HB * 2, L])
            linear_attention_stage(nc, A, C, S)
            S.x, S.xn, S.h2T = (mix.sb(n, [P, 2, D]) for n in ("x", "xn", "h2T"))
            S.h2T = S.h2T[:].rearrange("p a (b n) -> p (a b) n", n=L)
            merge_stage(nc, A, C, S)
            S.wgt, S.mask, S.pos, S.posp = (mix.sb(n, [P, 2, NE + 2]) for n in ("wgt", "mask", "pos", "posp"))
            S.count = mix.sb("count", [P, 1], I32)
            S.ring, S.landed = mix.sb("expert_ring", [P, EXPERT_RING, 2 * D]), mix.sems("expert_landed", EXPERT_RING)
            S.pick = mix.sb("bias_pick", [3 * NE, NE * SLOTS])
            S.slot, S.shift = mix.sb("slot_number", [P, SLOTS]), mix.sb("pass_start", [P, L // SLOTS])
            S.bparts = mix.sb("bias_parts", [3 * NE, 3 * D], BF16)
            S.acc = S.oa[:].rearrange("p (a b) n -> p a (b n)", a=2)
            S.put, S.work = S.ob, S.hT[:].rearrange("p k n -> p (k n)")
            router_stage(nc, A, C, S)
            expert_stage(nc, A, C, S)
            close_first_stage(nc, A, C, S)
        S.x = S.g
        attend_stage(nc, A, C, S)
        feed_forward_stage(nc, A, C, S, out)


def layouts(x):
    f = lambda a: np.ascontiguousarray(a)
    col = lambda a, n: f(np.asarray(a).reshape(n, P).T)
    w_in = x["w_in"][0]
    cuts = np.cumsum([0, D, D, D, D, 16, 16, 512, 512, D, D, 32, 2 * D])
    part = lambda i: w_in[:, cuts[i]:cuts[i + 1]]
    cols = np.concatenate([part(0), part(1), part(2)], axis=1)
    tiles = lambda w: w.reshape(KT, P, -1, P).transpose(2, 1, 0, 3)
    whole = tiles(np.concatenate([part(7), part(8)], axis=1))
    latent = tiles(np.concatenate([part(6), part(3), part(9), part(11)], axis=1))
    fill = np.concatenate([whole[:, None], latent.reshape(len(whole), 3, P, KT, P)], axis=1)
    a = {
        "xall": f(np.concatenate([x["ctx"][0], x["x"][0]], axis=0).reshape(NTILE, P, D)),
        "ccol": f(np.stack([x["c"][0], x["c_ctx"]]).reshape(2, KT, P).transpose(2, 1, 0)),
        "w_mod": f(x["w_mod"][0]),
        "b_mod": f(x["b_mod"]),
        "b_mod_col": col(x["b_mod"], NMOD * KT),
        "norm_mix_col": col(x["norm_mix_g"], KT),
        "norm_ffn_col": col(x["norm_ffn_g"], KT),
        "w_in_units": f(cols.reshape(KT, P, -1, UNIT).transpose(2, 1, 0, 3)),
        "w_fill": f(fill.reshape(-1, P, KT, P)),
        "w_small": f(np.concatenate([part(4), part(5), part(10)], axis=1).reshape(KT, P, 64).transpose(1, 0, 2)),
        "conv_w_col": f(x["conv_w"][0].reshape(9, 24, P).transpose(2, 1, 0)),
        "w_out_a": f(x["w_out_a"][0]), "w_out_b": f(x["w_out_b"][0]), "w_out": f(x["w_out"][0]),
        "head_gains": f(np.concatenate([col(x["gdn_norm_g"], 1), col(x["gla_norm_g"], 2)], axis=1)),
        "w_router": f(x["w_router"][0]), "b_router": f(x["b_router"]),
        "w_gu": f(x["w_gu"][0]), "b_gu": f(x["b_gu"][0]), "w_down": f(x["w_down"][0]), "b_down": f(x["b_down"][0]),
        "final_norm_g": f(x["final_norm_g"][None]),
        "w_in_2": f(x["w_in_2"][0]), "w_uq": f(x["w_uq_2"][0]), "w_ukv": f(x["w_ukv_2"][0]), "w_o": f(x["w_o_2"][0]),
        "gains2_col": f(np.concatenate([col(x["norm_mix_pre_2"], KT), col(x["q_lat_norm_2"], 3), col(x["kv_lat_norm_2"], 2),
                                        col(x["out_norm_a_2"], 4), col(x["out_norm_b_2"], 4)], axis=1)),
        "norm_mix_post": f(x["norm_mix_post_2"]), "norm_ffn_post": f(x["norm_ffn_post_2"]),
        "norm_ffn_pre_col": col(x["norm_ffn_pre_2"], KT),
        "w_up_units": f(x["w_up_2"][0].reshape(KT, P, 2, FT, P).transpose(3, 1, 0, 2, 4).reshape(FT, P, KT, 2 * P)),
        "w_down_2": f(x["w_down_2"][0]),
        "conv_2_col": f(np.concatenate([x["conv_w_2"][0], x["conv_b_2"]]).reshape(4, 2, FT, P)
                        .transpose(3, 2, 1, 0).reshape(P, FT, 8)),
        "gate_w": f(np.stack([x["gla_gate_w_f"][0], x["gla_gate_w_b"][0]], axis=1)),
        "gate_b": f(np.stack([x["gla_gate_b_f"][0], x["gla_gate_b_b"][0]]).reshape(2, HB, P).transpose(2, 0, 1)),
        "a_log": f(np.stack([x["a_log_f"][0], x["a_log_b"][0]], axis=1)),
        "dt_bias": f(np.stack([x["dt_bias_f"][0], x["dt_bias_b"][0]], axis=1)),
    }
    return a


def tables():
    i = np.arange(P)
    f = lambda a: np.ascontiguousarray(a, dtype=np.float32)
    lev = np.zeros((P, 2, LEVELS, P))
    for l in range(LEVELS):
        b = 1 << l
        same = (i[:, None] // (2 * b)) == (i[None, :] // (2 * b))
        fw = same & ((i[:, None] // b) % 2 == 0) & ((i[None, :] // b) % 2 == 1)
        lev[:, 0, l], lev[:, 1, l] = fw, fw.T
    tri = np.zeros((P, 2, 2, P))
    for d in range(2):
        after = (i[None, :] > i[:, None]) if d == 0 else (i[None, :] < i[:, None])
        tri[:, d, 0] = np.where(after, 0, NEG)
        tri[:, d, 1] = np.where(after | (i[None, :] == i[:, None]), 0, NEG)
    same = (i[:, None] // GC) == (i[None, :] // GC)
    pick = np.zeros((P, 2, 2, P), np.int32)
    for d in range(2):
        upto = (i[None, :] >= i[:, None]) if d == 0 else (i[None, :] <= i[:, None])
        pick[:, d, 0], pick[:, d, 1] = upto & same, upto & ~same
    t = np.arange(2 * L)
    scan = np.stack([t % P != 0, t % P != P - 1, t % GC != 0, t % GC != GC - 1])
    sel = np.zeros((P, 2))
    sel[0::32, 0] = 1
    sel[1::32, 1] = 1
    q, k = np.arange(L)[:, None], np.arange(L)[None, :]
    count = (abs(q - k) <= 64).astype(np.float64) + ((q - k) % 4 == 0) + ((q - k) % 16 == 0)
    logc = np.where(count > 0, np.log(np.maximum(count, 1)), NEG)
    key_bias = np.stack([logc - 2.0 ** -(h + 1) * abs(q - k) for h in range(H2)])
    ang = np.arange(L, dtype=np.float32)[:, None] * np.exp(
        -np.log(np.float32(10000.0)) * np.arange(0, ROPE, 2, dtype=np.float32) / ROPE)[None, :]
    rope = np.stack([np.cos(ang), np.sin(ang)]).reshape(2, 2, P, ROPE // 2).transpose(2, 0, 1, 3)
    pb = np.zeros((3 * NE, NE, SLOTS), np.float32)
    for e in range(NE):
        pb[e::NE, e] = 1
    return {
        "key_bias": f(key_bias.reshape(H2, 2, P, L).transpose(2, 0, 1, 3)), "rope": f(rope),
        "bias_pick": pb.reshape(3 * NE, NE * SLOTS),
        "iota": f(np.broadcast_to(i, (P, P))), "before_mask": f(i[:, None] < i[None, :]),
        "pass_start": f(np.broadcast_to(np.arange(L // SLOTS) * SLOTS, (P, L // SLOTS))),
        "consts": f(np.stack([np.eye(P), np.ones((P, P))], axis=1)),
        "pick_masks": pick, "level_masks": f(lev), "tri_masks": f(tri), "sel": f(sel),
        "scan_masks": f(np.broadcast_to(scan[None], (P, 4, 2 * L))),
    }


def kernel(**inputs):
    import concourse.bacc as _bacc
    from concourse.bass_utils import run_bass_kernel_spmd as _run

    nc = _bacc.Bacc("TRN2", target_bir_lowering=False, num_devices=1)
    arrays = {**layouts(inputs), **tables()}
    A = Bag()
    for name, a in arrays.items():
        A.__dict__[name] = nc.dram_tensor("in_" + name, a.shape, mybir.dt.from_np(a.dtype), kind="ExternalInput").ap()
    A.fill_whole = nc.dram_tensor("fill_whole", (3 * HB, P, 2 * L), F32).ap()
    A.fill_latent = nc.dram_tensor("fill_latent", (HB + 4 * HA, P, L), F32).ap()
    A.row_scratch = nc.dram_tensor("row_scratch", (2, NTILE, 2, HA, P), F32).ap()
    out = nc.dram_tensor("out", (1, L, D), F32, kind="ExternalOutput").ap()
    build(nc, A, out)
    r = _run(nc, [{"in_" + n: a for n, a in arrays.items()}], core_ids=[0])
    return r.results[0]["out"]
```
